# Optimizing a Trainium2 kernel written in Bass

```python
import math
import jax, jax.numpy as jnp
from jax import lax
import numpy as np

D_MODEL = 1024
BATCH = 1
SEQ = 2048
DEPTH = 1

CHUNK = 64
NORM_EPS = 1e-6
POOL_WIDTH = D_MODEL // 4
POOL_WINDOWS = (2, 4, 8, 16)
POOL_GROUPS = len(POOL_WINDOWS)
POOL_GROUP_DIM = POOL_WIDTH // POOL_GROUPS
ATTN_HEAD_DIM = 64
ATTN_HEADS = D_MODEL // 256
ATTN_V_DIM = 2 * ATTN_HEAD_DIM
ATTN_QK_WIDTH = ATTN_HEADS * 2 * ATTN_HEAD_DIM
ATTN_V_WIDTH = ATTN_HEADS * ATTN_V_DIM
ROPE_THETA = 10000.0
Q_BLOCK = 128
SSM_WIDTH = D_MODEL // 4
SSM_GROUP_DIM = 16
SSM_GROUPS = SSM_WIDTH // SSM_GROUP_DIM
SSM_STATE = 64
DT_MIN = 0.001
DT_MAX = 0.1
IN_WIDTH = POOL_WIDTH + 2 * ATTN_QK_WIDTH + ATTN_V_WIDTH + SSM_WIDTH
N_BRANCHES = 3
MOE_GROUPS = 4
EXPERTS_PER_GROUP = 8
N_EXPERTS = MOE_GROUPS * EXPERTS_PER_GROUP
TOP_K_EXPERT = 2
EXPERT_FF = 512
MOE_BLOCK = 128

kernel_name = "hybrid_chunk_causal_pool_diffattn_s5_hmoe"

def rmsnorm(x, g):
    xf = x.astype(jnp.float32)
    y = xf * lax.rsqrt(jnp.mean(xf * xf, axis=-1, keepdims=True) + NORM_EPS)
    return (y * g.astype(jnp.float32)).astype(x.dtype)

def modulate(h, shift, scale):
    return h * (1.0 + scale[:, None, :]) + shift[:, None, :]

def rope_tables(positions):
    inv = ROPE_THETA ** (-jnp.arange(0, ATTN_HEAD_DIM, 2, dtype=jnp.float32) / ATTN_HEAD_DIM)
    ang = positions.astype(jnp.float32)[..., None] * inv
    return jnp.cos(ang)[:, :, None, None, :], jnp.sin(ang)[:, :, None, None, :]

def apply_rope(t, cos, sin):
    t1, t2 = jnp.split(t, 2, axis=-1)
    return jnp.concatenate([t1 * cos - t2 * sin, t2 * cos + t1 * sin], axis=-1)

def pool_mixer(u, pool_w, pool_scale):
    B, S, _ = u.shape
    ug = u.astype(jnp.float32).reshape(B, S, POOL_GROUPS, POOL_GROUP_DIM)
    cs = jnp.cumsum(ug, axis=1)
    t = jnp.arange(1, S + 1, dtype=jnp.float32)
    outs = []
    for g, w in enumerate(POOL_WINDOWS):
        cg = cs[:, :, g]
        prev = jnp.pad(cg, ((0, 0), (w, 0), (0, 0)))[:, :S]
        cnt = jnp.minimum(t, float(w))[None, :, None]
        outs.append((cg - prev) / cnt - ug[:, :, g])
    pooled = jnp.stack(outs, axis=2)
    y = jnp.einsum('bsgc,gcd->bsgd', pooled, pool_w.astype(jnp.float32)).reshape(B, S, POOL_WIDTH)
    return (y * pool_scale.astype(jnp.float32)).astype(u.dtype)

def diff_attention(q, k, v, cos, sin, q_g, k_g, lq1, lk1, lq2, lk2, subln_g, lambda_init):
    B, S, _ = q.shape
    H, dh, E = ATTN_HEADS, ATTN_HEAD_DIM, ATTN_V_DIM
    qf = rmsnorm(q.astype(jnp.float32).reshape(B, S, H, 2, dh), q_g)
    kf = rmsnorm(k.astype(jnp.float32).reshape(B, S, H, 2, dh), k_g)
    vf = v.astype(jnp.float32).reshape(B, S, H, E)
    qf = apply_rope(qf, cos, sin) * (dh ** -0.5)
    kf = apply_rope(kf, cos, sin)
    lam = (jnp.exp(jnp.sum(lq1.astype(jnp.float32) * lk1.astype(jnp.float32)))
           - jnp.exp(jnp.sum(lq2.astype(jnp.float32) * lk2.astype(jnp.float32))) + lambda_init)
    nb = S // Q_BLOCK
    qb = jnp.moveaxis(qf.reshape(B, nb, Q_BLOCK, H, 2, dh), 1, 0)
    k_chunk = jnp.arange(S) // CHUNK

    def block(args):
        qi, i = args
        s = jnp.einsum('bqhmd,bkhmd->bhmqk', qi, kf)
        q_chunk = (i * Q_BLOCK + jnp.arange(Q_BLOCK)) // CHUNK
        mask = k_chunk[None, :] <= q_chunk[:, None]
        p = jax.nn.softmax(jnp.where(mask, s, -1e30), axis=-1)
        a = p[:, :, 0] - lam * p[:, :, 1]
        return jnp.einsum('bhqk,bkhe->bqhe', a, vf)

    o = lax.map(block, (qb, jnp.arange(nb)))
    o = jnp.moveaxis(o, 0, 1).reshape(B, S, H, E)
    o = rmsnorm(o, subln_g) * (1.0 - lambda_init)
    return o.reshape(B, S, H * E).astype(q.dtype)

def ssm_mixer(u, lam_re, lam_im, log_dt, b_re, b_im, c_re, c_im, d_skip, glu_w, glu_b):
    B, S, _ = u.shape
    f32 = jnp.float32
    uf = u.astype(f32)
    ug = uf.reshape(B, S, SSM_GROUPS, SSM_GROUP_DIM)
    lr, li = lam_re.astype(f32), lam_im.astype(f32)
    dt = jnp.exp(log_dt.astype(f32))[:, None]
    mag = jnp.exp(lr * dt)
    ar, ai = mag * jnp.cos(li * dt), mag * jnp.sin(li * dt)
    nr, ni = ar - 1.0, ai
    den = lr * lr + li * li
    kr, ki = (nr * lr + ni * li) / den, (ni * lr - nr * li) / den
    br, bi = b_re.astype(f32), b_im.astype(f32)
    bbr = kr[..., None] * br - ki[..., None] * bi
    bbi = kr[..., None] * bi + ki[..., None] * br
    bur = jnp.einsum('bsgc,gpc->bsgp', ug, bbr)
    bui = jnp.einsum('bsgc,gpc->bsgp', ug, bbi)
    a_r = jnp.broadcast_to(ar, bur.shape)
    a_i = jnp.broadcast_to(ai, bui.shape)

    def combine(e1, e2):
        a1r, a1i, b1r, b1i = e1
        a2r, a2i, b2r, b2i = e2
        return (a2r * a1r - a2i * a1i, a2r * a1i + a2i * a1r,
                a2r * b1r - a2i * b1i + b2r, a2r * b1i + a2i * b1r + b2i)

    _, _, xr, xi = lax.associative_scan(combine, (a_r, a_i, bur, bui), axis=1)
    y = (jnp.einsum('bsgp,gcp->bsgc', xr, c_re.astype(f32))
         - jnp.einsum('bsgp,gcp->bsgc', xi, c_im.astype(f32))).reshape(B, S, SSM_WIDTH)
    y = jax.nn.gelu(y + d_skip.astype(f32) * uf)
    y = y * jax.nn.sigmoid(y @ glu_w.astype(f32) + glu_b.astype(f32))
    return y.astype(u.dtype)

def moe_dispatch(ht, e_idx, e_w, w1, w3, w2):
    T, D = ht.shape
    n_slots = T * TOP_K_EXPERT
    e_flat = e_idx.reshape(-1)
    w_flat = e_w.reshape(-1)
    tok_flat = jnp.repeat(jnp.arange(T, dtype=jnp.int32), TOP_K_EXPERT)
    order = jnp.argsort(e_flat)
    e_s, tok_s, w_s = e_flat[order], tok_flat[order], w_flat[order]
    counts = jnp.zeros((N_EXPERTS,), jnp.int32).at[e_flat].add(1)
    padded = (counts + MOE_BLOCK - 1) // MOE_BLOCK * MOE_BLOCK
    start = jnp.cumsum(counts) - counts
    pend = jnp.cumsum(padded)
    pstart = pend - padded
    dest = pstart[e_s] + (jnp.arange(n_slots, dtype=jnp.int32) - start[e_s])
    L = n_slots + N_EXPERTS * MOE_BLOCK
    nblk = L // MOE_BLOCK
    buf_tok = jnp.zeros((L,), jnp.int32).at[dest].set(tok_s)
    buf_w = jnp.zeros((L,), w_s.dtype).at[dest].set(w_s)
    blk_start = jnp.arange(nblk, dtype=jnp.int32) * MOE_BLOCK
    blk_e = jnp.minimum(jnp.sum(pend[None, :] <= blk_start[:, None], axis=1), N_EXPERTS - 1)
    xb = ht[buf_tok].reshape(nblk, MOE_BLOCK, D)

    def run_block(args):
        xblk, e = args
        return (jax.nn.silu(xblk @ w1[e]) * (xblk @ w3[e])) @ w2[e]

    yb = lax.map(run_block, (xb, blk_e)).reshape(L, D)
    return jnp.zeros((T, D), yb.dtype).at[buf_tok].add(yb * buf_w[:, None].astype(yb.dtype))

def hier_moe(h, rg_w, rg_b, re_w, re_b, w1, w3, w2):
    B, S, D = h.shape
    ht = h.reshape(B * S, D)
    T = B * S
    pg = jax.nn.softmax((ht @ rg_w).astype(jnp.float32) + rg_b.astype(jnp.float32), axis=-1)
    pg_top, g_idx = lax.top_k(pg, 1)
    el = ((ht @ re_w).astype(jnp.float32) + re_b.astype(jnp.float32)).reshape(T, MOE_GROUPS, EXPERTS_PER_GROUP)
    el_sel = jnp.take_along_axis(el, g_idx[:, :, None], axis=1)[:, 0]
    pe = jax.nn.softmax(el_sel, axis=-1)
    pe_top, e_local = lax.top_k(pe, TOP_K_EXPERT)
    w = pg_top * pe_top / jnp.sum(pe_top, axis=-1, keepdims=True)
    e_idx = g_idx * EXPERTS_PER_GROUP + e_local
    return moe_dispatch(ht, e_idx, w, w1, w3, w2).reshape(B, S, D)

def setup_inputs(seed: int = 0) -> dict:
    key = jax.random.key(seed)
    ks = jax.random.split(key, 40)
    f32 = jnp.float32
    L, D = DEPTH, D_MODEL

    def nrm(k, shape, scale):
        return jax.random.normal(k, shape, f32) * scale

    x = nrm(ks[0], (BATCH, SEQ, D), 1.0)
    c = nrm(ks[1], (BATCH, D), 1.0)
    start = jax.random.randint(ks[2], (BATCH, 1), 0, 16384, dtype=jnp.int32)
    positions = start + jnp.arange(SEQ, dtype=jnp.int32)[None, :]
    n = jnp.arange(SSM_STATE, dtype=f32)
    return {
        "x": x,
        "c": c,
        "positions": positions,
        "ada_w": nrm(ks[3], (L, D, 6 * D), 0.5 * D ** -0.5),
        "ada_b": nrm(ks[4], (L, 6 * D), 0.01),
        "norm1_g": 1.0 + nrm(ks[5], (L, D), 0.02),
        "w_in": nrm(ks[6], (L, D, IN_WIDTH), D ** -0.5),
        "pool_w": nrm(ks[7], (L, POOL_GROUPS, POOL_GROUP_DIM, POOL_GROUP_DIM), POOL_GROUP_DIM ** -0.5),
        "pool_scale": 1.0 + nrm(ks[8], (L, POOL_WIDTH), 0.02),
        "q_norm_g": 1.0 + nrm(ks[9], (L, ATTN_HEAD_DIM), 0.02),
        "k_norm_g": 1.0 + nrm(ks[10], (L, ATTN_HEAD_DIM), 0.02),
        "lambda_q1": nrm(ks[11], (L, ATTN_HEAD_DIM), 0.1),
        "lambda_k1": nrm(ks[12], (L, ATTN_HEAD_DIM), 0.1),
        "lambda_q2": nrm(ks[13], (L, ATTN_HEAD_DIM), 0.1),
        "lambda_k2": nrm(ks[14], (L, ATTN_HEAD_DIM), 0.1),
        "subln_g": 1.0 + nrm(ks[15], (L, ATTN_V_DIM), 0.02),
        "lam_re": -0.5 + nrm(ks[16], (L, SSM_GROUPS, SSM_STATE), 0.01),
        "lam_im": math.pi * n + nrm(ks[17], (L, SSM_GROUPS, SSM_STATE), 0.01),
        "log_dt": jax.random.uniform(ks[18], (L, SSM_GROUPS), f32, math.log(DT_MIN), math.log(DT_MAX)),
        "b_re": nrm(ks[19], (L, SSM_GROUPS, SSM_STATE, SSM_GROUP_DIM), (2 * SSM_GROUP_DIM) ** -0.5),
        "b_im": nrm(ks[20], (L, SSM_GROUPS, SSM_STATE, SSM_GROUP_DIM), (2 * SSM_GROUP_DIM) ** -0.5),
        "c_re": nrm(ks[21], (L, SSM_GROUPS, SSM_GROUP_DIM, SSM_STATE), (2 * SSM_STATE) ** -0.5),
        "c_im": nrm(ks[22], (L, SSM_GROUPS, SSM_GROUP_DIM, SSM_STATE), (2 * SSM_STATE) ** -0.5),
        "d_skip": nrm(ks[23], (L, SSM_WIDTH), 1.0),
        "glu_w": nrm(ks[24], (L, SSM_WIDTH, SSM_WIDTH), SSM_WIDTH ** -0.5),
        "glu_b": nrm(ks[25], (L, SSM_WIDTH), 0.01),
        "proj_a": nrm(ks[26], (L, POOL_WIDTH, D), POOL_WIDTH ** -0.5),
        "proj_b": nrm(ks[27], (L, ATTN_V_WIDTH, D), ATTN_V_WIDTH ** -0.5),
        "proj_c": nrm(ks[28], (L, SSM_WIDTH, D), SSM_WIDTH ** -0.5),
        "gate_w": nrm(ks[29], (L, D, N_BRANCHES * D), D ** -0.5),
        "gate_b": nrm(ks[30], (L, N_BRANCHES * D), 0.01),
        "w_out": nrm(ks[31], (L, D, D), D ** -0.5),
        "norm2_g": 1.0 + nrm(ks[32], (L, D), 0.02),
        "router_g_w": nrm(ks[33], (L, D, MOE_GROUPS), D ** -0.5),
        "router_g_b": nrm(ks[34], (L, MOE_GROUPS), 0.01),
        "router_e_w": nrm(ks[35], (L, D, N_EXPERTS), D ** -0.5),
        "router_e_b": nrm(ks[36], (L, N_EXPERTS), 0.01),
        "moe_w1": nrm(ks[37], (L, N_EXPERTS, D, EXPERT_FF), D ** -0.5),
        "moe_w3": nrm(ks[38], (L, N_EXPERTS, D, EXPERT_FF), D ** -0.5),
        "moe_w2": nrm(ks[39], (L, N_EXPERTS, EXPERT_FF, D), EXPERT_FF ** -0.5),
    }

def reference(x, c, positions, ada_w, ada_b, norm1_g, w_in, pool_w, pool_scale,
              q_norm_g, k_norm_g, lambda_q1, lambda_k1, lambda_q2, lambda_k2, subln_g,
              lam_re, lam_im, log_dt, b_re, b_im, c_re, c_im, d_skip, glu_w, glu_b,
              proj_a, proj_b, proj_c, gate_w, gate_b, w_out, norm2_g,
              router_g_w, router_g_b, router_e_w, router_e_b, moe_w1, moe_w3, moe_w2):
    cos, sin = rope_tables(positions)
    c_act = jax.nn.silu(c)
    splits = [POOL_WIDTH, POOL_WIDTH + ATTN_QK_WIDTH, POOL_WIDTH + 2 * ATTN_QK_WIDTH,
              POOL_WIDTH + 2 * ATTN_QK_WIDTH + ATTN_V_WIDTH]
    for l in range(DEPTH):
        lambda_init = 0.8 - 0.6 * math.exp(-0.3 * l)
        mod = c_act @ ada_w[l] + ada_b[l]
        sh1, sc1, g1, sh2, sc2, g2 = jnp.split(mod, 6, axis=-1)
        h = modulate(rmsnorm(x, norm1_g[l]), sh1, sc1)
        z = h @ w_in[l]
        u_a, q, k, v, u_c = jnp.split(z, splits, axis=-1)
        ya = pool_mixer(u_a, pool_w[l], pool_scale[l])
        yb = diff_attention(q, k, v, cos, sin, q_norm_g[l], k_norm_g[l], lambda_q1[l], lambda_k1[l],
                            lambda_q2[l], lambda_k2[l], subln_g[l], lambda_init)
        yc = ssm_mixer(u_c, lam_re[l], lam_im[l], log_dt[l], b_re[l], b_im[l], c_re[l], c_im[l],
                       d_skip[l], glu_w[l], glu_b[l])
        ga, gb, gc = jnp.split(jax.nn.sigmoid(h @ gate_w[l] + gate_b[l]), N_BRANCHES, axis=-1)
        mixed = ga * (ya @ proj_a[l]) + gb * (yb @ proj_b[l]) + gc * (yc @ proj_c[l])
        x = x + g1[:, None, :] * (mixed @ w_out[l])
        h2 = modulate(rmsnorm(x, norm2_g[l]), sh2, sc2)
        x = x + g2[:, None, :] * hier_moe(h2, router_g_w[l], router_g_b[l], router_e_w[l], router_e_b[l],
                                          moe_w1[l], moe_w3[l], moe_w2[l])
    return x


_drawn_inputs = setup_inputs


def setup_inputs(seed=0):
    import zlib

    import numpy as np

    out = dict(_drawn_inputs(seed))
    spreads = {}
    factors = {'ada_b': 4.331,
     'norm1_g': 8.0,
     'pool_scale': 8.0,
     'q_norm_g': 8.0,
     'k_norm_g': 8.0,
     'lambda_q1': 4.368,
     'lambda_k1': 8.0,
     'lambda_q2': 8.0,
     'lambda_k2': 8.0,
     'subln_g': 55.953,
     'lam_re': 64.0,
     'lam_im': 55.96,
     'log_dt': 64.0,
     'b_re': 64.0,
     'b_im': 64.0,
     'c_re': 64.0,
     'c_im': 64.0,
     'glu_b': 200.0,
     'gate_b': 22.645,
     'norm2_g': 4.737,
     'router_g_b': 22.708,
     'router_e_b': 26.451}
    for name, (base, spread) in spreads.items():
        noise = np.random.default_rng([zlib.crc32(name.encode()), seed]).standard_normal(out[name].shape)
        drawn = base * np.exp(spread * noise) if base else spread * noise
        out[name] = __import__('jax').numpy.asarray(drawn.astype(out[name].dtype))
    for name, factor in factors.items():
        out[name] = (out[name] * factor).astype(out[name].dtype)
    return out
```

```python
import math
from contextlib import ExitStack

import numpy as np
import concourse.bass as bass
from concourse import mybir

F32 = mybir.dt.float32
I32 = mybir.dt.int32
U32 = mybir.dt.uint32
ALU = mybir.AluOpType
ACT = mybir.ActivationFunctionType
AX = mybir.AxisListType.X

P = 128
T = 2048
D = 1024
KD = D // P
NT = T // P
TB = T // 512
EPS = 1e-6
HEADS = 4
DH = 64
POOL_W = 256
QK_W = 512
SSM_W = 256
Q0 = POOL_W
K0 = Q0 + QK_W
V0 = K0 + QK_W
C0 = V0 + QK_W
LAMBDA_INIT = 0.8 - 0.6 * math.exp(-0.3 * 0)
NEG = -1e30
GROUPS = 16
SL = 8
SC = T // SL
NE = 32
FF = 512
NB_OUT = 66

CONSTS = {}
_at = 0
for _n, _w in (("ident", P), ("rot", P), ("swap", P), ("half", P), ("before", P), ("ones", P),
               ("mask", 512), ("inv", 1), ("sign", 1), ("upper", 1), ("cnt", 32), ("width", 2), ("iota", 32),
               ("blk", 96), ("tok", NT)):
    CONSTS[_n] = (_at, _at + _w)
    _at += _w
CONST_W = _at


def constant_pack():
    c = np.zeros((P, CONST_W), np.float32)

    def put(name, a):
        c[:, CONSTS[name][0]:CONSTS[name][1]] = a
    r = np.arange(P)
    i = np.eye(P, dtype=np.float32)
    put("ident", i)
    put("rot", i[:, r ^ 32])
    put("swap", np.concatenate([-i[:, 64:], i[:, :64]], 1))
    put("half", (r[:, None] // 64 == r[None, :] // 64) / 64.0)
    put("before", r[:, None] < r[None, :])
    put("ones", 1.0)
    m = np.zeros((P, 512), np.float32)
    m[:64, 448:] = NEG
    put("mask", m)
    put("inv", (10000.0 ** (-2.0 * (r % 32) / DH)).astype(np.float32)[:, None])
    put("sign", np.where(r % 64 < 32, -1.0, 1.0)[:, None])
    put("upper", np.where(r < 64, -1.0, 1.0)[:, None])
    w = np.stack([np.where(r < 64, 2, 4), np.where(r < 64, 8, 16)], 1)
    put("width", 1.0 / w)
    put("cnt", np.concatenate([1.0 / np.minimum(np.arange(1, 17)[None, :], w[:, h:h + 1])
                               for h in range(2)], 1))
    put("iota", np.arange(32)[None, :])
    put("blk", np.arange(96)[None, :])
    put("tok", r[:, None] + P * np.arange(NT)[None, :])
    return c


class Chain:

    def __init__(self, eng, sem):
        self.eng, self.sem, self.n = eng, sem, 0

    def __call__(self, ins):
        self.n += 1
        ins.then_inc(self.sem, 1)
        self.eng.wait_ge(self.sem, self.n)


KEPT = []


class Stage:

    def __init__(self, nc, name):
        self.nc, self.name, self.ctx, self.sems = nc, name, ExitStack(), []

    def __enter__(self):
        return self

    def __exit__(self, *a):
        return self.ctx.__exit__(*a)

    def sb(self, name, shape, dt=F32):
        return self.ctx.enter_context(self.nc.sbuf_tensor(f"{self.name}_{name}", shape, dt))

    def ps(self, name, shape):
        return self.ctx.enter_context(self.nc.psum_tensor(f"{self.name}_{name}", shape, F32))

    def sem(self, name):
        s = self.ctx.enter_context(self.nc.semaphore(f"{self.name}_{name}"))
        self.sems.append(s)
        return s

    def kept_sem(self, name):
        s = self.nc.semaphore(f"{self.name}_{name}")
        KEPT.append(s)
        return s.__enter__()

    def end(self):
        for s in self.sems:
            self.nc.sync.sem_clear(s)
        self.nc.all_engine_barrier()


def const(g, name):
    a, b = CONSTS[name]
    return g["consts"][:, a:b]


def wrap_angle(nc, link, ang, tmp):
    parts, rest = [], 2 * math.pi
    for bits in (5, 13, 21):
        part = math.floor(rest * 2.0 ** bits) / 2.0 ** bits
        parts.append(part)
        rest -= part
    parts.append(rest)
    magic = 1.5 * 2.0 ** 23
    link(nc.vector.tensor_scalar(tmp, ang, 1 / (2 * math.pi), None, ALU.mult))
    link(nc.vector.tensor_scalar(tmp, tmp, magic, None, ALU.add))
    link(nc.vector.tensor_scalar(tmp, tmp, magic, None, ALU.subtract))
    for part in parts:
        link(nc.vector.scalar_tensor_tensor(ang, tmp, -part, ang, ALU.mult, ALU.add))
    link(nc.vector.tensor_scalar(ang, ang, 3.1415925, -3.1415925, ALU.min, ALU.max))


def stage_mod(nc, g):
    ada_w = g["ada_w"][0].rearrange("(k p) n -> p k n", p=P)
    with Stage(nc, "mod") as s:
        ccol = s.sb("ccol", [P, KD])
        cexp = s.sb("cexp", [P, KD])
        crep = s.sb("crep", [P, KD, P])
        w = s.sb("w", [P, 4, KD, 512])
        bias = s.sb("bias", [P, 6, 512])
        mod = s.sb("mod", [P, 6, D])
        n1 = s.sb("n1", [P, D])
        n2 = s.sb("n2", [P, D])
        acc = [s.ps(f"acc{i}", [P, 512]) for i in range(4)]
        tr = [s.ps(f"tr{i}", [P, 512]) for i in range(4)]
        small, w_ready = s.sem("small"), [s.sem(f"w_ready{i}") for i in range(4)]
        exped, c_ready, summed, moded = s.sem("exped"), s.sem("c_ready"), s.sem("summed"), s.sem("moded")
        dve_done, turned, stored = s.sem("dve_done"), s.sem("turned"), s.sem("stored")

        with nc.Block() as block:
            @block.sync
            def _(sp):
                sp.dma_start(ccol[:], g["c"].rearrange("a (k p) -> p (a k)", p=P), allow_slow_non_contiguous=True).then_inc(small, 16)
                sp.dma_start(g["consts"][:], g["const_pack"]).then_inc(small, 16)
                sp.dma_start(n1[:], g["norm1_g"].broadcast_to([P, D])).then_inc(small, 16)
                sp.dma_start(n2[:], g["norm2_g"].broadcast_to([P, D])).then_inc(small, 16)

            @block.scalar
            def _(act):
                act.wait_ge(small, 64)
                nc.scalar.activation(cexp[:], ccol[:], ACT.Exp, scale=-1.0).then_inc(exped, 1)

            @block.vector
            def _(dve):
                link = Chain(dve, dve_done)
                dve.wait_ge(small, 64)
                dve.wait_ge(exped, 1)
                link(nc.vector.tensor_scalar(cexp[:], cexp[:], 1.0, None, ALU.add))
                link(nc.vector.reciprocal(cexp[:], cexp[:]))
                link(nc.vector.tensor_tensor(ccol[:], ccol[:], cexp[:], ALU.mult))
                for k in range(KD):
                    link(nc.vector.tensor_scalar(crep[:, k, :], const(g, "ones"), ccol[:, k:k + 1], None, ALU.mult))
        s.end()

        PER = 6
        with nc.Fori(0, 2) as turn:
            with nc.Block() as block:
                @block.sync
                def _(sp):
                    sp.dma_start(bias[:].rearrange("p a n -> p (a n)"),
                                 g["ada_b"][:, bass.ds(turn * (PER * 512), PER * 512)].broadcast_to([P, PER * 512])).then_inc(small, 16)
                    for i in range(PER):
                        if i >= 4:
                            sp.wait_ge(summed, i - 3)
                        sp.dma_start(w[:, i % 4], ada_w[:, :, bass.ds(turn * (PER * 512) + i * 512, 512)]).then_inc(w_ready[i % 4], 16)

                @block.tensor
                def _(pe):
                    for i in range(PER):
                        pe.wait_ge(w_ready[i % 4], 16 * (i // 4 + 1))
                        if i >= 4:
                            pe.wait_ge(moded, i - 3)
                        for k in range(KD):
                            mm = pe.matmul(acc[i % 4][:], crep[:, k, :], w[:, i % 4, k, :], start=k == 0, stop=k == KD - 1)
                        mm.then_inc(summed, 1)

                @block.vector
                def _(dve):
                    dve.wait_ge(small, 16)
                    flat = mod[:].rearrange("p a n -> p (a n)")
                    for i in range(PER):
                        dve.wait_ge(summed, i + 1)
                        nc.vector.tensor_tensor(flat[:, bass.ds(turn * (PER * 512) + i * 512, 512)], acc[i % 4][:],
                                                bias[:, i, :], ALU.add).then_inc(moded, 1)
            s.end()

        with nc.Block() as block:
            @block.vector
            def _(dve):
                link = Chain(dve, dve_done)
                link(nc.vector.scalar_tensor_tensor(mod[:, 1], mod[:, 1], 1.0, n1[:], ALU.add, ALU.mult))
                nc.vector.scalar_tensor_tensor(mod[:, 4], mod[:, 4], 1.0, n2[:], ALU.add, ALU.mult).then_inc(moded, 1)
                for b in range(4):
                    dve.wait_ge(turned, b + 1)
                    nc.vector.tensor_copy(g["col1"][:, b // 2, (b % 2) * 4:(b % 2) * 4 + 4],
                                          tr[b][:].rearrange("p (a n) -> p a n", n=P)[:, :, 0]).then_inc(c_ready, 1)

            @block.tensor
            def _(pe):
                pe.wait_ge(moded, 1)
                for b in range(4):
                    for j in range(4):
                        k = (b % 2) * 4 + j
                        mm = pe.transpose(tr[b][:, j * P:(j + 1) * P], mod[:, b // 2, k * P:(k + 1) * P], const(g, "ident"))
                    mm.then_inc(turned, 1)

            @block.sync
            def _(sp):
                sp.wait_ge(moded, 1)
                for r in (2, 3, 4, 5):
                    sp.dma_start(g["rows"][r - 2:r - 1, :], mod[0:1, r, :]).then_inc(stored, 16)
                sp.wait_ge(stored, 64)
        s.end()


def stage_norm1(nc, g):
    U = 8
    x_t = g["x"][0].rearrange("(t p) n -> p t n", p=P)
    with Stage(nc, "norm1") as s:
        x = s.sb("x", [P, U, D])
        sq = s.sb("sq", [P, D])
        ss = s.sb("ss", [P, U])
        eps = s.sb("eps", [P, 1])
        bank = [[s.ps(f"tr{i}{j}", [P, 4, P]) for j in range(2)] for i in range(4)]
        x_ready = [s.sem(f"x_ready{i}") for i in range(U)]
        small, act_done, rooted, dve_done = s.sem("small"), s.sem("act_done"), s.sem("rooted"), s.sem("dve_done")
        act_moved = s.sem("act_moved")
        scaled, turned, moved = s.sem("scaled"), s.sem("turned"), s.sem("moved")
        with nc.Fori(0, NT // U) as turn:
            with nc.Block() as block:
                @block.sync
                def _(sp):
                    for i in range(U):
                        sp.dma_start(x[:, i, :], x_t[:, bass.ds(turn * U + i, 1), :].rearrange("p a n -> p (a n)")).then_inc(x_ready[i], 16)

                @block.gpsimd
                def _(pool):
                    nc.gpsimd.memset(eps[:], EPS).then_inc(small, 1)

                @block.scalar
                def _(act):
                    link = Chain(act, act_done)

                    def place(i):
                        act.wait_ge(turned, i + 1)
                        for k in range(4, KD):
                            nc.scalar.activation(g["hT"][:, k, bass.ds((turn * U + i) * P, P)], bank[i % 4][1][:, k % 4, :], ACT.Identity,
                                                 scale=g["col1"][:, 1, k:k + 1], bias=g["col1"][:, 0, k:k + 1]).then_inc(act_moved, 1)
                    act.wait_ge(small, 1)
                    for i in range(U + 2):
                        if i < U:
                            act.wait_ge(x_ready[i], 16)
                            link(nc.scalar.activation(sq[:], x[:, i, :], ACT.Square, accum_out=ss[:, i:i + 1]))
                            nc.scalar.activation(ss[:, i:i + 1], ss[:, i:i + 1], ACT.Sqrt, scale=1.0 / D, bias=eps[:]).then_inc(rooted, 1)
                        if i >= 2:
                            place(i - 2)

                @block.vector
                def _(dve):
                    link = Chain(dve, dve_done)
                    for i in range(U + 2):
                        if i < U:
                            dve.wait_ge(rooted, i + 1)
                            link(nc.vector.reciprocal(ss[:, i:i + 1], ss[:, i:i + 1]))
                            nc.vector.tensor_scalar(x[:, i, :], x[:, i, :], ss[:, i:i + 1], None, ALU.mult).then_inc(scaled, 1)
                        if i >= 2:
                            j = i - 2
                            dve.wait_ge(turned, j + 1)
                            for k in range(4):
                                nc.vector.tensor_scalar(g["hT"][:, k, bass.ds((turn * U + j) * P, P)], bank[j % 4][0][:, k, :],
                                                        g["col1"][:, 1, k:k + 1], g["col1"][:, 0, k:k + 1],
                                                        ALU.mult, ALU.add).then_inc(moved, 1)

                @block.tensor
                def _(pe):
                    for i in range(U):
                        pe.wait_ge(scaled, i + 1)
                        if i >= 4:
                            pe.wait_ge(moved, 4 * (i - 3))
                            pe.wait_ge(act_moved, 4 * (i - 3))
                        for k in range(KD):
                            mm = pe.transpose(bank[i % 4][k // 4][:, k % 4, :], x[:, i, k * P:(k + 1) * P], const(g, "ident"))
                        mm.then_inc(turned, 1)
            s.end()


def stage_angles(nc, g, cos, sin):
    with Stage(nc, "ang") as s:
        pos = s.sb("pos", [P, T], I32)
        ang = s.sb("ang", [P, T])
        tmp = s.sb("tmp", [P, T])
        half_pi = s.sb("half_pi", [P, 1])
        small, dve_done, wrapped, sined, ready = s.sem("small"), s.sem("dve_done"), s.sem("wrapped"), s.sem("sined"), s.sem("ready")
        with nc.Block() as block:
            @block.sync
            def _(sp):
                sp.dma_start(pos[:], g["positions"].broadcast_to([P, T])).then_inc(small, 16)

            @block.vector
            def _(dve):
                link = Chain(dve, dve_done)
                link(nc.vector.memset(half_pi[:], math.pi / 2))
                dve.wait_ge(small, 16)
                link(nc.vector.tensor_copy(ang[:], pos[:]))
                link(nc.vector.tensor_scalar(ang[:], ang[:], const(g, "inv"), None, ALU.mult))
                wrap_angle(nc, link, ang[:], tmp[:])
                nc.vector.scalar_tensor_tensor(tmp[:], ang[:], -1.0, ang[:], ALU.mult, ALU.max).then_inc(wrapped, 1)
                dve.wait_ge(sined, 1)
                link(nc.vector.tensor_scalar(sin[:], sin[:], const(g, "sign"), None, ALU.mult))

            @block.scalar
            def _(act):
                act.wait_ge(wrapped, 1)
                nc.scalar.activation(sin[:], ang[:], ACT.Sin).then_inc(sined, 1)
                nc.scalar.activation(cos[:], tmp[:], ACT.Sin, scale=-1.0, bias=half_pi[:]).then_inc(ready, 1)
        s.end()


LATE = 9


def clear_late_blocks(sp, g, zero, turn, sem):
    for i in range(LATE):
        sp.dma_start(g["ybuf"][bass.ds((turn * LATE + (NB_OUT - 4 * LATE + i)) * P, P), :].rearrange("p (a n) -> p a n", n=P),
                     zero[:].unsqueeze(1).broadcast_to([P, KD, P])).then_inc(sem, 16)


def stage_attention(nc, g):
    w_in = g["w_in"][0].rearrange("(k p) n -> p k n", p=P)
    hT, ybT = g["hT"], g["ybT"]
    RING = 3
    with Stage(nc, "att") as s:
        cos, sin = s.sb("cos", [P, T]), s.sb("sin", [P, T])
        stage_angles(nc, g, cos, sin)
        w = s.sb("w", [P, 3, KD, P])
        qk = s.sb("qk", [P, 2, T])
        val = s.sb("val", [P, NT, P])
        S = s.sb("S", [P, RING, 2, T])
        vT = S[:, 1, 1, :]
        aT = s.sb("aT", [P, 2, 4, P])
        o = qk[:, 0, :].rearrange("p (t e) -> p t e", e=P)
        osq = s.sb("osq", [P, 2, P])
        zero = s.sb("zero", [P, P])
        sq2, rs2 = S[:, 0, 0, 0:1024].rearrange("p (a n) -> p a n", a=2), S[:, 0, 0, 1024:2048].rearrange("p (a n) -> p a n", a=2)
        qn2, tt = S[:, 0, 1, 0:1024].rearrange("p (a n) -> p a n", a=2), S[:, 0, 1, 1024:1536]
        gcol = s.sb("gcol", [P, 4])
        lq = S[:, 1, 0, 0:4 * DH].rearrange("p (a n) -> p a n", n=DH)
        eps = s.sb("eps", [P, 1])
        mx = s.sb("mx", [P, RING, 2, 4])
        nm = s.sb("nm", [P, RING, 2])
        den = s.sb("den", [P, RING, 2])
        ss = s.sb("ss", [P, NT])
        bank = [s.ps(f"bank{i}", [P, 512]) for i in range(8)]
        names = ("small dve_done act_done pool_done w_ready w_ready2 projected squared meaned rooted normed rotated "
                 "rotary v_copied v_turned v_placed scored evacuated maxed exped scaled weighed a_turned a_placed "
                 "summed o_copied o_squared o_rooted o_normed o_turned o_placed lam cleared").split()
        q = {n: s.sem(n) for n in names}

        def load_w(sp, h, sem):
            for j, c0 in enumerate((Q0, K0, V0)):
                sp.dma_start(w[:, j], w_in[:, :, bass.ds(h * P + c0, P)]).then_inc(sem, 16)

        with nc.Block() as block:
            @block.sync
            def _(sp):
                for j, n in enumerate(("q_norm_g", "k_norm_g")):
                    for m in range(2):
                        sp.dma_start(gcol[m * DH:(m + 1) * DH, j:j + 1], g[n].rearrange("a n -> n a"), allow_slow_non_contiguous=True).then_inc(q["small"], 16)
                sp.dma_start(gcol[:, 2:3], g["subln_g"].rearrange("a n -> n a"), allow_slow_non_contiguous=True).then_inc(q["small"], 16)
                for j, n in enumerate(("lambda_q1", "lambda_k1", "lambda_q2", "lambda_k2")):
                    sp.dma_start(lq[:, j], g[n].broadcast_to([P, DH])).then_inc(q["small"], 16)
                load_w(sp, 0, q["w_ready"])
                sp.wait_ge(q["w_ready"], 48)

            @block.vector
            def _(dve):
                link = Chain(dve, q["dve_done"])
                link(nc.vector.memset(eps[:], EPS))
                link(nc.vector.memset(zero[:], 0.0))
                dve.wait_ge(q["small"], 16 * 9)
                link(nc.vector.tensor_scalar(gcol[:, 0:1], gcol[:, 0:1], DH ** -0.5, None, ALU.mult))
                link(nc.vector.tensor_scalar(gcol[:, 2:3], gcol[:, 2:3], 1.0 - LAMBDA_INIT, None, ALU.mult))
                for j in range(2):
                    link(nc.vector.tensor_tensor_reduce(lq[:, 2 * j], lq[:, 2 * j], lq[:, 2 * j + 1], 1.0, 0.0, ALU.mult,
                                                        ALU.add, den[:, 0, j:j + 1]))
                nc.vector.memset(nm[:, 0, 0:1], 0.0).then_inc(q["maxed"], 1)
                dve.wait_ge(q["lam"], 1)
                link(nc.vector.tensor_tensor(gcol[:, 3:4], den[:, 1, 0:1], den[:, 1, 1:2], ALU.subtract))
                link(nc.vector.tensor_scalar(gcol[:, 3:4], gcol[:, 3:4], LAMBDA_INIT, None, ALU.add))

            @block.scalar
            def _(act):
                act.wait_ge(q["maxed"], 1)
                nc.scalar.activation(den[:, 1, :], den[:, 0, :], ACT.Exp).then_inc(q["lam"], 1)
        s.end()

        with nc.Fori(0, HEADS) as h:
            units = [(m, tb) for m in range(3) for tb in range(TB)]
            nqk = 2 * TB
            score_units = [(i, m, c, min(512, (i + 1) * P - c * 512), c == i // 4)
                           for i in range(NT) for m in range(2) for c in range(i // 4 + 1)]
            first_unit = [next(n for n, u in enumerate(score_units) if u[0] == i) for i in range(NT)] + [len(score_units)]
            turn_units = [(i, c, min(4, i + 1 - 4 * c)) for i in range(NT) for c in range(i // 4 + 1)]
            first_turn = [next(n for n, u in enumerate(turn_units) if u[0] == i) for i in range(NT)] + [len(turn_units)]

            with nc.Block() as block:
                @block.sync
                def _(sp):
                    sp.wait_ge(q["projected"], 12)
                    load_w(sp, h + 1, q["w_ready"])
                    clear_late_blocks(sp, g, zero, h, q["cleared"])
                    sp.wait_ge(q["w_ready"], 48)
                    sp.wait_ge(q["cleared"], 16 * LATE)

                @block.tensor
                def _(pe):
                    def project(n):
                        m, tb = units[n]
                        if n >= 4:
                            if n - 4 < nqk:
                                pe.wait_ge(q["normed"], n - 3)
                            else:
                                pe.wait_ge(q["v_copied"], n - 3 - nqk)
                        for k in range(KD):
                            mm = pe.matmul(bank[n % 4][:], w[:, m, k, :], hT[:, k, tb * 512:(tb + 1) * 512],
                                           start=k == 0, stop=k == KD - 1)
                        mm.then_inc(q["projected"], 1)

                    def mean(n):
                        pe.wait_ge(q["squared"], n + 1)
                        if n >= 2:
                            pe.wait_ge(q["rooted"], n - 1)
                        pe.matmul(bank[4 + n % 2][:], const(g, "half"), sq2[:, n % 2, :], start=True, stop=True).then_inc(q["meaned"], 1)

                    def rotate(n):
                        pe.wait_ge(q["normed"], n + 1)
                        if n >= 2:
                            pe.wait_ge(q["rotary"], n - 1)
                        pe.matmul(bank[6 + n % 2][:], const(g, "rot"), qn2[:, n % 2, :], start=True, stop=True).then_inc(q["rotated"], 1)

                    for n in range(len(units) + 2):
                        if n < len(units):
                            project(n)
                        if 1 <= n <= nqk:
                            mean(n - 1)
                        if 2 <= n <= nqk + 1:
                            rotate(n - 2)
                    for tb in range(TB):
                        pe.wait_ge(q["v_copied"], tb + 1)
                        if tb < 2:
                            pe.wait_ge(q["rooted"], nqk)
                        else:
                            pe.wait_ge(q["v_placed"], tb - 1)
                        for j in range(4):
                            mm = pe.transpose(bank[4 + tb % 2][:, j * P:(j + 1) * P],
                                              vT[:, tb * 512 + j * P:tb * 512 + (j + 1) * P], const(g, "ident"))
                        mm.then_inc(q["v_turned"], 1)

                    def score(n):
                        i, m, c, width, _ = score_units[n]
                        if n >= 4:
                            pe.wait_ge(q["evacuated"], n - 3)
                        pe.matmul(bank[n % 4][:, :width], qk[m * DH:(m + 1) * DH, 0, i * P:(i + 1) * P],
                                  qk[m * DH:(m + 1) * DH, 1, c * 512:c * 512 + width], start=True, stop=True).then_inc(q["scored"], 1)

                    def turn_a(n):
                        i, c, blocks = turn_units[n]
                        if n >= 2:
                            pe.wait_ge(q["a_placed"], n - 1)
                        for j in range(blocks):
                            mm = pe.transpose(bank[4 + n % 2][:, j * P:(j + 1) * P],
                                              S[:, i % RING, 0, (4 * c + j) * P:(4 * c + j + 1) * P], const(g, "ident"))
                        mm.then_inc(q["a_turned"], 1)

                    def weigh_v(n):
                        i, c, blocks = turn_units[n]
                        pe.wait_ge(q["a_placed"], n + 1)
                        for j in range(blocks):
                            mm = pe.matmul(bank[6 + i % 2][:, 0:P], aT[:, n % 2, j, :], val[:, 4 * c + j, :],
                                           start=4 * c + j == 0, stop=4 * c + j == i)
                        mm.then_inc(q["summed"], 1)

                    pe.wait_ge(q["rotary"], nqk)
                    pe.wait_ge(q["v_copied"], TB)
                    for n in range(first_unit[2]):
                        score(n)
                    pe.wait_ge(q["v_placed"], TB)
                    for i in range(NT):
                        ahead = list(range(first_unit[i + 2], first_unit[i + 3])) if i + 2 < NT else []
                        lo, hi = first_turn[i], first_turn[i + 1]
                        pe.wait_ge(q["weighed"], i + 1)
                        if i >= 2:
                            pe.wait_ge(q["o_copied"], i - 1)
                            pe.wait_ge(q["o_squared"], i - 1)
                        for n in range(lo, hi + 1):
                            if n < hi:
                                turn_a(n)
                            for _ in range(-(-len(ahead) // (hi + 1 - n))):
                                score(ahead.pop(0))
                            if n > lo:
                                weigh_v(n - 1)
                    for c in range(4):
                        pe.wait_ge(q["o_normed"], 4 * c + 4)
                        pe.wait_ge(q["a_placed"], len(turn_units))
                        for j in range(4):
                            mm = pe.transpose(bank[c][:, j * P:(j + 1) * P], o[:, 4 * c + j, :], const(g, "ident"))
                        mm.then_inc(q["o_turned"], 1)

                @block.scalar
                def _(act):
                    link = Chain(act, q["act_done"])

                    def square(n):
                        act.wait_ge(q["projected"], n + 1)
                        if n >= 2:
                            act.wait_ge(q["meaned"], n - 1)
                        nc.scalar.activation(sq2[:, n % 2, :], bank[n % 4][:], ACT.Square).then_inc(q["squared"], 1)

                    def root(n):
                        act.wait_ge(q["meaned"], n + 1)
                        if n >= 2:
                            act.wait_ge(q["normed"], n - 1)
                        nc.scalar.activation(rs2[:, n % 2, :], bank[4 + n % 2][:], ACT.Sqrt, bias=eps[:]).then_inc(q["rooted"], 1)

                    for n in range(nqk + 1):
                        if n < nqk:
                            square(n)
                        if n >= 1:
                            root(n - 1)
                    for tb in range(TB):
                        act.wait_ge(q["projected"], nqk + tb + 1)
                        nc.scalar.copy(vT[:, tb * 512:(tb + 1) * 512], bank[(nqk + tb) % 4][:]).then_inc(q["v_copied"], 1)
                    for tb in range(TB):
                        act.wait_ge(q["v_turned"], tb + 1)
                        nc.scalar.copy(val[:, 4 * tb:4 * tb + 4, :], bank[4 + tb % 2][:].rearrange("p (a b) -> p a b", a=4)).then_inc(q["v_placed"], 1)

                    def exps(i):
                        act.wait_ge(q["maxed"], i + 1)
                        if i >= RING:
                            act.wait_ge(q["weighed"], i - RING + 1)
                        n = (i + 1) * P
                        for m in (1, 0):
                            nc.scalar.activation(S[:, i % RING, m, :n], S[:, i % RING, m, :n], ACT.Exp, bias=nm[:, i % RING, m:m + 1],
                                                 accum_out=den[:, i % RING, m:m + 1]).then_inc(q["exped"], 1)

                    def place(i):
                        for n in range(first_turn[i], first_turn[i + 1]):
                            act.wait_ge(q["a_turned"], n + 1)
                            if n >= 2:
                                act.wait_ge(q["summed"], n - 1)
                            b = turn_units[n][2]
                            nc.scalar.copy(aT[:, n % 2, :b, :], bank[4 + n % 2][:, :b * P].rearrange("p (a b) -> p a b", b=P)).then_inc(q["a_placed"], 1)
                        act.wait_ge(q["summed"], first_turn[i + 1])
                        nc.scalar.copy(o[:, i, :], bank[6 + i % 2][:, 0:P]).then_inc(q["o_copied"], 1)
                        if i >= 2:
                            act.wait_ge(q["o_squared"], i - 1)
                        nc.scalar.activation(osq[:, i % 2, :], bank[6 + i % 2][:, 0:P], ACT.Square,
                                             accum_out=ss[:, i:i + 1]).then_inc(q["o_squared"], 1)

                    exps(0)
                    exps(1)
                    for i in range(NT):
                        place(i)
                        if i + 2 < NT:
                            exps(i + 2)
                    act.wait_ge(q["o_squared"], NT)
                    nc.scalar.activation(ss[:], ss[:], ACT.Sqrt, scale=1.0 / P, bias=eps[:]).then_inc(q["o_rooted"], 1)
                    for c in range(4):
                        act.wait_ge(q["o_turned"], c + 1)
                        nc.scalar.activation(ybT[:, bass.ds(h, 1), c * 512:(c + 1) * 512].rearrange("p a n -> p (a n)"),
                                             bank[c][:], ACT.Copy, scale=gcol[:, 2:3]).then_inc(q["o_placed"], 1)

                @block.gpsimd
                def _(pool):
                    for i in range(NT):
                        pool.wait_ge(q["scaled"], i + 1)
                        n = (i + 1) * P
                        nc.gpsimd.tensor_scalar(S[:, i % RING, 1, :n], S[:, i % RING, 1, :n], den[:, i % RING, 1:2], None, ALU.mult).then_inc(q["pool_done"], 1)

                @block.vector
                def _(dve):
                    link = Chain(dve, q["dve_done"])

                    def norm(n):
                        m, tb = units[n]
                        dve.wait_ge(q["rooted"], n + 1)
                        link(nc.vector.reciprocal(rs2[:, n % 2, :], rs2[:, n % 2, :]))
                        if n >= 2:
                            dve.wait_ge(q["rotated"], n - 1)
                        nc.vector.scalar_tensor_tensor(qn2[:, n % 2, :], bank[n % 4][:], gcol[:, m:m + 1], rs2[:, n % 2, :],
                                                       ALU.mult, ALU.mult).then_inc(q["normed"], 1)

                    def rope(n):
                        m, tb = units[n]
                        to = slice(tb * 512, (tb + 1) * 512)
                        dve.wait_ge(q["normed"], n + 1)
                        link(nc.vector.tensor_tensor(qk[:, m, to], qn2[:, n % 2, :], cos[:, to], ALU.mult))
                        dve.wait_ge(q["rotated"], n + 1)
                        link(nc.vector.tensor_tensor(tt, bank[6 + n % 2][:], sin[:, to], ALU.mult))
                        nc.vector.tensor_tensor(qk[:, m, to], qk[:, m, to], tt, ALU.add).then_inc(q["rotary"], 1)

                    for n in range(nqk + 1):
                        if n < nqk:
                            norm(n)
                        if n >= 1:
                            rope(n - 1)

                    def evacuate(n):
                        i, m, c, width, diag = score_units[n]
                        if n == first_unit[i]:
                            if i >= RING:
                                dve.wait_ge(q["a_turned"], first_turn[i - RING + 1])
                            if i == 0:
                                dve.wait_ge(q["rotary"], nqk)
                            if i == 1:
                                dve.wait_ge(q["v_turned"], TB)
                        dve.wait_ge(q["scored"], n + 1)
                        to = S[:, i % RING, m, c * 512:c * 512 + width]
                        if diag:
                            ins = nc.vector.tensor_tensor_reduce(to, bank[n % 4][:, :width], const(g, "mask")[:, 512 - width:], 1.0, NEG,
                                                                 ALU.add, ALU.max, mx[:, i % RING, m, c:c + 1])
                        else:
                            ins = nc.vector.tensor_scalar(to, bank[n % 4][:, :width], 1.0, None, ALU.mult, ALU.max,
                                                          accum_out=mx[:, i % RING, m, c:c + 1])
                        ins.then_inc(q["evacuated"], 1)

                    def maxima(i):
                        dve.wait_ge(q["evacuated"], first_unit[i + 1])
                        if i >= RING:
                            dve.wait_ge(q["exped"], 2 * (i - RING) + 2)
                        nc.vector.tensor_reduce(nm[:, i % RING, :], mx[:, i % RING, :, :i // 4 + 1], AX, ALU.max, negate=True).then_inc(q["maxed"], 1)

                    def scales(i):
                        dve.wait_ge(q["exped"], 2 * i + 2)
                        link(nc.vector.reciprocal(den[:, i % RING, :], den[:, i % RING, :]))
                        nc.vector.tensor_tensor(den[:, i % RING, 1:2], den[:, i % RING, 1:2], gcol[:, 3:4], ALU.mult).then_inc(q["scaled"], 1)

                    def weigh(i):
                        n = (i + 1) * P
                        dve.wait_ge(q["pool_done"], i + 1)
                        nc.vector.scalar_tensor_tensor(S[:, i % RING, 0, :n], S[:, i % RING, 0, :n], den[:, i % RING, 0:1], S[:, i % RING, 1, :n],
                                                       ALU.mult, ALU.subtract).then_inc(q["weighed"], 1)

                    for i in range(2):
                        for n in range(first_unit[i], first_unit[i + 1]):
                            evacuate(n)
                        maxima(i)
                    scales(0)
                    weigh(0)
                    for i in range(NT - 1):
                        ahead = list(range(first_unit[i + 2], first_unit[i + 3])) if i + 2 < NT else []
                        half, most = len(ahead) // 2, len(ahead) * 3 // 4
                        for n in ahead[:half]:
                            evacuate(n)
                        scales(i + 1)
                        for n in ahead[half:most]:
                            evacuate(n)
                        weigh(i + 1)
                        for n in ahead[most:]:
                            evacuate(n)
                        if i + 2 < NT:
                            maxima(i + 2)
                    dve.wait_ge(q["o_rooted"], 1)
                    link(nc.vector.reciprocal(ss[:], ss[:]))
                    dve.wait_ge(q["o_copied"], NT)
                    for i in range(NT):
                        nc.vector.tensor_scalar(o[:, i, :], o[:, i, :], ss[:, i:i + 1], None, ALU.mult).then_inc(q["o_normed"], 1)
            s.end()


def cols(nc, sp, to, row, n, sem):
    sp.dma_start(to, row.rearrange("a (k p) -> p (a k)", p=P), allow_slow_non_contiguous=True).then_inc(sem, 16)


def stage_pool(nc, g, uc):
    w_in = g["w_in"][0].rearrange("(k p) n -> p k n", p=P)
    hT, yaT = g["hT"], g["yaT"]
    with Stage(nc, "pooling") as s:
        w = s.sb("w", [P, 2, KD, 256])
        ua = s.sb("ua", [P, 2, T])
        A, B = s.sb("A", [P, T]), s.sb("B", [P, T])
        pw = s.sb("pw", [P, 2, P])
        ps_col = s.sb("ps_col", [P, 2])
        first = s.sb("first", [P, 2, 16])
        bank = [s.ps(f"bank{i}", [P, 512]) for i in range(8)]
        w_ready = [s.sem("w_ready0"), s.sem("w_ready1")]
        small, zeroed, projected, copied = s.sem("small"), s.sem("zeroed"), s.sem("projected"), s.sem("copied")
        dve_done, pooled, mixed, placed = s.sem("dve_done"), s.sem("pooled"), s.sem("mixed"), s.sem("placed")
        units = [(m, c, tb) for m in range(2) for c in range(2) for tb in range(TB)]
        with nc.Block() as block:
            @block.sync
            def _(sp):
                sp.dma_start(w[:, 0], w_in[:, :, 0:256]).then_inc(w_ready[0], 16)
                sp.dma_start(w[:, 1], w_in[:, :, C0:C0 + 256]).then_inc(w_ready[1], 16)
                cols(nc, sp, ps_col[:], g["pool_scale"], 2, small)
                sp.wait_ge(zeroed, 1)
                for gr in range(4):
                    at = slice((gr % 2) * 64, (gr % 2) * 64 + 64)
                    sp.dma_start(pw[at, gr // 2, at], g["pool_w"][0, gr]).then_inc(small, 16)

            @block.gpsimd
            def _(pool):
                nc.gpsimd.memset(pw[:], 0.0).then_inc(zeroed, 1)

            @block.tensor
            def _(pe):
                for n, (m, c, tb) in enumerate(units):
                    if n % 8 == 0:
                        pe.wait_ge(w_ready[m], 16)
                    if n >= 6:
                        pe.wait_ge(copied, n - 5)
                    for k in range(KD):
                        mm = pe.matmul(bank[n % 6][:], w[:, m, k, c * P:(c + 1) * P], hT[:, k, tb * 512:(tb + 1) * 512],
                                       start=k == 0, stop=k == KD - 1)
                    mm.then_inc(projected, 1)
                pe.wait_ge(small, 16 * 5)
                for n in range(8):
                    c, tb = n // TB, n % TB
                    pe.wait_ge(pooled, c + 1)
                    if n >= 2:
                        pe.wait_ge(placed, n - 1)
                    pe.matmul(bank[6 + n % 2][:], pw[:, c, :], ua[:, c, tb * 512:(tb + 1) * 512], start=True, stop=True).then_inc(mixed, 1)

            @block.scalar
            def _(act):
                for n, (m, c, tb) in enumerate(units):
                    act.wait_ge(projected, n + 1)
                    nc.scalar.copy((ua if m == 0 else uc)[:, c, tb * 512:(tb + 1) * 512], bank[n % 6][:]).then_inc(copied, 1)
                act.wait_ge(small, 16 * 5)
                for n in range(8):
                    c, tb = n // TB, n % TB
                    act.wait_ge(mixed, n + 1)
                    nc.scalar.activation(yaT[:, c, tb * 512:(tb + 1) * 512], bank[6 + n % 2][:], ACT.Copy,
                                         scale=ps_col[:, c:c + 1]).then_inc(placed, 1)

            @block.vector
            def _(dve):
                link = Chain(dve, dve_done)

                def wider(to, frm, by, at=slice(0, P)):
                    link(nc.vector.tensor_copy(to[at, 0:by], frm[at, 0:by]))
                    link(nc.vector.tensor_tensor(to[at, by:], frm[at, by:], frm[at, :T - by], ALU.add))
                for c in range(2):
                    dve.wait_ge(copied, 4 * c + 4)
                    u = ua[:, c, :]
                    wider(A[:], u, 1)
                    if c == 1:
                        wider(B[:], A[:], 2)
                        wider(A[:], B[:], 4)
                        wider(B[:], A[:], 8, slice(64, P))
                    else:
                        wider(B[:], A[:], 2, slice(64, P))
                    for half, sums in ((slice(0, 64), A), (slice(64, P), B)):
                        cnt = const(g, "cnt")[half, c * 16:(c + 1) * 16]
                        link(nc.vector.tensor_tensor(first[half, c, :], sums[half, 0:16], cnt, ALU.mult))
                        link(nc.vector.tensor_tensor(first[half, c, :], first[half, c, :], u[half, 0:16], ALU.subtract))
                        link(nc.vector.scalar_tensor_tensor(u[half, :], sums[half, :], const(g, "width")[half, c:c + 1], u[half, :],
                                                            ALU.mult, ALU.subtract))
                        link(nc.vector.tensor_copy(u[half, 0:16], first[half, c, :]))
                    nc.vector.tensor_copy(first[:, c, :], u[:, 0:16]).then_inc(pooled, 1)
        s.end()


def stage_ssm(nc, g, uc):
    GU = 4
    LEVELS = (SC - 1).bit_length()
    with Stage(nc, "ssm") as s:
        UY = s.sb("UY", [P, 2, GROUPS, SL * 16])
        B1, B2 = s.sb("B1", [P, GROUPS, 16]), s.sb("B2", [P, GROUPS, 16])
        C1, C2 = s.sb("C1", [P, GROUPS, 16]), s.sb("C2", [P, GROUPS, 16])
        q1, q2 = s.sb("q1", [P, GROUPS, 16]), s.sb("q2", [P, GROUPS, 16])
        craw = s.sb("craw", [P, 2, 2, P])
        lam = s.sb("lam", [GROUPS, 2, P])
        lrli = s.sb("lrli", [P, 2, GROUPS])
        dt = s.sb("dt", [P, GROUPS])
        half_pi = s.sb("half_pi", [P, 1])
        pw = s.sb("pw", [P, 2, SL + 1, GROUPS])
        prev = s.sb("prev", [P, 2, GROUPS, SL])
        pfwd = s.sb("pfwd", [P, 2, GROUPS, SL])
        ap = s.sb("ap", [P, 2, LEVELS, GROUPS])
        t = [s.sb(f"t{i}", [P, GROUPS]) for i in range(6)]
        dcol = s.sb("dcol", [P, 2, 2])
        glu = s.sb("glu", [P, 2, 256])
        E = s.sb("E", [P, GU, 2 * SL, 16])
        Et = s.sb("Et", [P, GU, SL, 16])
        M2 = s.sb("M2", [P, GU, SL, 16])
        c1 = s.sb("c1", [P, GU, 16])
        M1 = s.sb("M1", [P, GU, P])
        TT = s.sb("TT", [P, GU, P])
        X = s.sb("X", [P, GU, SC + 1])
        RJ, R, ucp, U = (g["ycT"][:].rearrange("p a n -> p (a n)")[:, i * 1024:(i + 1) * 1024] for i in range(4))
        RJ = RJ.rearrange("p (a b n) -> p a b n", a=2, b=GU)
        R = R.rearrange("p (a b n) -> p a b n", a=2, b=GU)
        ucp = ucp.rearrange("p (a b n) -> p a b n", a=2, b=GU)
        U = U.rearrange("p (b n) -> p b n", b=GU)
        apt = s.sb("apt", [P, 2, LEVELS, GU])
        ycp = s.sb("ycp", [P, 2, 4, P])
        bank = [s.ps(f"bank{i}", [P, 512]) for i in range(8)]
        names = ("small dve_done act_done exped exped2 wrapped sined turned placed c_turned ready "
                 "e_ready u_copied u_turned u_placed m_turned m_placed k_summed k_placed v_summed v_placed "
                 "rj_ready r_ready stepped scanned y_summed y_placed m2_ready y_turned skipped squared "
                 "gated gelued glued opened").split()
        q = {n: s.sem(n) for n in names}

        with nc.Block() as block:
            @block.sync
            def _(sp):
                for j, n in enumerate(("lam_re", "lam_im")):
                    for r in range(2):
                        sp.dma_start(lam[:, j, r * 64:(r + 1) * 64], g[n][0]).then_inc(q["small"], 16)
                sp.dma_start(dt[:], g["log_dt"].broadcast_to([P, GROUPS])).then_inc(q["small"], 16)
                for to, names_ in ((q1, ("b_re", "b_im")), (q2, ("b_im", "b_re"))):
                    for r in range(2):
                        sp.dma_start(to[r * 64:(r + 1) * 64], g[names_[r]][0].rearrange("g p c -> p g c")).then_inc(q["small"], 16)
                for m, names_ in enumerate((("c_re", "c_im"), ("c_im", "c_re"))):
                    for r in range(2):
                        sp.dma_start(craw[:, m, :, r * 64:(r + 1) * 64],
                                     g[names_[r]][0].rearrange("(h g) c p -> (g c) h p", h=2)).then_inc(q["small"], 16)
                cols(nc, sp, dcol[:, 0, :], g["d_skip"], 2, q["small"])
                cols(nc, sp, dcol[:, 1, :], g["glu_b"], 2, q["small"])
                sp.dma_start(glu[:], g["glu_w"][0].rearrange("(k p) n -> p k n", p=P)).then_inc(q["small"], 16)

            @block.tensor
            def _(pe):
                n = 0
                for hc in range(2):
                    for f in range(2):
                        for j0 in range(0, SL, 4):
                            if n >= 4:
                                pe.wait_ge(q["placed"], n - 3)
                            v = uc[:, hc, f * 1024:(f + 1) * 1024].rearrange("p (n j) -> p j n", j=SL)
                            for j in range(4):
                                mm = pe.transpose(bank[n % 4][:, j * P:(j + 1) * P], v[:, j0 + j, :], const(g, "ident"))
                            mm.then_inc(q["turned"], 1)
                            n += 1
                pe.wait_ge(q["small"], 16 * 16)
                for j in range(2):
                    mm = pe.transpose(bank[4][:, j * 16:(j + 1) * 16], lam[:, j, :], const(g, "ident")[0:16, 0:16])
                mm.then_inc(q["c_turned"], 1)
                for m in range(2):
                    for hc in range(2):
                        mm = pe.transpose(bank[5][:, (2 * m + hc) * P:(2 * m + hc + 1) * P], craw[:, m, hc, :], const(g, "ident"))
                mm.then_inc(q["c_turned"], 1)

            @block.scalar
            def _(act):
                n = 0
                for hc in range(2):
                    for f in range(2):
                        for j0 in range(0, SL, 4):
                            act.wait_ge(q["turned"], n + 1)
                            for j in range(4):
                                ins = nc.scalar.copy(UY[:, f, hc * 8:(hc + 1) * 8, (j0 + j) * 16:(j0 + j + 1) * 16],
                                                     bank[n % 4][:, j * P:(j + 1) * P].rearrange("p (g c) -> p g c", c=16))
                            ins.then_inc(q["placed"], 1)
                            n += 1
                act.wait_ge(q["small"], 16 * 16)
                nc.scalar.activation(dt[:], dt[:], ACT.Exp).then_inc(q["exped"], 1)
                act.wait_ge(q["exped2"], 1)
                nc.scalar.activation(t[2][:], t[0][:], ACT.Exp).then_inc(q["exped"], 1)
                act.wait_ge(q["wrapped"], 1)
                nc.scalar.activation(t[3][:], t[1][:], ACT.Sin).then_inc(q["sined"], 1)
                nc.scalar.activation(t[5][:], t[4][:], ACT.Sin, scale=-1.0, bias=half_pi[:]).then_inc(q["sined"], 1)

            @block.vector
            def _(dve):
                link = Chain(dve, q["dve_done"])
                tt, ts = nc.vector.tensor_tensor, nc.vector.tensor_scalar
                link(nc.vector.memset(half_pi[:], math.pi / 2))
                link(nc.vector.memset(E[:], 0.0))
                link(nc.vector.memset(X[:], 0.0))
                dve.wait_ge(q["c_turned"], 1)
                link(nc.vector.tensor_copy(lrli[:].rearrange("p a b -> p (a b)"), bank[4][:, 0:32]))
                lr, li = lrli[:, 0, :], lrli[:, 1, :]
                dve.wait_ge(q["exped"], 1)
                link(tt(t[1][:], li, dt[:], ALU.mult))
                tt(t[0][:], lr, dt[:], ALU.mult).then_inc(q["exped2"], 1)
                wrap_angle(nc, link, t[1][:], t[4][:])
                nc.vector.scalar_tensor_tensor(t[4][:], t[1][:], -1.0, t[1][:], ALU.mult, ALU.max).then_inc(q["wrapped"], 1)
                dve.wait_ge(q["sined"], 2)
                dve.wait_ge(q["exped"], 2)
                link(nc.vector.memset(pw[:, 0, 0, :], 1.0))
                link(nc.vector.memset(pw[:, 1, 0, :], 0.0))
                ar, ai = pw[:, 0, 1, :], pw[:, 1, 1, :]
                link(tt(ar, t[2][:], t[5][:], ALU.mult))
                link(tt(ai, t[2][:], t[3][:], ALU.mult))

                def product(out_r, out_i, xr, xi, yr, yi):
                    link(tt(t[0][:], xr, yr, ALU.mult))
                    link(tt(t[1][:], xi, yi, ALU.mult))
                    link(tt(t[2][:], xr, yi, ALU.mult))
                    link(tt(t[3][:], xi, yr, ALU.mult))
                    link(tt(out_r, t[0][:], t[1][:], ALU.subtract))
                    link(tt(out_i, t[2][:], t[3][:], ALU.add))
                for n in range(2, SL + 1):
                    product(pw[:, 0, n, :], pw[:, 1, n, :], pw[:, 0, n // 2, :], pw[:, 1, n // 2, :],
                            pw[:, 0, n - n // 2, :], pw[:, 1, n - n // 2, :])
                for r in range(2):
                    link(nc.vector.tensor_copy(ap[:, r, 0, :], pw[:, r, SL, :]))
                    link(nc.vector.tensor_copy(pfwd[:, r].rearrange("p g n -> p n g"), pw[:, r, 1:SL + 1, :]))
                    for n in range(SL):
                        link(nc.vector.tensor_copy(prev[:, r, :, SL - 1 - n], pw[:, r, n, :]))
                for n in range(1, LEVELS):
                    product(ap[:, 0, n, :], ap[:, 1, n, :], ap[:, 0, n - 1, :], ap[:, 1, n - 1, :],
                            ap[:, 0, n - 1, :], ap[:, 1, n - 1, :])
                link(ts(t[4][:], ar, -1.0, None, ALU.add))
                link(tt(t[0][:], lr, lr, ALU.mult))
                link(tt(t[1][:], li, li, ALU.mult))
                link(tt(t[0][:], t[0][:], t[1][:], ALU.add))
                link(nc.vector.reciprocal(t[5][:], t[0][:]))
                link(tt(t[0][:], t[4][:], lr, ALU.mult))
                link(tt(t[1][:], ai, li, ALU.mult))
                link(tt(t[0][:], t[0][:], t[1][:], ALU.add))
                link(tt(t[2][:], t[0][:], t[5][:], ALU.mult))
                link(tt(t[0][:], ai, lr, ALU.mult))
                link(tt(t[1][:], t[4][:], li, ALU.mult))
                link(tt(t[0][:], t[0][:], t[1][:], ALU.subtract))
                link(tt(t[3][:], t[0][:], t[5][:], ALU.mult))
                kr = t[2][:].unsqueeze(2).broadcast_to([P, GROUPS, 16])
                ki = t[3][:].unsqueeze(2).broadcast_to([P, GROUPS, 16])
                link(ts(q2[:], q2[:], const(g, "upper"), None, ALU.mult))
                link(tt(B1[:], q1[:], kr, ALU.mult))
                link(tt(C2[:], q2[:], ki, ALU.mult))
                link(tt(B1[:], B1[:], C2[:], ALU.add))
                link(tt(B2[:], q2[:], kr, ALU.mult))
                link(tt(C2[:], q1[:], ki, ALU.mult))
                link(tt(B2[:], B2[:], C2[:], ALU.subtract))
                dve.wait_ge(q["c_turned"], 2)
                link(ts(C1[:].rearrange("p g c -> p (g c)"), bank[5][:, 0:256], const(g, "upper"), -1.0, ALU.mult, ALU.mult))
                link(ts(C2[:].rearrange("p g c -> p (g c)"), bank[5][:, 256:512], -1.0, None, ALU.mult))
        s.end()

        with nc.Fori(0, GROUPS // GU) as turn:
            with nc.Block() as block:
                mine = bass.ds(turn * GU, GU)

                @block.vector
                def _(dve):
                    link = Chain(dve, q["dve_done"])
                    tt = nc.vector.tensor_tensor

                    def by_power(out, tmp, p2, b1, b2, sem):
                        def pb(r):
                            return p2[:, r, mine, :].unsqueeze(3).broadcast_to([P, GU, SL, 16])

                        def bb(b):
                            return b[:, mine, :].unsqueeze(2).broadcast_to([P, GU, SL, 16])
                        link(tt(out, pb(0), bb(b1), ALU.mult))
                        link(tt(tmp, pb(1), bb(b2), ALU.mult))
                        tt(out, out, tmp, ALU.add).then_inc(sem, 1)
                    by_power(E[:, :, 0:SL, :], Et[:], prev, B1, B2, q["e_ready"])
                    link(nc.vector.tensor_copy(apt[:], ap[:, :, :, mine]))
                    dve.wait_ge(q["e_ready"], 1)
                    by_power(M2[:], Et[:], pfwd, C1, C2, q["m2_ready"])
                    dve.wait_ge(q["m_turned"], 1)
                    nc.vector.tensor_copy(M1[:].rearrange("p g n -> p (g n)"), bank[2][:]).then_inc(q["m_placed"], 1)
                    dve.wait_ge(q["k_summed"], 1)
                    nc.vector.tensor_copy(TT[:].rearrange("p g n -> p (g n)"), bank[3][:]).then_inc(q["k_placed"], 1)
                    for b in range(2):
                        dve.wait_ge(q["v_summed"], b + 1)
                        nc.vector.tensor_copy(X[:, 2 * b:2 * b + 2, 1:], bank[4 + b][:].rearrange("p (g n) -> p g n", g=2)).then_inc(q["scanned"], 1)
                    for lv in range(LEVELS):
                        if lv >= 2:
                            dve.wait_ge(q["stepped"], 2 * lv - 2)
                        for gi in range(GU):
                            dve.wait_ge(q["rj_ready"], GU * lv + gi + 1)
                            nc.vector.scalar_tensor_tensor(R[:, lv % 2, gi, :], const(g, "ident"), apt[:, 0, lv, gi:gi + 1],
                                                           RJ[:, lv % 2, gi, :], ALU.mult, ALU.add).then_inc(q["r_ready"], 1)
                        by = 1 << lv
                        for b in range(2):
                            dve.wait_ge(q["stepped"], 2 * lv + b + 1)
                            dve.wait_ge(q["scanned"], 2 * lv + b + 1)
                            gs = slice(2 * b, 2 * b + 2)
                            tt(X[:, gs, 1 + by:], X[:, gs, 1 + by:],
                               bank[(lv % 2) * 2 + b][:].rearrange("p (g n) -> p g n", g=2)[:, :, :SC - by], ALU.add).then_inc(q["scanned"], 1)

                @block.scalar
                def _(act):
                    nc.scalar.copy(ucp[:], UY[:, :, mine, :]).then_inc(q["u_copied"], 1)
                    nc.scalar.copy(c1[:], C1[:, mine, :]).then_inc(q["u_copied"], 1)
                    for b in range(2):
                        act.wait_ge(q["u_turned"], b + 1)
                        nc.scalar.copy(U[:, 2 * b:2 * b + 2, :].rearrange("p g n -> p (g n)"), bank[b][:]).then_inc(q["u_placed"], 1)
                    act.wait_ge(q["m2_ready"], 1)
                    for lv in range(LEVELS):
                        for gi in range(GU):
                            if lv >= 2:
                                act.wait_ge(q["r_ready"], GU * (lv - 2) + gi + 1)
                            nc.scalar.activation(RJ[:, lv % 2, gi, :], const(g, "swap"), ACT.Copy,
                                                 scale=apt[:, 1, lv, gi:gi + 1]).then_inc(q["rj_ready"], 1)
                    for f in range(2):
                        act.wait_ge(q["y_summed"], f + 1)
                        nc.scalar.copy(UY[:, f, mine, :], bank[6 + f][:].rearrange("p (g n) -> p g n", g=GU)).then_inc(q["y_placed"], 1)

                @block.tensor
                def _(pe):
                    ident = const(g, "ident")
                    pe.wait_ge(q["u_copied"], 2)
                    for b in range(2):
                        for gi in (2 * b, 2 * b + 1):
                            for f in range(2):
                                at = (gi % 2) * SC + f * P
                                mm = pe.transpose(bank[b][:, at:at + P], ucp[:, f, gi, :], ident)
                        mm.then_inc(q["u_turned"], 1)
                    pe.wait_ge(q["e_ready"], 1)
                    for gi in range(GU):
                        mm = pe.transpose(bank[2][:, gi * P:(gi + 1) * P], E[:, gi, 0:SL, :].rearrange("p s c -> p (s c)"), ident)
                    mm.then_inc(q["m_turned"], 1)
                    for gi in range(GU):
                        for i in range(SL):
                            at = gi * P + i * 16
                            mm = pe.matmul(bank[3][:, at:at + 16], E[:, gi, SL - 1 - i:2 * SL - 1 - i, :].rearrange("p s c -> p (s c)"),
                                           c1[:, gi, :], start=True, stop=True)
                    mm.then_inc(q["k_summed"], 1)
                    pe.wait_ge(q["m_placed"], 1)
                    for b in range(2):
                        pe.wait_ge(q["u_placed"], b + 1)
                        for gi in (2 * b, 2 * b + 1):
                            mm = pe.matmul(bank[4 + b][:, (gi % 2) * SC:(gi % 2 + 1) * SC], M1[:, gi, :], U[:, gi, :], start=True, stop=True)
                        mm.then_inc(q["v_summed"], 1)
                    pe.wait_ge(q["k_placed"], 1)
                    for lv in range(LEVELS):
                        by = 1 << lv
                        for b in range(2):
                            pe.wait_ge(q["scanned"], 2 * lv + b + 1)
                            for gi in (2 * b, 2 * b + 1):
                                pe.wait_ge(q["r_ready"], GU * lv + gi + 1)
                                at = (gi % 2) * SC
                                mm = pe.matmul(bank[(lv % 2) * 2 + b][:, at:at + SC - by], R[:, lv % 2, gi, :],
                                               X[:, gi, 1:1 + SC - by], start=True, stop=True)
                            mm.then_inc(q["stepped"], 1)
                    pe.wait_ge(q["scanned"], 2 * LEVELS + 2)
                    for f in range(2):
                        for gi in range(GU):
                            to = bank[6 + f][:, gi * P:(gi + 1) * P]
                            pe.matmul(to, U[:, gi, f * P:(f + 1) * P], TT[:, gi, :], start=True, stop=False)
                            mm = pe.matmul(to, X[:, gi, f * P:(f + 1) * P], M2[:, gi].rearrange("p i c -> p (i c)"),
                                           start=False, stop=True)
                        mm.then_inc(q["y_summed"], 1)
            s.end()

        ycT = g["ycT"]
        G2 = 2 * math.sqrt(2 / math.pi)
        with nc.Block() as block:
            units = [(hc, f, i0) for hc in range(2) for f in range(2) for i0 in (0, 4)]

            @block.tensor
            def _(pe):
                for n, (hc, f, i0) in enumerate(units):
                    if n >= 4:
                        pe.wait_ge(q["skipped"], n - 3)
                    pe.wait_ge(q["u_copied"], n + 1)
                    for i in range(4):
                        mm = pe.transpose(bank[n % 4][:, i * P:(i + 1) * P], ycp[:, n % 2, i, :], const(g, "ident"))
                    mm.then_inc(q["y_turned"], 1)
                for n in range(8):
                    c, tb = n % 2, n // 2
                    pe.wait_ge(q["gelued"], 4 + tb + 1)
                    if n >= 4:
                        pe.wait_ge(q["glued"], n - 3)
                    for k in range(2):
                        mm = pe.matmul(bank[4 + n % 4][:], glu[:, k, c * P:(c + 1) * P], ycT[:, k, tb * 512:(tb + 1) * 512],
                                       start=k == 0, stop=k == 1)
                    mm.then_inc(q["opened"], 1)

            @block.vector
            def _(dve):
                link = Chain(dve, q["dve_done"])
                for n, (hc, f, i0) in enumerate(units):
                    dve.wait_ge(q["y_turned"], n + 1)

                    def tokens(a):
                        return a[:, hc, f * 1024:(f + 1) * 1024].rearrange("p (n i) -> p i n", i=SL)[:, i0:i0 + 4, :]
                    nc.vector.scalar_tensor_tensor(tokens(ycT), tokens(uc), dcol[:, 0, hc:hc + 1],
                                                   bank[n % 4][:].rearrange("p (i n) -> p i n", i=4), ALU.mult, ALU.add).then_inc(q["skipped"], 1)
                dve.wait_ge(q["skipped"], 8)
                for n in range(8):
                    c, tb = n // 4, n % 4
                    y = ycT[:, c, tb * 512:(tb + 1) * 512]
                    b = uc[:, c, tb * 512:(tb + 1) * 512]
                    link(nc.vector.tensor_tensor(b, y, y, ALU.mult))
                    link(nc.vector.tensor_scalar(b, b, 0.044715, 1.0, ALU.mult, ALU.add))
                    nc.vector.tensor_tensor(b, b, y, ALU.mult).then_inc(q["squared"], 1)
                for n in range(8):
                    c, tb = n // 4, n % 4
                    y = ycT[:, c, tb * 512:(tb + 1) * 512]
                    b = uc[:, c, tb * 512:(tb + 1) * 512]
                    dve.wait_ge(q["gated"], n + 1)
                    nc.vector.tensor_tensor(y, y, b, ALU.mult).then_inc(q["gelued"], 1)
                for n in range(8):
                    c, tb = n % 2, n // 2
                    y = ycT[:, c, tb * 512:(tb + 1) * 512]
                    b = uc[:, c, tb * 512:(tb + 1) * 512]
                    dve.wait_ge(q["opened"], n - n % 2 + 2)
                    dve.wait_ge(q["glued"], n + 1)
                    nc.vector.tensor_tensor(y, y, b, ALU.mult).then_inc(q["ready"], 1)

            @block.scalar
            def _(act):
                for n, (hc, f, i0) in enumerate(units):
                    if n >= 2:
                        act.wait_ge(q["y_turned"], n - 1)
                    for i in range(4):
                        ins = nc.scalar.copy(ycp[:, n % 2, i, :].rearrange("p (g c) -> p g c", c=16),
                                             UY[:, f, hc * 8:(hc + 1) * 8, (i0 + i) * 16:(i0 + i + 1) * 16])
                    ins.then_inc(q["u_copied"], 1)
                for n in range(8):
                    c, tb = n // 4, n % 4
                    b = uc[:, c, tb * 512:(tb + 1) * 512]
                    act.wait_ge(q["squared"], n + 1)
                    nc.scalar.activation(b, b, ACT.Sigmoid, scale=G2).then_inc(q["gated"], 1)
                for n in range(8):
                    c, tb = n % 2, n // 2
                    act.wait_ge(q["opened"], n + 1)
                    act.wait_ge(q["gelued"], 4 * c + tb + 1)
                    nc.scalar.activation(uc[:, c, tb * 512:(tb + 1) * 512], bank[4 + n % 4][:], ACT.Sigmoid,
                                         bias=dcol[:, 1, c:c + 1]).then_inc(q["glued"], 1)
        s.end()


def stage_merge(nc, g):
    hT = g["hT"]
    gate_w = g["gate_w"][0].rearrange("(k p) (b n) -> p b k n", p=P, b=3)
    projs = [g[n][0].rearrange("(k p) n -> p k n", p=P) for n in ("proj_a", "proj_b", "proj_c")]
    ks = [(0, 2), (2, 4), (6, 2)]
    with Stage(nc, "merge") as s:
        wg = s.sb("wg", [P, 2, 3, KD, P])
        wp = s.sb("wp", [P, 2, KD, P])
        gb = s.sb("gb", [P, 3, KD])
        gbt = s.sb("gbt", [P, 3, 2])
        sg = s.sb("sg", [P, 2, 512])
        pr = s.sb("pr", [P, 512])
        mx = s.sb("mx", [P, 2, 512])
        bank = [s.ps(f"bank{i}", [P, 512]) for i in range(8)]
        w_ready = [s.sem("w_ready0"), s.sem("w_ready1")]
        small, biased, summed, gated, multiplied, mixed = (s.sem(n) for n in "small biased summed gated multiplied mixed".split())
        dve_done = s.sem("dve_done")
        stored = [s.sem("stored0"), s.sem("stored1")]
        units = [(u, tb, br) for u in range(2) for tb in range(TB) for br in range(3)]

        def load(sp, u, j):
            for br in range(3):
                sp.dma_start(wg[:, u, br], gate_w[:, br, :, bass.ds(j * P, P)]).then_inc(w_ready[u], 16)
                k0, kn = ks[br]
                sp.dma_start(wp[:, u, k0:k0 + kn], projs[br][:, :, bass.ds(j * P, P)]).then_inc(w_ready[u], 16)

        with nc.Block() as block:
            @block.sync
            def _(sp):
                sp.dma_start(gb[:].rearrange("p b k -> p (b k)"), g["gate_b"].rearrange("a (k p) -> p (a k)", p=P),
                             allow_slow_non_contiguous=True).then_inc(small, 16)
                load(sp, 0, 0)
                sp.wait_ge(small, 16)
                sp.wait_ge(w_ready[0], 96)
        s.end()
        with nc.Fori(0, KD // 2) as turn:
            with nc.Block() as block:
                @block.sync
                def _(sp):
                    load(sp, 1, turn * 2 + 1)
                    for m in range(2 * TB):
                        u, tb = m // TB, m % TB
                        if m == TB:
                            sp.wait_ge(summed, 12)
                            load(sp, 0, (turn + 1) % (KD // 2) * 2)
                        sp.wait_ge(mixed, m + 1)
                        sp.dma_start(g["mixT"][:, bass.ds(turn * 2 + u, 1), tb * 512:(tb + 1) * 512].rearrange("p a n -> p (a n)"),
                                     mx[:, m % 2, :]).then_inc(stored[m % 2], 16)
                    for b in range(2):
                        sp.wait_ge(stored[b], 16 * TB)
                    sp.wait_ge(w_ready[1], 96)
                    sp.wait_ge(w_ready[0], 96)

                @block.tensor
                def _(pe):
                    for n, (u, tb, br) in enumerate(units):
                        if n == 12:
                            pe.wait_ge(w_ready[1], 96)
                        if n >= 4:
                            pe.wait_ge(multiplied, n - 3)
                        for k in range(KD):
                            mm = pe.matmul(bank[2 * (n % 4)][:], wg[:, u, br, k, :], hT[:, k, tb * 512:(tb + 1) * 512],
                                           start=k == 0, stop=k == KD - 1)
                        k0, kn = ks[br]
                        y = (g["yaT"], g["ybT"], g["ycT"])[br]
                        for k in range(kn):
                            mm = pe.matmul(bank[2 * (n % 4) + 1][:], wp[:, u, k0 + k, :], y[:, k, tb * 512:(tb + 1) * 512],
                                           start=k == 0, stop=k == kn - 1)
                        mm.then_inc(summed, 1)

                @block.scalar
                def _(act):
                    act.wait_ge(biased, 1)
                    for n, (u, tb, br) in enumerate(units):
                        act.wait_ge(summed, n + 1)
                        if n >= 2:
                            act.wait_ge(multiplied, n - 1)
                        nc.scalar.activation(sg[:, n % 2, :], bank[2 * (n % 4)][:], ACT.Sigmoid, bias=gbt[:, br, u:u + 1]).then_inc(gated, 1)

                @block.vector
                def _(dve):
                    link = Chain(dve, dve_done)
                    nc.vector.tensor_copy(gbt[:], gb[:, :, bass.ds(turn * 2, 2)]).then_inc(biased, 1)
                    for n, (u, tb, br) in enumerate(units):
                        m = n // 3
                        if br == 0 and m >= 2:
                            dve.wait_ge(stored[m % 2], 16 * (m // 2))
                        dve.wait_ge(gated, n + 1)
                        to = mx[:, m % 2, :] if br == 0 else pr[:]
                        if br == 2:
                            dve.wait_ge(dve_done, 2 * m + 1)
                        nc.vector.tensor_tensor(to, sg[:, n % 2, :], bank[2 * (n % 4) + 1][:], ALU.mult).then_inc(multiplied, 1)
                        dve.wait_ge(multiplied, n + 1)
                        if br == 1:
                            nc.vector.tensor_tensor(mx[:, m % 2, :], mx[:, m % 2, :], pr[:], ALU.add).then_inc(dve_done, 1)
                        if br == 2:
                            nc.vector.tensor_tensor(mx[:, m % 2, :], mx[:, m % 2, :], pr[:], ALU.add).then_inc(dve_done, 1)
                            dve.wait_ge(dve_done, 2 * m + 2)
                            dve.sem_inc(mixed, 1)
            s.end()


def stage_out(nc, g, lg):
    U = 4
    x_t = g["x"][0].rearrange("(t p) n -> p t n", p=P)
    x1_t = g["x1"].rearrange("(t p) n -> p t n", p=P)
    h2_t = g["h2"].rearrange("(t p) n -> p t n", p=P)
    with Stage(nc, "out") as s:
        w = s.sb("w", [P, KD, D])
        rows = s.sb("rows", [P, 3, D])
        wr = s.sb("wr", [P, KD, 36])
        mT = s.sb("mT", [P, U, KD, P])
        x = s.sb("x", [P, U, D])
        h2 = s.sb("h2", [P, 2, D])
        t = s.sb("t", [P, D])
        h2T = s.sb("h2T", [P, 2, KD, P])
        sq = s.sb("sq", [P, D])
        ss = s.sb("ss", [P, U])
        eps = s.sb("eps", [P, 1])
        bank = [s.ps(f"bank{i}", [P, 512]) for i in range(8)]
        names = ("small dve_done act_done summed added squared rooted scaled shifted turned placed routed logged stored_x").split()
        q = {n: s.sem(n) for n in names}
        m_ready = [s.sem(f"m_ready{i}") for i in range(U)]
        x_ready = [s.sem(f"x_ready{i}") for i in range(U)]
        stored = [s.sem("stored0"), s.sem("stored1")]

        def load_m(sp, i, turn):
            sp.dma_start(mT[:, i], g["mixT"][:, :, bass.ds(turn * 512 + i * P, P)]).then_inc(m_ready[i], 16)

        with nc.Block() as block:
            @block.sync
            def _(sp):
                sp.dma_start(w[:], g["w_out"][0].rearrange("(k p) n -> p k n", p=P)).then_inc(q["small"], 16)
                for i, r in enumerate((0, 1, 2)):
                    sp.dma_start(rows[:, i, :], g["rows"][r:r + 1, :].broadcast_to([P, D])).then_inc(q["small"], 16)
                sp.dma_start(wr[:, :, 0:4], g["router_g_w"][0].rearrange("(k p) n -> p k n", p=P)).then_inc(q["small"], 16)
                sp.dma_start(wr[:, :, 4:36], g["router_e_w"][0].rearrange("(k p) n -> p k n", p=P)).then_inc(q["small"], 16)
                for i in range(U):
                    load_m(sp, i, 0)
                sp.wait_ge(q["small"], 96)
                for i in range(U):
                    sp.wait_ge(m_ready[i], 16)

            @block.gpsimd
            def _(pool):
                nc.gpsimd.memset(eps[:], EPS).then_inc(q["logged"], 1)
        s.end()
        with nc.Fori(0, NT // U) as turn:
            with nc.Block() as block:
                @block.sync
                def _(sp):
                    for i in range(U):
                        sp.dma_start(x[:, i, :], x_t[:, bass.ds(turn * U + i, 1), :].rearrange("p a n -> p (a n)")).then_inc(x_ready[i], 16)
                    nxt = (turn + 1) % (NT // U)
                    for i in range(U + 1):
                        if i < U:
                            sp.wait_ge(q["summed"], 2 * i + 2)
                            load_m(sp, i, nxt)
                        if i >= 1:
                            j = i - 1
                            sp.wait_ge(q["stored_x"], j + 1)
                            sp.dma_start(x1_t[:, bass.ds(turn * U + j, 1), :].rearrange("p a n -> p (a n)"), x[:, j, :]).then_inc(q["small"], 16)
                            sp.wait_ge(q["shifted"], j + 1)
                            sp.dma_start(h2_t[:, bass.ds(turn * U + j, 1), :].rearrange("p a n -> p (a n)"), h2[:, j % 2, :]).then_inc(stored[j % 2], 16)
                    for b in range(2):
                        sp.wait_ge(stored[b], 16 * U // 2)
                    sp.wait_ge(q["small"], 16 * U)
                    for i in range(U):
                        sp.wait_ge(m_ready[i], 16)

                @block.tensor
                def _(pe):
                    def product(i):
                        for nh in range(2):
                            b = (i % 2) * 2 + nh
                            if i >= 2:
                                pe.wait_ge(q["added"], 2 * (i - 2) + nh + 1)
                            for k in range(KD):
                                mm = pe.matmul(bank[b][:], mT[:, i, k, :], w[:, k, nh * 512:(nh + 1) * 512], start=k == 0, stop=k == KD - 1)
                            mm.then_inc(q["summed"], 1)

                    def route(i):
                        pe.wait_ge(q["shifted"], i + 1)
                        for half in range(2):
                            if i >= 1:
                                pe.wait_ge(q["placed"], 2 * (i - 1) + half + 1)
                            for j in range(4):
                                k = half * 4 + j
                                mm = pe.transpose(bank[4 + half][:, j * P:(j + 1) * P], h2[:, i % 2, k * P:(k + 1) * P], const(g, "ident"))
                            mm.then_inc(q["turned"], 1)
                        pe.wait_ge(q["placed"], 2 * i + 2)
                        if i >= 2:
                            pe.wait_ge(q["logged"], i - 1)
                        for k in range(KD):
                            mm = pe.matmul(bank[6 + i % 2][:, 0:36], h2T[:, i % 2, k, :], wr[:, k, :], start=k == 0, stop=k == KD - 1)
                        mm.then_inc(q["routed"], 1)
                    product(0)
                    for i in range(U):
                        if i + 1 < U:
                            product(i + 1)
                        route(i)

                @block.vector
                def _(dve):
                    link = Chain(dve, q["dve_done"])
                    for i in range(U):
                        dve.wait_ge(x_ready[i], 16)
                        for nh in range(2):
                            at = slice(nh * 512, (nh + 1) * 512)
                            dve.wait_ge(q["summed"], 2 * i + nh + 1)
                            if i >= 1:
                                dve.wait_ge(q["stored_x"], i)
                            nc.vector.tensor_tensor(t[:, at], bank[(i % 2) * 2 + nh][:], rows[:, 0, at], ALU.mult).then_inc(q["added"], 1)
                        dve.wait_ge(q["added"], 2 * i + 2)
                        nc.vector.tensor_tensor(x[:, i, :], x[:, i, :], t[:], ALU.add).then_inc(q["stored_x"], 1)
                        dve.wait_ge(q["rooted"], i + 1)
                        link(nc.vector.reciprocal(ss[:, i:i + 1], ss[:, i:i + 1]))
                        if i >= 2:
                            dve.wait_ge(q["turned"], 2 * i - 2)
                            dve.wait_ge(stored[i % 2], 16)
                        nc.vector.scalar_tensor_tensor(h2[:, i % 2, :], x[:, i, :], ss[:, i:i + 1], rows[:, 2, :], ALU.mult, ALU.mult).then_inc(q["scaled"], 1)

                @block.gpsimd
                def _(pool):
                    for i in range(U):
                        pool.wait_ge(q["scaled"], i + 1)
                        nc.gpsimd.tensor_tensor(h2[:, i % 2, :], h2[:, i % 2, :], rows[:, 1, :], ALU.add).then_inc(q["shifted"], 1)

                @block.scalar
                def _(act):
                    link = Chain(act, q["act_done"])
                    for i in range(U + 1):
                        if i < U:
                            act.wait_ge(q["stored_x"], i + 1)
                            if i >= 1:
                                act.wait_ge(q["squared"], i)
                            nc.scalar.activation(sq[:], x[:, i, :], ACT.Square, accum_out=ss[:, i:i + 1]).then_inc(q["squared"], 1)
                            act.wait_ge(q["squared"], i + 1)
                            nc.scalar.activation(ss[:, i:i + 1], ss[:, i:i + 1], ACT.Sqrt, scale=1.0 / D, bias=eps[:]).then_inc(q["rooted"], 1)
                        if i >= 1:
                            j = i - 1
                            for half in range(2):
                                act.wait_ge(q["turned"], 2 * j + half + 1)
                                if j >= 2:
                                    act.wait_ge(q["routed"], j - 1)
                                nc.scalar.copy(h2T[:, j % 2, half * 4:half * 4 + 4, :], bank[4 + half][:].rearrange("p (a n) -> p a n", n=P)).then_inc(q["placed"], 1)
                            act.wait_ge(q["routed"], j + 1)
                            nc.scalar.copy(lg[:, bass.ds(turn * U + j, 1), :].rearrange("p a n -> p (a n)"), bank[6 + j % 2][:, 0:36]).then_inc(q["logged"], 1)
            s.end()


def stage_route(nc, g, r, lg):
    NB = 72
    with Stage(nc, "route") as s:
        rb = s.sb("rb", [P, 36])
        gm, sm = s.sb("gm", [P, NT]), s.sb("sm", [P, NT])
        eg = s.sb("eg", [P, NT, 4])
        cand = s.sb("cand", [P, NT, 4])
        em = s.sb("em", [P, NT, 32])
        top = s.sb("top", [P, NT, 8])
        idx = s.sb("idx", [P, NT, 8], U32)
        ef = s.sb("ef", [P, 2, NT])
        O = s.sb("O", [P, 2, NT, NE])
        M = s.sb("M", [P, NT, NE])
        rank = s.sb("rank", [P, NT, NE])
        pre = s.sb("pre", [P, NT + 1, NE])
        cs = s.sb("cs", [P, NT, NE])
        ti = s.sb("ti", [P, NE], I32)
        nb = s.sb("nb", [P, NE])
        e0, e1 = s.sb("e0", [P, NE]), s.sb("e1", [P, NE])
        dest = s.sb("dest", [P, 2, NT])
        at = s.sb("at", [P, 2, NT], I32)
        hi = s.sb("hi", [P, 2, NT], I32)
        scat = s.sb("scat", [P, 2, NT], U32)
        tok = s.sb("tok", [P, NT], U32)
        zero = s.sb("zero", [P, NB], U32)
        cmp = s.sb("cmp", [1, 96, NE])
        blk = s.sb("blk", [1, 96])
        pa, pb = s.ps("pa", [P, 512]), s.ps("pb", [P, 512])
        names = "small dve_done act_done shifted exped diffed exped2 counted ranked placed ready zeroed".split()
        q = {n: s.sem(n) for n in names}
        q["scattered"] = s.kept_sem("scattered")
        with nc.Block() as block:
            @block.sync
            def _(sp):
                sp.dma_start(rb[:, 0:4], g["router_g_b"].broadcast_to([P, 4])).then_inc(q["small"], 16)
                sp.dma_start(rb[:, 4:36], g["router_e_b"].broadcast_to([P, 32])).then_inc(q["small"], 16)

            @block.scalar
            def _(act):
                act.wait_ge(q["shifted"], 1)
                nc.scalar.activation(eg[:], eg[:], ACT.Exp).then_inc(q["exped"], 1)
                act.wait_ge(q["diffed"], 1)
                nc.scalar.activation(sm[:], sm[:], ACT.Exp).then_inc(q["exped2"], 1)

            @block.tensor
            def _(pe):
                pe.wait_ge(q["counted"], 1)
                m = M[:].rearrange("p t e -> p (t e)")
                pe.matmul(pa[:], const(g, "before"), m, start=True, stop=True).then_inc(q["ranked"], 1)
                pe.matmul(pb[:], const(g, "ones"), m, start=True, stop=True).then_inc(q["ranked"], 1)

            @block.gpsimd
            def _(pool):
                nc.gpsimd.memset(zero[:], 0.0).then_inc(q["zeroed"], 1)
                pool.wait_ge(q["zeroed"], 1)
                pool.dma_start(g["slots"].rearrange("(p b) a -> p (b a)", p=P), zero[:]).then_inc(q["scattered"], 16)
                pool.wait_ge(q["scattered"], 16)
                pool.wait_ge(q["ready"], 1)
                for a in range(2):
                    for t in range(NT):
                        pool.indirect_dma_start(out=g["slots"], out_offset=bass.IndirectOffsetOnAxis(ap=scat[:, a, t:t + 1], axis=0),
                                                in_=tok[:, t:t + 1], in_offset=None).then_inc(q["scattered"], 16)
                pool.wait_ge(q["scattered"], 16 * (1 + 2 * NT))
                pool.dma_start(r["slot_tok"][:], g["slots"].rearrange("(p b) a -> p (b a)", p=P)).then_inc(q["scattered"], 16)
                pool.wait_ge(q["scattered"], 16 * (2 + 2 * NT))

            @block.vector
            def _(dve):
                link = Chain(dve, q["dve_done"])
                tt, ts = nc.vector.tensor_tensor, nc.vector.tensor_scalar

                def over(a, shape):
                    return a.unsqueeze(2).broadcast_to(shape)
                link(nc.vector.tensor_copy(tok[:], const(g, "tok")))
                dve.wait_ge(q["small"], 32)
                link(tt(lg[:], lg[:], rb[:].unsqueeze(1).broadcast_to([P, NT, 36]), ALU.add))
                gl, el = lg[:, :, 0:4], lg[:, :, 4:36]
                link(nc.vector.tensor_reduce(gm[:], gl, AX, ALU.max))
                link(tt(cand[:], gl, over(gm[:], [P, NT, 4]), ALU.is_equal))
                tt(eg[:], gl, over(gm[:], [P, NT, 4]), ALU.subtract).then_inc(q["shifted"], 1)
                link(ts(cand[:], cand[:], -1000.0, None, ALU.mult))
                link(tt(cand[:], cand[:], const(g, "iota")[:, 0:4].unsqueeze(1).broadcast_to([P, NT, 4]), ALU.add))
                link(nc.vector.tensor_reduce(gm[:], cand[:], AX, ALU.min))
                link(tt(cand[:], cand[:], over(gm[:], [P, NT, 4]), ALU.is_equal))
                link(ts(cand[:], cand[:], -NEG, NEG, ALU.mult, ALU.add))
                for k in range(8):
                    link(tt(em[:].rearrange("p t (a b) -> p t a b", b=8)[:, :, :, k],
                            el.rearrange("p t (a b) -> p t a b", b=8)[:, :, :, k], cand[:], ALU.add))
                for t in range(NT):
                    link(nc.vector.max(top[:, t, :], em[:, t, :]))
                    link(nc.vector.max_index(idx[:, t, :], top[:, t, :], em[:, t, :]))
                dve.wait_ge(q["exped"], 1)
                link(nc.vector.tensor_reduce(gm[:], eg[:], AX, ALU.add))
                tt(sm[:], top[:, :, 1], top[:, :, 0], ALU.subtract).then_inc(q["diffed"], 1)
                dve.wait_ge(q["exped2"], 1)
                link(ts(r["wt"][:, 0, :], sm[:], 1.0, None, ALU.add))
                link(tt(r["wt"][:, 0, :], r["wt"][:, 0, :], gm[:], ALU.mult))
                link(nc.vector.reciprocal(r["wt"][:, 0, :], r["wt"][:, 0, :]))
                link(tt(r["wt"][:, 1, :], r["wt"][:, 0, :], sm[:], ALU.mult))
                for a in range(2):
                    link(nc.vector.tensor_copy(ef[:, a, :], idx[:, :, a]))
                    link(tt(O[:, a], const(g, "iota").unsqueeze(1).broadcast_to([P, NT, NE]), over(ef[:, a, :], [P, NT, NE]), ALU.is_equal))
                tt(M[:], O[:, 0], O[:, 1], ALU.add).then_inc(q["counted"], 1)
                link(nc.vector.memset(pre[:, 0, :], 0.0))
                dve.wait_ge(q["ranked"], 2)
                link(nc.vector.tensor_copy(cs[:].rearrange("p t e -> p (t e)"), pb[:]))
                for t in range(NT):
                    link(tt(pre[:, t + 1, :], pre[:, t, :], cs[:, t, :], ALU.add))
                link(ts(ti[:], pre[:, NT, :], 127.0, None, ALU.add))
                link(ts(ti[:], ti[:], 7, None, ALU.arith_shift_right))
                link(nc.vector.tensor_copy(nb[:], ti[:]))
                link(ts(nb[:], nb[:], 1.0, None, ALU.max))
                link(nc.vector.tensor_copy(e0[:], nb[:]))
                frm, to = e0, e1
                for lv in range(5):
                    by = 1 << lv
                    link(nc.vector.tensor_copy(to[:, :by], frm[:, :by]))
                    link(tt(to[:, by:], frm[:, by:], frm[:, :NE - by], ALU.add))
                    frm, to = to, frm
                ends, starts = frm, to
                link(tt(starts[:], ends[:], nb[:], ALU.subtract))
                link(ts(starts[:], starts[:], float(P), None, ALU.mult))
                link(tt(rank[:], pa[:].rearrange("p (t e) -> p t e", e=NE), pre[:, 0:NT, :], ALU.add))
                link(tt(rank[:], rank[:], starts[:].unsqueeze(1).broadcast_to([P, NT, NE]), ALU.add))
                for a in range(2):
                    link(tt(O[:, a], O[:, a], rank[:], ALU.mult))
                    link(nc.vector.tensor_reduce(dest[:, a, :], O[:, a], AX, ALU.add))
                link(nc.vector.tensor_copy(r["dest"][:], dest[:]))
                link(nc.vector.tensor_copy(at[:], dest[:]))
                link(ts(hi[:], at[:], 7, None, ALU.arith_shift_right))
                link(ts(at[:], at[:], 127, None, ALU.bitwise_and))
                link(ts(at[:], at[:], float(NB), None, ALU.mult))
                link(tt(scat[:], at[:], hi[:], ALU.add))
                nc.vector.memset(nb[:], 0.0).then_inc(q["ready"], 1)
                link(tt(cmp[:], ends[0:1, :].unsqueeze(1).broadcast_to([1, 96, NE]),
                        const(g, "blk")[0:1, :].unsqueeze(2).broadcast_to([1, 96, NE]), ALU.is_le))
                link(nc.vector.tensor_reduce(blk[:], cmp[:], AX, ALU.add))
                link(ts(blk[:], blk[:], float(NE - 1), None, ALU.min))
                link(nc.vector.tensor_copy(r["blk"][0:1, 0:96], blk[:]))
                link(nc.vector.tensor_copy(r["blk"][0:1, 96:96 + NE], ends[0:1, :]))
                link(ts(r["blk"][0:1, 128:129], r["blk"][0:1, 96 + NE - 1:96 + NE], 1, None, ALU.arith_shift_right))
        s.end()


def stage_experts(nc, g, r):
    w1, w3 = (g[n][0].rearrange("e (k p) n -> e p k n", p=P) for n in ("moe_w1", "moe_w3"))
    w2 = g["moe_w2"][0].rearrange("e (k p) n -> e p k n", p=P)
    KF = FF // P
    W13, SLOT = KD * FF, 3 * KD * FF
    h2 = g["h2"]
    with Stage(nc, "moe") as s:
        W = s.sb("W", [P, 2 * SLOT])
        x = [s.sb(f"x{i}", [P, D]) for i in range(2)]
        idx = [s.sb(f"idx{i}", [P, 1], U32) for i in range(2)]
        xT = s.sb("xT", [P, 2, KD, P])
        sg, hm = s.sb("sg", [P, FF]), s.sb("hm", [P, FF])
        hT = s.sb("hT", [P, KF, P])
        y = s.sb("y", [P, 2, D])
        xb = [s.ps(f"xb{i}", [P, 512]) for i in range(2)]
        h1b, h3b, htb = s.ps("h1b", [P, 512]), s.ps("h3b", [P, 512]), s.ps("htb", [P, 512])
        yb = [s.ps(f"yb{i}", [P, 512]) for i in range(2)]
        names = ("w13_arrived w2_arrived block_done idx_copied x_turned x_placed h_summed gated silued hidden h_turned h_placed "
                 "y_placed go gathering finished").split()
        q = {n: s.sem(n) for n in names}
        w13_ready = [s.sem("w13_ready0"), s.sem("w13_ready1")]
        w2_ready = [s.sem("w2_ready0"), s.sem("w2_ready1")]
        x_ready = [s.kept_sem("x_ready0"), s.kept_sem("x_ready1")]
        stored = [s.sem("stored0"), s.sem("stored1")]

        def pairs(eng):
            return eng.value_load(r["blk"][0:1, 128:129], min_val=NE // 2, max_val=32)

        with nc.Block() as block:
            @block.sync
            def _(sp):
                def load(e, u, src, c0, k, sem):
                    sp.dma_start(W[:, u * SLOT + c0:u * SLOT + c0 + W13].rearrange("p (k n) -> p k n", k=k),
                                 src[bass.ds(e, 1)].rearrange("a p k n -> p (a k) n")).then_inc(sem[u], 16)

                def load_13(e, u):
                    load(e, u, w1, 0, KD, w13_ready)
                    load(e, u, w3, W13, KD, w13_ready)

                def load_2(e, u):
                    load(e, u, w2, 2 * W13, KF, w2_ready)
                for u in range(2):
                    load_13(u, u)
                    load_2(u, u)
                    sp.wait_ge(w13_ready[u], 32)
                    sp.sem_inc(q["w13_arrived"], 1)
                    sp.wait_ge(w2_ready[u], 16)
                    sp.sem_inc(q["w2_arrived"], 1)
                with sp.Fori(1, NE // 2) as i:
                    for u in range(2):
                        end = sp.value_load(r["blk"][0:1, bass.ds(i * 2 + (96 + u - 2), 1)], min_val=1, max_val=64)
                        sp.wait_ge(q["h_summed"], end * 2)
                        sp.sem_inc(q["go"], 1)
                        load_13(i * 2 + u, u)
                        sp.wait_ge(q["block_done"], end)
                        sp.sem_inc(q["go"], 1)
                        load_2(i * 2 + u, u)
                        sp.wait_ge(w13_ready[u], i * 32 + 32)
                        sp.sem_inc(q["w13_arrived"], 1)
                        sp.wait_ge(w2_ready[u], i * 16 + 16)
                        sp.sem_inc(q["w2_arrived"], 1)

            @block.gpsimd
            def _(pool):
                def gather(b, n, par):
                    pool.wait_ge(q["x_turned"], b + 1)
                    nc.gpsimd.tensor_copy(idx[par][:], r["slot_tok"][:, bass.ds(b, 1)]).then_inc(q["idx_copied"], 1)
                    pool.wait_ge(q["idx_copied"], b + 1)
                    pool.sem_inc(q["gathering"], 1)
                    pool.indirect_dma_start(out=x[par][:], out_offset=None, in_=h2,
                                            in_offset=bass.IndirectOffsetOnAxis(ap=idx[par][:, 0:1], axis=0)).then_inc(x_ready[par], 16)
                count = pairs(pool)
                gather(0, 0, 0)
                gather(1, 0, 1)
                with pool.Fori(0, count) as i:
                    for b, par in ((i * 2 + 2, 0), (i * 2 + 3, 1)):
                        gather(b, i + 1, par)
                pool.wait_ge(x_ready[1], count * 16 + 16)
                pool.sem_inc(q["finished"], 1)

            @block.tensor
            def _(pe):
                ident = const(g, "ident")

                def turn_x(b, n, par):
                    pe.wait_ge(x_ready[par], n * 16 + 16)
                    for half in range(2):
                        for j in range(4):
                            k = half * 4 + j
                            mm = pe.transpose(xb[half][:, j * P:(j + 1) * P], x[par][:, k * P:(k + 1) * P], ident)
                    mm.then_inc(q["x_turned"], 1)

                def products_13(b, par, e):
                    pe.wait_ge(q["x_placed"], b * 2 + 2)
                    pe.wait_ge(q["w13_arrived"], e + 1)
                    base = (e % 2) * SLOT
                    for hb, c0 in ((h1b, 0), (h3b, W13)):
                        for k in range(KD):
                            mm = pe.matmul(hb[:], xT[:, par, k, :], W[:, bass.ds(base + (c0 + k * FF), FF)], start=k == 0, stop=k == KD - 1)
                        mm.then_inc(q["h_summed"], 1)

                def turn_h(b):
                    pe.wait_ge(q["hidden"], b + 1)
                    for k in range(KF):
                        mm = pe.transpose(htb[:, k * P:(k + 1) * P], hm[:, k * P:(k + 1) * P], ident)
                    mm.then_inc(q["h_turned"], 1)

                def product_2(b, e):
                    pe.wait_ge(q["h_placed"], b + 1)
                    pe.wait_ge(q["y_placed"], b * 2 + 2)
                    pe.wait_ge(q["w2_arrived"], e + 1)
                    base = (e % 2) * SLOT + 2 * W13
                    for nh in range(2):
                        for k in range(KF):
                            mm = pe.matmul(yb[nh][:], hT[:, k, :], W[:, bass.ds(base + (k * D + nh * 512), 512)], start=k == 0, stop=k == KF - 1)
                    mm.then_inc(q["block_done"], 1)

                def expert(b):
                    return pe.value_load(r["blk"][0:1, bass.ds(b, 1)], min_val=0, max_val=NE - 1)
                count = pairs(pe)
                pe.sem_inc(q["x_turned"], 2)
                turn_x(0, 0, 0)
                products_13(0, 0, expert(0))
                turn_x(1, 0, 1)
                turn_h(0)
                with pe.Fori(0, count) as i:
                    for b, par in ((i * 2 + 1, 1), (i * 2 + 2, 0)):
                        products_13(b, par, expert(b))
                        turn_x(b + 1, i + 1, 1 - par)
                        product_2(b - 1, expert(b - 1))
                        turn_h(b)
                product_2(count * 2, expert(count * 2))

            @block.scalar
            def _(act):
                def place_x(b, par):
                    act.wait_ge(q["x_turned"], b + 3)
                    for half in range(2):
                        nc.scalar.copy(xT[:, par, half * 4:half * 4 + 4, :], xb[half][:].rearrange("p (a n) -> p a n", n=P)).then_inc(q["x_placed"], 1)

                def place_y(b, n, par):
                    act.wait_ge(q["block_done"], b + 1)
                    act.wait_ge(stored[par], n * 16 + 16)
                    for nh in range(2):
                        nc.scalar.copy(y[:, par, nh * 512:(nh + 1) * 512], yb[nh][:]).then_inc(q["y_placed"], 1)
                    act.wait_ge(q["y_placed"], b * 2 + 4)
                    act.dma_start(g["ybuf"][bass.ds(b * P, P), :], y[:, par, :]).then_inc(stored[par], 16)
                count = pairs(act)
                act.sem_inc(q["y_placed"], 2)
                for par in range(2):
                    act.sem_inc(stored[par], 16)
                place_x(0, 0)
                act.wait_ge(q["h_summed"], 1)
                nc.scalar.activation(sg[:], h1b[:], ACT.Sigmoid).then_inc(q["gated"], 1)
                place_x(1, 1)
                with act.Fori(0, count) as i:
                    for b, par in ((i * 2 + 1, 1), (i * 2 + 2, 0)):
                        act.wait_ge(q["h_summed"], b * 2 + 1)
                        act.wait_ge(q["hidden"], b)
                        nc.scalar.activation(sg[:], h1b[:], ACT.Sigmoid).then_inc(q["gated"], 1)
                        place_x(b + 1, 1 - par)
                        place_y(b - 1, i, 1 - par)
                place_y(count * 2, count, 0)
                act.wait_ge(stored[0], count * 16 + 32)
                act.wait_ge(stored[1], count * 16 + 16)
                act.sem_inc(q["finished"], 1)

            @block.vector
            def _(dve):
                def hidden(b, first=False):
                    dve.wait_ge(q["gated"], b + 1)
                    if not first:
                        dve.wait_ge(q["h_turned"], b)
                    nc.vector.tensor_tensor(hm[:], sg[:], h1b[:], ALU.mult).then_inc(q["silued"], 1)
                    dve.wait_ge(q["silued"], b + 1)
                    dve.wait_ge(q["h_summed"], b * 2 + 2)
                    nc.vector.tensor_tensor(hm[:], hm[:], h3b[:], ALU.mult).then_inc(q["hidden"], 1)

                def place_h(b):
                    dve.wait_ge(q["h_turned"], b + 1)
                    nc.vector.tensor_copy(hT[:].rearrange("p k n -> p (k n)"), htb[:]).then_inc(q["h_placed"], 1)
                count = pairs(dve)
                hidden(0, True)
                place_h(0)
                with dve.Fori(0, count) as i:
                    for b in (i * 2 + 1, i * 2 + 2):
                        hidden(b)
                        place_h(b)
        s.end()


def stage_combine(nc, g, r):
    U = 8
    x1_t = g["x1"].rearrange("(t p) n -> p t n", p=P)
    o_t = g["out"][0].rearrange("(t p) n -> p t n", p=P)
    with Stage(nc, "comb") as s:
        row = s.sb("row", [P, D])
        x = s.sb("x", [P, U, D])
        ya = [[s.sb(f"y{a}{i}", [P, D]) for i in range(U)] for a in range(2)]
        idx = s.sb("idx", [P, 2, U], U32)
        wt = s.sb("wt", [P, 2, U])
        small, copied, weighted, summed, scaled, done, stored = (s.sem(n) for n in "small copied weighted summed scaled done stored".split())
        x_ready = [s.sem(f"x_ready{i}") for i in range(U)]
        y_ready = [s.kept_sem(f"y_ready{i}") for i in range(U)]
        with nc.Block() as block:
            @block.sync
            def _(sp):
                sp.dma_start(row[:], g["rows"][3:4, :].broadcast_to([P, D])).then_inc(small, 16)
                sp.wait_ge(small, 16)
        s.end()
        with nc.Fori(0, NT // U) as turn:
            with nc.Block() as block:
                @block.sync
                def _(sp):
                    for i in range(U):
                        sp.dma_start(x[:, i, :], x1_t[:, bass.ds(turn * U + i, 1), :].rearrange("p a n -> p (a n)")).then_inc(x_ready[i], 16)
                    for i in range(U):
                        sp.wait_ge(done, i + 1)
                        sp.dma_start(o_t[:, bass.ds(turn * U + i, 1), :].rearrange("p a n -> p (a n)"), x[:, i, :]).then_inc(stored, 16)
                    sp.wait_ge(stored, 16 * U)

                @block.gpsimd
                def _(pool):
                    nc.gpsimd.tensor_copy(idx[:], r["dest"][:, :, bass.ds(turn * U, U)]).then_inc(copied, 1)
                    pool.wait_ge(copied, 1)
                    for i in range(U):
                        for a in range(2):
                            pool.indirect_dma_start(out=ya[a][i][:], out_offset=None, in_=g["ybuf"],
                                                    in_offset=bass.IndirectOffsetOnAxis(ap=idx[:, a, i:i + 1], axis=0)).then_inc(y_ready[i], 16)

                @block.scalar
                def _(act):
                    nc.scalar.copy(wt[:], r["wt"][:, :, bass.ds(turn * U, U)]).then_inc(weighted, 1)
                    act.wait_ge(weighted, 1)
                    for i in range(U):
                        act.wait_ge(y_ready[i], turn * 32 + 32)
                        nc.scalar.activation(ya[0][i][:], ya[0][i][:], ACT.Copy, scale=wt[:, 0, i:i + 1]).then_inc(scaled, 1)

                @block.vector
                def _(dve):
                    for i in range(U):
                        dve.wait_ge(scaled, i + 1)
                        dve.wait_ge(x_ready[i], 16)
                        a, b = ya[0][i][:], ya[1][i][:]
                        nc.vector.scalar_tensor_tensor(a, b, wt[:, 1, i:i + 1], a, ALU.mult, ALU.add).then_inc(summed, 1)
                        dve.wait_ge(summed, 3 * i + 1)
                        nc.vector.tensor_tensor(a, a, row[:], ALU.mult).then_inc(summed, 1)
                        dve.wait_ge(summed, 3 * i + 2)
                        nc.vector.tensor_tensor(x[:, i, :], x[:, i, :], a, ALU.add).then_inc(summed, 1)
                        dve.wait_ge(summed, 3 * i + 3)
                        dve.sem_inc(done, 1)
            s.end()


INPUTS = ("x c positions ada_w ada_b norm1_g w_in pool_w pool_scale q_norm_g k_norm_g lambda_q1 lambda_k1 lambda_q2 lambda_k2 "
          "subln_g lam_re lam_im log_dt b_re b_im c_re c_im d_skip glu_w glu_b proj_a proj_b proj_c gate_w gate_b w_out norm2_g "
          "router_g_w router_g_b router_e_w router_e_b moe_w1 moe_w3 moe_w2").split()


def program(nc, g):
    g["rows"] = nc.dram_tensor("rows", (4, D), F32, kind="Internal").ap()
    g["mixT"] = nc.dram_tensor("mixT", (P, KD, T), F32, kind="Internal").ap()
    for n in ("x1", "h2"):
        g[n] = nc.dram_tensor(n, (T, D), F32, kind="Internal").ap()
    g["slots"] = nc.dram_tensor("slots", (P * 72, 1), U32, kind="Internal").ap()
    g["ybuf"] = nc.dram_tensor("ybuf", (NB_OUT * P, D), F32, kind="Internal").ap()
    with ExitStack() as keep:
        def sb(name, shape, dt=F32, ctx=keep):
            return ctx.enter_context(nc.sbuf_tensor(name, shape, dt))
        g["consts"] = sb("consts", [P, CONST_W])
        g["col1"] = sb("col1", [P, 2, KD])
        stage_mod(nc, g)
        with ExitStack() as mixers:
            g["hT"] = sb("hT", [P, KD, T], ctx=mixers)
            stage_norm1(nc, g)
            g["ybT"] = sb("ybT", [P, HEADS, T], ctx=mixers)
            stage_attention(nc, g)
            g["yaT"] = sb("yaT", [P, 2, T], ctx=mixers)
            g["ycT"] = sb("ycT", [P, 2, T], ctx=mixers)
            with nc.sbuf_tensor("uc", [P, 2, T], F32) as uc:
                stage_pool(nc, g, uc)
                stage_ssm(nc, g, uc)
            stage_merge(nc, g)
        moe_part(nc, g, sb)


def moe_part(nc, g, sb):
    lg = sb("lg", [P, NT, 36])
    r = {"wt": sb("wt", [P, 2, NT]), "dest": sb("dest", [P, 2, NT], U32),
         "slot_tok": sb("slot_tok", [P, 72], U32), "blk": sb("blk", [1, 136], I32)}
    stage_out(nc, g, lg)
    stage_route(nc, g, r, lg)
    stage_experts(nc, g, r)
    stage_combine(nc, g, r)


def kernel(**inputs):
    import numpy as _np
    import concourse.bacc as _bacc
    from concourse.bass_utils import run_bass_kernel_spmd as _run

    nc = _bacc.Bacc("TRN2", target_bir_lowering=False, num_devices=1)
    arrays, g = {}, {}
    for name in INPUTS:
        a = _np.ascontiguousarray(inputs[name])
        arrays[f"in_{name}"] = a
        g[name] = nc.dram_tensor(f"in_{name}", a.shape, mybir.dt.from_np(a.dtype), kind="ExternalInput").ap()
    pack = constant_pack()
    arrays["const_pack"] = pack
    g["const_pack"] = nc.dram_tensor("const_pack", pack.shape, F32, kind="ExternalInput").ap()
    g["out"] = nc.dram_tensor("out", (1, T, D), F32, kind="ExternalOutput").ap()
    program(nc, g)
    r = _run(nc, [arrays], core_ids=[0])
    return r.results[0]["out"]
```

```python
import math
from contextlib import ExitStack

import numpy as np
import concourse.bass as bass
from concourse import mybir

F32 = mybir.dt.float32
F32R = mybir.dt.float32r
I32 = mybir.dt.int32
U32 = mybir.dt.uint32
ALU = mybir.AluOpType
ACT = mybir.ActivationFunctionType
AX = mybir.AxisListType.X

P = 128
T = 2048
D = 1024
KD = D // P
NT = T // P
TB = T // 512
EPS = 1e-6
HEADS = 4
DH = 64
POOL_W = 256
QK_W = 512
SSM_W = 256
Q0 = POOL_W
K0 = Q0 + QK_W
V0 = K0 + QK_W
C0 = V0 + QK_W
IN_W = C0 + SSM_W
LAMBDA_INIT = 0.8 - 0.6 * math.exp(-0.3 * 0)
NEG = -1e30
GROUPS = 16
SL = 8
SC = T // SL
NE = 32
FF = 512
NB_OUT = 66

CONSTS = {}
_at = 0
for _n, _w in (("ident", P), ("rot", P), ("swap", P), ("half", P), ("before", P), ("ones", P),
               ("mask", 512), ("inv", 1), ("sign", 1), ("upper", 1), ("cnt", 32), ("width", 2), ("iota", 32),
               ("blk", 96), ("tok", NT)):
    CONSTS[_n] = (_at, _at + _w)
    _at += _w
CONST_W = _at


def constant_pack():
    c = np.zeros((P, CONST_W), np.float32)

    def put(name, a):
        c[:, CONSTS[name][0]:CONSTS[name][1]] = a
    r = np.arange(P)
    i = np.eye(P, dtype=np.float32)
    put("ident", i)
    put("rot", i[:, r ^ 32])
    put("swap", np.concatenate([-i[:, 64:], i[:, :64]], 1))
    put("half", (r[:, None] // 64 == r[None, :] // 64) / 64.0)
    put("before", r[:, None] < r[None, :])
    put("ones", 1.0)
    m = np.zeros((P, 512), np.float32)
    m[:64, 448:] = NEG
    put("mask", m)
    put("inv", (10000.0 ** (-2.0 * (r % 32) / DH)).astype(np.float32)[:, None])
    put("sign", np.where(r % 64 < 32, -1.0, 1.0)[:, None])
    put("upper", np.where(r < 64, -1.0, 1.0)[:, None])
    w = np.stack([np.where(r < 64, 2, 4), np.where(r < 64, 8, 16)], 1)
    put("width", 1.0 / w)
    put("cnt", np.concatenate([1.0 / np.minimum(np.arange(1, 17)[None, :], w[:, h:h + 1])
                               for h in range(2)], 1))
    put("iota", np.arange(32)[None, :])
    put("blk", np.arange(96)[None, :])
    put("tok", r[:, None] + P * np.arange(NT)[None, :])
    return c


class Chain:

    def __init__(self, eng, sem):
        self.eng, self.sem, self.n = eng, sem, 0

    def __call__(self, ins):
        self.n += 1
        ins.then_inc(self.sem, 1)
        self.eng.wait_ge(self.sem, self.n)


KEPT = []


class Stage:

    def __init__(self, nc, name):
        self.nc, self.name, self.ctx, self.sems = nc, name, ExitStack(), []

    def __enter__(self):
        return self

    def __exit__(self, *a):
        return self.ctx.__exit__(*a)

    def sb(self, name, shape, dt=F32):
        return self.ctx.enter_context(self.nc.sbuf_tensor(f"{self.name}_{name}", shape, dt))

    def ps(self, name, shape):
        return self.ctx.enter_context(self.nc.psum_tensor(f"{self.name}_{name}", shape, F32))

    def sem(self, name):
        s = self.ctx.enter_context(self.nc.semaphore(f"{self.name}_{name}"))
        self.sems.append(s)
        return s

    def kept_sem(self, name):
        s = self.nc.semaphore(f"{self.name}_{name}")
        KEPT.append(s)
        return s.__enter__()

    def end(self):
        for s in self.sems:
            self.nc.sync.sem_clear(s)
        self.nc.all_engine_barrier()


def const(g, name):
    a, b = CONSTS[name]
    return g["consts"][:, a:b]


def wrap_angle(nc, link, ang, tmp):
    parts, rest = [], 2 * math.pi
    for bits in (5, 13, 21):
        part = math.floor(rest * 2.0 ** bits) / 2.0 ** bits
        parts.append(part)
        rest -= part
    parts.append(rest)
    magic = 1.5 * 2.0 ** 23
    link(nc.vector.tensor_scalar(tmp, ang, 1 / (2 * math.pi), None, ALU.mult))
    link(nc.vector.tensor_scalar(tmp, tmp, magic, None, ALU.add))
    link(nc.vector.tensor_scalar(tmp, tmp, magic, None, ALU.subtract))
    for part in parts:
        link(nc.vector.scalar_tensor_tensor(ang, tmp, -part, ang, ALU.mult, ALU.add))
    link(nc.vector.tensor_scalar(ang, ang, 3.1415925, -3.1415925, ALU.min, ALU.max))


def stage_mod(nc, g):
    ada_w = g["ada_w"][0].rearrange("(k p) n -> p k n", p=P)
    with Stage(nc, "mod") as s:
        ccol = s.sb("ccol", [P, KD])
        cexp = s.sb("cexp", [P, KD])
        crep = s.sb("crep", [P, KD, P])
        w = s.sb("w", [P, 4, KD, 512])
        bias = s.sb("bias", [P, 6, 512])
        mod = s.sb("mod", [P, 6, D])
        n1 = s.sb("n1", [P, D])
        n2 = s.sb("n2", [P, D])
        acc = [s.ps(f"acc{i}", [P, 512]) for i in range(4)]
        tr = [s.ps(f"tr{i}", [P, 512]) for i in range(4)]
        small, w_ready = s.sem("small"), [s.sem(f"w_ready{i}") for i in range(4)]
        exped, c_ready, summed, moded = s.sem("exped"), s.sem("c_ready"), s.sem("summed"), s.sem("moded")
        dve_done, turned, stored = s.sem("dve_done"), s.sem("turned"), s.sem("stored")

        with nc.Block() as block:
            @block.sync
            def _(sp):
                sp.dma_start(ccol[:], g["c"].rearrange("a (k p) -> p (a k)", p=P), allow_slow_non_contiguous=True).then_inc(small, 16)
                sp.dma_start(g["consts"][:], g["const_pack"]).then_inc(small, 16)
                sp.dma_start(n1[:], g["norm1_g"].broadcast_to([P, D])).then_inc(small, 16)
                sp.dma_start(n2[:], g["norm2_g"].broadcast_to([P, D])).then_inc(small, 16)

            @block.scalar
            def _(act):
                act.wait_ge(small, 64)
                nc.scalar.activation(cexp[:], ccol[:], ACT.Exp, scale=-1.0).then_inc(exped, 1)

            @block.vector
            def _(dve):
                link = Chain(dve, dve_done)
                dve.wait_ge(small, 64)
                dve.wait_ge(exped, 1)
                link(nc.vector.tensor_scalar(cexp[:], cexp[:], 1.0, None, ALU.add))
                link(nc.vector.reciprocal(cexp[:], cexp[:]))
                link(nc.vector.tensor_tensor(ccol[:], ccol[:], cexp[:], ALU.mult))
                for k in range(KD):
                    link(nc.vector.tensor_scalar(crep[:, k, :], const(g, "ones"), ccol[:, k:k + 1], None, ALU.mult))
        s.end()

        PER = 6
        with nc.Fori(0, 2) as turn:
            with nc.Block() as block:
                @block.sync
                def _(sp):
                    sp.dma_start(bias[:].rearrange("p a n -> p (a n)"),
                                 g["ada_b"][:, bass.ds(turn * (PER * 512), PER * 512)].broadcast_to([P, PER * 512])).then_inc(small, 16)
                    for i in range(PER):
                        if i >= 4:
                            sp.wait_ge(summed, i - 3)
                        sp.dma_start(w[:, i % 4], ada_w[:, :, bass.ds(turn * (PER * 512) + i * 512, 512)]).then_inc(w_ready[i % 4], 16)

                @block.tensor
                def _(pe):
                    for i in range(PER):
                        pe.wait_ge(w_ready[i % 4], 16 * (i // 4 + 1))
                        if i >= 4:
                            pe.wait_ge(moded, i - 3)
                        for k in range(KD):
                            mm = pe.matmul(acc[i % 4][:], crep[:, k, :], w[:, i % 4, k, :], start=k == 0, stop=k == KD - 1)
                        mm.then_inc(summed, 1)

                @block.vector
                def _(dve):
                    dve.wait_ge(small, 16)
                    flat = mod[:].rearrange("p a n -> p (a n)")
                    for i in range(PER):
                        dve.wait_ge(summed, i + 1)
                        nc.vector.tensor_tensor(flat[:, bass.ds(turn * (PER * 512) + i * 512, 512)], acc[i % 4][:],
                                                bias[:, i, :], ALU.add).then_inc(moded, 1)
            s.end()

        with nc.Block() as block:
            @block.vector
            def _(dve):
                link = Chain(dve, dve_done)
                link(nc.vector.scalar_tensor_tensor(mod[:, 1], mod[:, 1], 1.0, n1[:], ALU.add, ALU.mult))
                nc.vector.scalar_tensor_tensor(mod[:, 4], mod[:, 4], 1.0, n2[:], ALU.add, ALU.mult).then_inc(moded, 1)
                for b in range(4):
                    dve.wait_ge(turned, b + 1)
                    nc.vector.tensor_copy(g["col1"][:, b // 2, (b % 2) * 4:(b % 2) * 4 + 4],
                                          tr[b][:].rearrange("p (a n) -> p a n", n=P)[:, :, 0]).then_inc(c_ready, 1)

            @block.tensor
            def _(pe):
                pe.wait_ge(moded, 1)
                for b in range(4):
                    for j in range(4):
                        k = (b % 2) * 4 + j
                        mm = pe.transpose(tr[b][:, j * P:(j + 1) * P], mod[:, b // 2, k * P:(k + 1) * P], const(g, "ident"))
                    mm.then_inc(turned, 1)

            @block.sync
            def _(sp):
                sp.wait_ge(moded, 1)
                for r in (2, 3, 4, 5):
                    sp.dma_start(g["rows"][r - 2:r - 1, :], mod[0:1, r, :]).then_inc(stored, 16)
                sp.wait_ge(stored, 64)
        s.end()


def stage_norm1(nc, g):
    U = 8
    x_t = g["x"][0].rearrange("(t p) n -> p t n", p=P)
    with Stage(nc, "norm1") as s:
        x = s.sb("x", [P, U, D])
        sq = s.sb("sq", [P, D])
        ss = s.sb("ss", [P, U])
        eps = s.sb("eps", [P, 1])
        bank = [[s.ps(f"tr{i}{j}", [P, 4, P]) for j in range(2)] for i in range(4)]
        x_ready = [s.sem(f"x_ready{i}") for i in range(U)]
        small, act_done, rooted, dve_done = s.sem("small"), s.sem("act_done"), s.sem("rooted"), s.sem("dve_done")
        act_moved = s.sem("act_moved")
        scaled, turned, moved = s.sem("scaled"), s.sem("turned"), s.sem("moved")
        with nc.Fori(0, NT // U) as turn:
            with nc.Block() as block:
                @block.sync
                def _(sp):
                    for i in range(U):
                        sp.dma_start(x[:, i, :], x_t[:, bass.ds(turn * U + i, 1), :].rearrange("p a n -> p (a n)")).then_inc(x_ready[i], 16)

                @block.gpsimd
                def _(pool):
                    nc.gpsimd.memset(eps[:], EPS).then_inc(small, 1)

                @block.scalar
                def _(act):
                    link = Chain(act, act_done)

                    def place(i):
                        act.wait_ge(turned, i + 1)
                        for k in range(4, KD):
                            nc.scalar.activation(g["hT"][:, k, bass.ds((turn * U + i) * P, P)], bank[i % 4][1][:, k % 4, :], ACT.Identity,
                                                 scale=g["col1"][:, 1, k:k + 1], bias=g["col1"][:, 0, k:k + 1]).then_inc(act_moved, 1)
                    act.wait_ge(small, 1)
                    for i in range(U + 2):
                        if i < U:
                            act.wait_ge(x_ready[i], 16)
                            link(nc.scalar.activation(sq[:], x[:, i, :], ACT.Square, accum_out=ss[:, i:i + 1]))
                            nc.scalar.activation(ss[:, i:i + 1], ss[:, i:i + 1], ACT.Sqrt, scale=1.0 / D, bias=eps[:]).then_inc(rooted, 1)
                        if i >= 2:
                            place(i - 2)

                @block.vector
                def _(dve):
                    link = Chain(dve, dve_done)
                    for i in range(U + 2):
                        if i < U:
                            dve.wait_ge(rooted, i + 1)
                            link(nc.vector.reciprocal(ss[:, i:i + 1], ss[:, i:i + 1]))
                            nc.vector.tensor_scalar(x[:, i, :], x[:, i, :], ss[:, i:i + 1], None, ALU.mult).then_inc(scaled, 1)
                        if i >= 2:
                            j = i - 2
                            dve.wait_ge(turned, j + 1)
                            for k in range(4):
                                nc.vector.tensor_scalar(g["hT"][:, k, bass.ds((turn * U + j) * P, P)], bank[j % 4][0][:, k, :],
                                                        g["col1"][:, 1, k:k + 1], g["col1"][:, 0, k:k + 1],
                                                        ALU.mult, ALU.add).then_inc(moved, 1)

                @block.tensor
                def _(pe):
                    for i in range(U):
                        pe.wait_ge(scaled, i + 1)
                        if i >= 4:
                            pe.wait_ge(moved, 4 * (i - 3))
                            pe.wait_ge(act_moved, 4 * (i - 3))
                        for k in range(KD):
                            mm = pe.transpose(bank[i % 4][k // 4][:, k % 4, :], x[:, i, k * P:(k + 1) * P], const(g, "ident"))
                        mm.then_inc(turned, 1)
            s.end()


LATE = 9


def clear_late_blocks(sp, g, zero, turn, sem):
    for i in range(LATE):
        sp.dma_start(g["ybuf"][bass.ds((turn * LATE + (NB_OUT - 4 * LATE + i)) * P, P), :].rearrange("p (a n) -> p a n", n=P),
                     zero[:].unsqueeze(1).broadcast_to([P, KD, P])).then_inc(sem, 16)


def stage_attention(nc, g):
    ybT = g["ybT"]
    RING = 3
    with Stage(nc, "att") as s:
        vT = s.sb("vT", [P, T])
        qk = s.sb("qk", [P, 2, T])
        val = s.sb("val", [P, NT, P])
        S = s.sb("S", [P, RING, 2, T])
        aT = s.sb("aT", [P, 2, 4, P])
        o = s.sb("o", [P, NT, P])
        osq = s.sb("osq", [P, 2, P])
        zero = s.sb("zero", [P, P])
        gcol = s.sb("gcol", [P, 2])
        lq = S[:, 1, 0, 0:4 * DH].rearrange("p (a n) -> p a n", n=DH)
        eps = s.sb("eps", [P, 1])
        mx = s.sb("mx", [P, RING, 2, 4])
        nm = s.sb("nm", [P, RING, 2])
        den = s.sb("den", [P, RING, 2])
        ss = s.sb("ss", [P, NT])
        bank = [s.ps(f"bank{i}", [P, 512]) for i in range(8)]
        names = ("small dve_done pool_done z_ready "
                 "v_turned v_placed scored evacuated maxed exped scaled weighed a_turned a_placed "
                 "summed o_copied o_squared o_rooted o_normed o_turned o_placed lam cleared").split()
        q = {n: s.sem(n) for n in names}

        def load_z(sp, h, j, sem):
            c0 = (Q0, K0, V0)[j] // P
            sp.dma_start(vT[:] if j == 2 else qk[:, j, :], g["zT"][bass.ds(h + c0, 1)].rearrange("a p n -> p (a n)")).then_inc(sem, 16)

        with nc.Block() as block:
            @block.sync
            def _(sp):
                sp.dma_start(gcol[:, 0:1], g["subln_g"].rearrange("a n -> n a"), allow_slow_non_contiguous=True).then_inc(q["small"], 16)
                for j, n in enumerate(("lambda_q1", "lambda_k1", "lambda_q2", "lambda_k2")):
                    sp.dma_start(lq[:, j], g[n].broadcast_to([P, DH])).then_inc(q["small"], 16)
                for j in range(3):
                    load_z(sp, 0, j, q["z_ready"])
                sp.wait_ge(q["z_ready"], 48)

            @block.vector
            def _(dve):
                link = Chain(dve, q["dve_done"])
                link(nc.vector.memset(eps[:], EPS))
                link(nc.vector.memset(zero[:], 0.0))
                dve.wait_ge(q["small"], 16 * 5)
                link(nc.vector.tensor_scalar(gcol[:, 0:1], gcol[:, 0:1], 1.0 - LAMBDA_INIT, None, ALU.mult))
                for j in range(2):
                    link(nc.vector.tensor_tensor_reduce(lq[:, 2 * j], lq[:, 2 * j], lq[:, 2 * j + 1], 1.0, 0.0, ALU.mult,
                                                        ALU.add, den[:, 0, j:j + 1]))
                nc.vector.memset(nm[:, 0, 0:1], 0.0).then_inc(q["maxed"], 1)
                dve.wait_ge(q["lam"], 1)
                link(nc.vector.tensor_tensor(gcol[:, 1:2], den[:, 1, 0:1], den[:, 1, 1:2], ALU.subtract))
                link(nc.vector.tensor_scalar(gcol[:, 1:2], gcol[:, 1:2], LAMBDA_INIT, None, ALU.add))

            @block.scalar
            def _(act):
                act.wait_ge(q["maxed"], 1)
                nc.scalar.activation(den[:, 1, :], den[:, 0, :], ACT.Exp).then_inc(q["lam"], 1)
        s.end()

        with nc.Fori(0, HEADS) as h:
            score_units = [(i, m, c, min(512, (i + 1) * P - c * 512), c == i // 4)
                           for i in range(NT) for m in range(2) for c in range(i // 4 + 1)]
            first_unit = [next(n for n, u in enumerate(score_units) if u[0] == i) for i in range(NT)] + [len(score_units)]
            turn_units = [(i, c, min(4, i + 1 - 4 * c)) for i in range(NT) for c in range(i // 4 + 1)]
            first_turn = [next(n for n, u in enumerate(turn_units) if u[0] == i) for i in range(NT)] + [len(turn_units)]

            with nc.Block() as block:
                @block.sync
                def _(sp):
                    sp.wait_ge(q["v_turned"], TB)
                    load_z(sp, h + 1, 2, q["z_ready"])
                    clear_late_blocks(sp, g, zero, h, q["cleared"])
                    sp.wait_ge(q["scored"], len(score_units))
                    for j in range(2):
                        load_z(sp, h + 1, j, q["z_ready"])
                    sp.wait_ge(q["z_ready"], 48)
                    sp.wait_ge(q["cleared"], 16 * LATE)

                @block.tensor
                def _(pe):
                    def score(n):
                        i, m, c, width, _ = score_units[n]
                        if n >= 4:
                            pe.wait_ge(q["evacuated"], n - 3)
                        pe.matmul(bank[n % 4][:, :width], qk[m * DH:(m + 1) * DH, 0, i * P:(i + 1) * P],
                                  qk[m * DH:(m + 1) * DH, 1, c * 512:c * 512 + width], start=True, stop=True).then_inc(q["scored"], 1)

                    def turn_a(n):
                        i, c, blocks = turn_units[n]
                        if n >= 2:
                            pe.wait_ge(q["a_placed"], n - 1)
                        for j in range(blocks):
                            mm = pe.transpose(bank[4 + n % 2][:, j * P:(j + 1) * P],
                                              S[:, i % RING, 0, (4 * c + j) * P:(4 * c + j + 1) * P], const(g, "ident"))
                        mm.then_inc(q["a_turned"], 1)

                    def weigh_v(n):
                        i, c, blocks = turn_units[n]
                        pe.wait_ge(q["a_placed"], n + 1)
                        for j in range(blocks):
                            mm = pe.matmul(bank[6 + i % 2][:, 0:P], aT[:, n % 2, j, :], val[:, 4 * c + j, :],
                                           start=4 * c + j == 0, stop=4 * c + j == i)
                        mm.then_inc(q["summed"], 1)

                    for n in range(first_unit[2]):
                        score(n)
                    for tb in range(TB):
                        for j in range(4):
                            mm = pe.transpose(bank[4 + tb][:, j * P:(j + 1) * P],
                                              vT[:, tb * 512 + j * P:tb * 512 + (j + 1) * P], const(g, "ident"))
                        mm.then_inc(q["v_turned"], 1)
                    pe.wait_ge(q["v_placed"], TB)
                    for i in range(NT):
                        ahead = list(range(first_unit[i + 2], first_unit[i + 3])) if i + 2 < NT else []
                        lo, hi = first_turn[i], first_turn[i + 1]
                        pe.wait_ge(q["weighed"], i + 1)
                        if i >= 2:
                            pe.wait_ge(q["o_copied"], i - 1)
                            pe.wait_ge(q["o_squared"], i - 1)
                        for n in range(lo, hi + 1):
                            if n < hi:
                                turn_a(n)
                            for _ in range(-(-len(ahead) // (hi + 1 - n))):
                                score(ahead.pop(0))
                            if n > lo:
                                weigh_v(n - 1)
                    for c in range(4):
                        pe.wait_ge(q["o_normed"], 4 * c + 4)
                        pe.wait_ge(q["a_placed"], len(turn_units))
                        for j in range(4):
                            mm = pe.transpose(bank[c][:, j * P:(j + 1) * P], o[:, 4 * c + j, :], const(g, "ident"))
                        mm.then_inc(q["o_turned"], 1)

                @block.scalar
                def _(act):
                    for tb in range(TB):
                        act.wait_ge(q["v_turned"], tb + 1)
                        nc.scalar.copy(val[:, 4 * tb:4 * tb + 4, :], bank[4 + tb][:].rearrange("p (a b) -> p a b", a=4)).then_inc(q["v_placed"], 1)

                    def exps(i):
                        act.wait_ge(q["maxed"], i + 1)
                        if i >= RING:
                            act.wait_ge(q["weighed"], i - RING + 1)
                        n = (i + 1) * P
                        for m in (1, 0):
                            nc.scalar.activation(S[:, i % RING, m, :n], S[:, i % RING, m, :n], ACT.Exp, bias=nm[:, i % RING, m:m + 1],
                                                 accum_out=den[:, i % RING, m:m + 1]).then_inc(q["exped"], 1)

                    def place(i):
                        for n in range(first_turn[i], first_turn[i + 1]):
                            act.wait_ge(q["a_turned"], n + 1)
                            if n >= 2:
                                act.wait_ge(q["summed"], n - 1)
                            b = turn_units[n][2]
                            nc.scalar.copy(aT[:, n % 2, :b, :], bank[4 + n % 2][:, :b * P].rearrange("p (a b) -> p a b", b=P)).then_inc(q["a_placed"], 1)
                        act.wait_ge(q["summed"], first_turn[i + 1])
                        nc.scalar.copy(o[:, i, :], bank[6 + i % 2][:, 0:P]).then_inc(q["o_copied"], 1)
                        if i >= 2:
                            act.wait_ge(q["o_squared"], i - 1)
                        nc.scalar.activation(osq[:, i % 2, :], bank[6 + i % 2][:, 0:P], ACT.Square,
                                             accum_out=ss[:, i:i + 1]).then_inc(q["o_squared"], 1)

                    exps(0)
                    exps(1)
                    for i in range(NT):
                        place(i)
                        if i + 2 < NT:
                            exps(i + 2)
                    act.wait_ge(q["o_squared"], NT)
                    nc.scalar.activation(ss[:], ss[:], ACT.Sqrt, scale=1.0 / P, bias=eps[:]).then_inc(q["o_rooted"], 1)
                    for c in range(4):
                        act.wait_ge(q["o_turned"], c + 1)
                        nc.scalar.activation(ybT[:, bass.ds(h, 1), c * 512:(c + 1) * 512].rearrange("p a n -> p (a n)"),
                                             bank[c][:], ACT.Copy, scale=gcol[:, 0:1]).then_inc(q["o_placed"], 1)

                @block.gpsimd
                def _(pool):
                    for i in range(NT):
                        pool.wait_ge(q["scaled"], i + 1)
                        n = (i + 1) * P
                        nc.gpsimd.tensor_scalar(S[:, i % RING, 1, :n], S[:, i % RING, 1, :n], den[:, i % RING, 1:2], None, ALU.mult).then_inc(q["pool_done"], 1)

                @block.vector
                def _(dve):
                    link = Chain(dve, q["dve_done"])

                    def evacuate(n):
                        i, m, c, width, diag = score_units[n]
                        if n == first_unit[i]:
                            if i >= RING:
                                dve.wait_ge(q["a_turned"], first_turn[i - RING + 1])
                        dve.wait_ge(q["scored"], n + 1)
                        to = S[:, i % RING, m, c * 512:c * 512 + width]
                        if diag:
                            ins = nc.vector.tensor_tensor_reduce(to, bank[n % 4][:, :width], const(g, "mask")[:, 512 - width:], 1.0, NEG,
                                                                 ALU.add, ALU.max, mx[:, i % RING, m, c:c + 1])
                        else:
                            ins = nc.vector.tensor_scalar(to, bank[n % 4][:, :width], 1.0, None, ALU.mult, ALU.max,
                                                          accum_out=mx[:, i % RING, m, c:c + 1])
                        ins.then_inc(q["evacuated"], 1)

                    def maxima(i):
                        dve.wait_ge(q["evacuated"], first_unit[i + 1])
                        if i >= RING:
                            dve.wait_ge(q["exped"], 2 * (i - RING) + 2)
                        nc.vector.tensor_reduce(nm[:, i % RING, :], mx[:, i % RING, :, :i // 4 + 1], AX, ALU.max, negate=True).then_inc(q["maxed"], 1)

                    def scales(i):
                        dve.wait_ge(q["exped"], 2 * i + 2)
                        link(nc.vector.reciprocal(den[:, i % RING, :], den[:, i % RING, :]))
                        nc.vector.tensor_tensor(den[:, i % RING, 1:2], den[:, i % RING, 1:2], gcol[:, 1:2], ALU.mult).then_inc(q["scaled"], 1)

                    def weigh(i):
                        n = (i + 1) * P
                        dve.wait_ge(q["pool_done"], i + 1)
                        nc.vector.scalar_tensor_tensor(S[:, i % RING, 0, :n], S[:, i % RING, 0, :n], den[:, i % RING, 0:1], S[:, i % RING, 1, :n],
                                                       ALU.mult, ALU.subtract).then_inc(q["weighed"], 1)

                    for i in range(2):
                        for n in range(first_unit[i], first_unit[i + 1]):
                            evacuate(n)
                        maxima(i)
                    scales(0)
                    weigh(0)
                    for i in range(NT - 1):
                        ahead = list(range(first_unit[i + 2], first_unit[i + 3])) if i + 2 < NT else []
                        half, most = len(ahead) // 2, len(ahead) * 3 // 4
                        for n in ahead[:half]:
                            evacuate(n)
                        scales(i + 1)
                        for n in ahead[half:most]:
                            evacuate(n)
                        weigh(i + 1)
                        for n in ahead[most:]:
                            evacuate(n)
                        if i + 2 < NT:
                            maxima(i + 2)
                    dve.wait_ge(q["o_rooted"], 1)
                    link(nc.vector.reciprocal(ss[:], ss[:]))
                    dve.wait_ge(q["o_copied"], NT)
                    for i in range(NT):
                        nc.vector.tensor_scalar(o[:, i, :], o[:, i, :], ss[:, i:i + 1], None, ALU.mult).then_inc(q["o_normed"], 1)
            s.end()


def cols(nc, sp, to, row, n, sem):
    sp.dma_start(to, row.rearrange("a (k p) -> p (a k)", p=P), allow_slow_non_contiguous=True).then_inc(sem, 16)


def stage_pool(nc, g, uc):
    yaT = g["yaT"]
    with Stage(nc, "pooling") as s:
        ua = s.sb("ua", [P, 2, T])
        A, B = s.sb("A", [P, T]), s.sb("B", [P, T])
        pw = s.sb("pw", [P, 2, P])
        ps_col = s.sb("ps_col", [P, 2])
        first = s.sb("first", [P, 2, 16])
        bank = [s.ps(f"bank{i}", [P, 512]) for i in range(8)]
        u_ready = [s.sem("u_ready0"), s.sem("u_ready1")]
        small, zeroed, c_ready = s.sem("small"), s.sem("zeroed"), s.sem("c_ready")
        dve_done, pooled, mixed, placed = s.sem("dve_done"), s.sem("pooled"), s.sem("mixed"), s.sem("placed")
        with nc.Block() as block:
            @block.sync
            def _(sp):
                for c in range(2):
                    sp.dma_start(ua[:, c, :], g["zT"][c]).then_inc(u_ready[c], 16)
                cols(nc, sp, ps_col[:], g["pool_scale"], 2, small)
                sp.wait_ge(zeroed, 1)
                for gr in range(4):
                    at = slice((gr % 2) * 64, (gr % 2) * 64 + 64)
                    sp.dma_start(pw[at, gr // 2, at], g["pool_w"][0, gr]).then_inc(small, 16)
                for c in range(2):
                    sp.dma_start(uc[:, c, :], g["zT"][C0 // P + c]).then_inc(c_ready, 16)
                sp.wait_ge(c_ready, 32)

            @block.gpsimd
            def _(pool):
                nc.gpsimd.memset(pw[:], 0.0).then_inc(zeroed, 1)

            @block.tensor
            def _(pe):
                pe.wait_ge(small, 16 * 5)
                for n in range(8):
                    c, tb = n // TB, n % TB
                    pe.wait_ge(pooled, c + 1)
                    if n >= 2:
                        pe.wait_ge(placed, n - 1)
                    pe.matmul(bank[6 + n % 2][:], pw[:, c, :], ua[:, c, tb * 512:(tb + 1) * 512], start=True, stop=True).then_inc(mixed, 1)

            @block.scalar
            def _(act):
                act.wait_ge(small, 16 * 5)
                for n in range(8):
                    c, tb = n // TB, n % TB
                    act.wait_ge(mixed, n + 1)
                    nc.scalar.activation(yaT[:, c, tb * 512:(tb + 1) * 512], bank[6 + n % 2][:], ACT.Copy,
                                         scale=ps_col[:, c:c + 1]).then_inc(placed, 1)

            @block.vector
            def _(dve):
                link = Chain(dve, dve_done)

                def wider(to, frm, by, at=slice(0, P)):
                    link(nc.vector.tensor_copy(to[at, 0:by], frm[at, 0:by]))
                    link(nc.vector.tensor_tensor(to[at, by:], frm[at, by:], frm[at, :T - by], ALU.add))
                for c in range(2):
                    dve.wait_ge(u_ready[c], 16)
                    u = ua[:, c, :]
                    wider(A[:], u, 1)
                    if c == 1:
                        wider(B[:], A[:], 2)
                        wider(A[:], B[:], 4)
                        wider(B[:], A[:], 8, slice(64, P))
                    else:
                        wider(B[:], A[:], 2, slice(64, P))
                    for half, sums in ((slice(0, 64), A), (slice(64, P), B)):
                        cnt = const(g, "cnt")[half, c * 16:(c + 1) * 16]
                        link(nc.vector.tensor_tensor(first[half, c, :], sums[half, 0:16], cnt, ALU.mult))
                        link(nc.vector.tensor_tensor(first[half, c, :], first[half, c, :], u[half, 0:16], ALU.subtract))
                        link(nc.vector.scalar_tensor_tensor(u[half, :], sums[half, :], const(g, "width")[half, c:c + 1], u[half, :],
                                                            ALU.mult, ALU.subtract))
                        link(nc.vector.tensor_copy(u[half, 0:16], first[half, c, :]))
                    nc.vector.tensor_copy(first[:, c, :], u[:, 0:16]).then_inc(pooled, 1)
        s.end()


def stage_ssm(nc, g, uc):
    GU = 4
    LEVELS = (SC - 1).bit_length()
    with Stage(nc, "ssm") as s:
        UY = s.sb("UY", [P, 2, GROUPS, SL * 16])
        B1, B2 = s.sb("B1", [P, GROUPS, 16]), s.sb("B2", [P, GROUPS, 16])
        C1, C2 = s.sb("C1", [P, GROUPS, 16]), s.sb("C2", [P, GROUPS, 16])
        q1, q2 = s.sb("q1", [P, GROUPS, 16]), s.sb("q2", [P, GROUPS, 16])
        craw = s.sb("craw", [P, 2, 2, P])
        lam = s.sb("lam", [GROUPS, 2, P])
        lrli = s.sb("lrli", [P, 2, GROUPS])
        dt = s.sb("dt", [P, GROUPS])
        half_pi = s.sb("half_pi", [P, 1])
        pw = s.sb("pw", [P, 2, SL + 1, GROUPS])
        prev = s.sb("prev", [P, 2, GROUPS, SL])
        pfwd = s.sb("pfwd", [P, 2, GROUPS, SL])
        ap = s.sb("ap", [P, 2, LEVELS, GROUPS])
        t = [s.sb(f"t{i}", [P, GROUPS]) for i in range(6)]
        dcol = s.sb("dcol", [P, 2, 2])
        glu = s.sb("glu", [P, 2, 256])
        E = s.sb("E", [P, GU, 2 * SL, 16])
        Et = s.sb("Et", [P, GU, SL, 16])
        M2 = s.sb("M2", [P, GU, SL, 16])
        c1 = s.sb("c1", [P, GU, 16])
        M1 = s.sb("M1", [P, GU, P])
        TT = s.sb("TT", [P, GU, P])
        X = s.sb("X", [P, GU, SC + 1])
        RJ, R, ucp, U = (g["ycT"][:].rearrange("p a n -> p (a n)")[:, i * 1024:(i + 1) * 1024] for i in range(4))
        RJ = RJ.rearrange("p (a b n) -> p a b n", a=2, b=GU)
        R = R.rearrange("p (a b n) -> p a b n", a=2, b=GU)
        ucp = ucp.rearrange("p (a b n) -> p a b n", a=2, b=GU)
        U = U.rearrange("p (b n) -> p b n", b=GU)
        apt = s.sb("apt", [P, 2, LEVELS, GU])
        ycp = s.sb("ycp", [P, 2, 4, P])
        bank = [s.ps(f"bank{i}", [P, 512]) for i in range(8)]
        names = ("small dve_done act_done exped exped2 wrapped sined turned placed c_turned ready "
                 "e_ready u_copied u_turned u_placed m_turned m_placed k_summed k_placed v_summed v_placed "
                 "rj_ready r_ready stepped scanned y_summed y_placed m2_ready y_turned skipped squared "
                 "gated gelued glued opened").split()
        q = {n: s.sem(n) for n in names}

        with nc.Block() as block:
            @block.sync
            def _(sp):
                for j, n in enumerate(("lam_re", "lam_im")):
                    for r in range(2):
                        sp.dma_start(lam[:, j, r * 64:(r + 1) * 64], g[n][0]).then_inc(q["small"], 16)
                sp.dma_start(dt[:], g["log_dt"].broadcast_to([P, GROUPS])).then_inc(q["small"], 16)
                for to, names_ in ((q1, ("b_re", "b_im")), (q2, ("b_im", "b_re"))):
                    for r in range(2):
                        sp.dma_start(to[r * 64:(r + 1) * 64], g[names_[r]][0].rearrange("g p c -> p g c")).then_inc(q["small"], 16)
                for m, names_ in enumerate((("c_re", "c_im"), ("c_im", "c_re"))):
                    for r in range(2):
                        sp.dma_start(craw[:, m, :, r * 64:(r + 1) * 64],
                                     g[names_[r]][0].rearrange("(h g) c p -> (g c) h p", h=2)).then_inc(q["small"], 16)
                cols(nc, sp, dcol[:, 0, :], g["d_skip"], 2, q["small"])
                cols(nc, sp, dcol[:, 1, :], g["glu_b"], 2, q["small"])
                sp.dma_start(glu[:], g["glu_w"][0].rearrange("(k p) n -> p k n", p=P)).then_inc(q["small"], 16)

            @block.tensor
            def _(pe):
                n = 0
                for hc in range(2):
                    for f in range(2):
                        for j0 in range(0, SL, 4):
                            if n >= 4:
                                pe.wait_ge(q["placed"], n - 3)
                            v = uc[:, hc, f * 1024:(f + 1) * 1024].rearrange("p (n j) -> p j n", j=SL)
                            for j in range(4):
                                mm = pe.transpose(bank[n % 4][:, j * P:(j + 1) * P], v[:, j0 + j, :], const(g, "ident"))
                            mm.then_inc(q["turned"], 1)
                            n += 1
                pe.wait_ge(q["small"], 16 * 16)
                for j in range(2):
                    mm = pe.transpose(bank[4][:, j * 16:(j + 1) * 16], lam[:, j, :], const(g, "ident")[0:16, 0:16])
                mm.then_inc(q["c_turned"], 1)
                for m in range(2):
                    for hc in range(2):
                        mm = pe.transpose(bank[5][:, (2 * m + hc) * P:(2 * m + hc + 1) * P], craw[:, m, hc, :], const(g, "ident"))
                mm.then_inc(q["c_turned"], 1)

            @block.scalar
            def _(act):
                n = 0
                for hc in range(2):
                    for f in range(2):
                        for j0 in range(0, SL, 4):
                            act.wait_ge(q["turned"], n + 1)
                            for j in range(4):
                                ins = nc.scalar.copy(UY[:, f, hc * 8:(hc + 1) * 8, (j0 + j) * 16:(j0 + j + 1) * 16],
                                                     bank[n % 4][:, j * P:(j + 1) * P].rearrange("p (g c) -> p g c", c=16))
                            ins.then_inc(q["placed"], 1)
                            n += 1
                act.wait_ge(q["small"], 16 * 16)
                nc.scalar.activation(dt[:], dt[:], ACT.Exp).then_inc(q["exped"], 1)
                act.wait_ge(q["exped2"], 1)
                nc.scalar.activation(t[2][:], t[0][:], ACT.Exp).then_inc(q["exped"], 1)
                act.wait_ge(q["wrapped"], 1)
                nc.scalar.activation(t[3][:], t[1][:], ACT.Sin).then_inc(q["sined"], 1)
                nc.scalar.activation(t[5][:], t[4][:], ACT.Sin, scale=-1.0, bias=half_pi[:]).then_inc(q["sined"], 1)

            @block.vector
            def _(dve):
                link = Chain(dve, q["dve_done"])
                tt, ts = nc.vector.tensor_tensor, nc.vector.tensor_scalar
                link(nc.vector.memset(half_pi[:], math.pi / 2))
                link(nc.vector.memset(E[:], 0.0))
                link(nc.vector.memset(X[:], 0.0))
                dve.wait_ge(q["c_turned"], 1)
                link(nc.vector.tensor_copy(lrli[:].rearrange("p a b -> p (a b)"), bank[4][:, 0:32]))
                lr, li = lrli[:, 0, :], lrli[:, 1, :]
                dve.wait_ge(q["exped"], 1)
                link(tt(t[1][:], li, dt[:], ALU.mult))
                tt(t[0][:], lr, dt[:], ALU.mult).then_inc(q["exped2"], 1)
                wrap_angle(nc, link, t[1][:], t[4][:])
                nc.vector.scalar_tensor_tensor(t[4][:], t[1][:], -1.0, t[1][:], ALU.mult, ALU.max).then_inc(q["wrapped"], 1)
                dve.wait_ge(q["sined"], 2)
                dve.wait_ge(q["exped"], 2)
                link(nc.vector.memset(pw[:, 0, 0, :], 1.0))
                link(nc.vector.memset(pw[:, 1, 0, :], 0.0))
                ar, ai = pw[:, 0, 1, :], pw[:, 1, 1, :]
                link(tt(ar, t[2][:], t[5][:], ALU.mult))
                link(tt(ai, t[2][:], t[3][:], ALU.mult))

                def product(out_r, out_i, xr, xi, yr, yi):
                    link(tt(t[0][:], xr, yr, ALU.mult))
                    link(tt(t[1][:], xi, yi, ALU.mult))
                    link(tt(t[2][:], xr, yi, ALU.mult))
                    link(tt(t[3][:], xi, yr, ALU.mult))
                    link(tt(out_r, t[0][:], t[1][:], ALU.subtract))
                    link(tt(out_i, t[2][:], t[3][:], ALU.add))
                for n in range(2, SL + 1):
                    product(pw[:, 0, n, :], pw[:, 1, n, :], pw[:, 0, n // 2, :], pw[:, 1, n // 2, :],
                            pw[:, 0, n - n // 2, :], pw[:, 1, n - n // 2, :])
                for r in range(2):
                    link(nc.vector.tensor_copy(ap[:, r, 0, :], pw[:, r, SL, :]))
                    link(nc.vector.tensor_copy(pfwd[:, r].rearrange("p g n -> p n g"), pw[:, r, 1:SL + 1, :]))
                    for n in range(SL):
                        link(nc.vector.tensor_copy(prev[:, r, :, SL - 1 - n], pw[:, r, n, :]))
                for n in range(1, LEVELS):
                    product(ap[:, 0, n, :], ap[:, 1, n, :], ap[:, 0, n - 1, :], ap[:, 1, n - 1, :],
                            ap[:, 0, n - 1, :], ap[:, 1, n - 1, :])
                link(ts(t[4][:], ar, -1.0, None, ALU.add))
                link(tt(t[0][:], lr, lr, ALU.mult))
                link(tt(t[1][:], li, li, ALU.mult))
                link(tt(t[0][:], t[0][:], t[1][:], ALU.add))
                link(nc.vector.reciprocal(t[5][:], t[0][:]))
                link(tt(t[0][:], t[4][:], lr, ALU.mult))
                link(tt(t[1][:], ai, li, ALU.mult))
                link(tt(t[0][:], t[0][:], t[1][:], ALU.add))
                link(tt(t[2][:], t[0][:], t[5][:], ALU.mult))
                link(tt(t[0][:], ai, lr, ALU.mult))
                link(tt(t[1][:], t[4][:], li, ALU.mult))
                link(tt(t[0][:], t[0][:], t[1][:], ALU.subtract))
                link(tt(t[3][:], t[0][:], t[5][:], ALU.mult))
                kr = t[2][:].unsqueeze(2).broadcast_to([P, GROUPS, 16])
                ki = t[3][:].unsqueeze(2).broadcast_to([P, GROUPS, 16])
                link(ts(q2[:], q2[:], const(g, "upper"), None, ALU.mult))
                link(tt(B1[:], q1[:], kr, ALU.mult))
                link(tt(C2[:], q2[:], ki, ALU.mult))
                link(tt(B1[:], B1[:], C2[:], ALU.add))
                link(tt(B2[:], q2[:], kr, ALU.mult))
                link(tt(C2[:], q1[:], ki, ALU.mult))
                link(tt(B2[:], B2[:], C2[:], ALU.subtract))
                dve.wait_ge(q["c_turned"], 2)
                link(ts(C1[:].rearrange("p g c -> p (g c)"), bank[5][:, 0:256], const(g, "upper"), -1.0, ALU.mult, ALU.mult))
                link(ts(C2[:].rearrange("p g c -> p (g c)"), bank[5][:, 256:512], -1.0, None, ALU.mult))
        s.end()

        with nc.Fori(0, GROUPS // GU) as turn:
            with nc.Block() as block:
                mine = bass.ds(turn * GU, GU)

                @block.vector
                def _(dve):
                    link = Chain(dve, q["dve_done"])
                    tt = nc.vector.tensor_tensor

                    def by_power(out, tmp, p2, b1, b2, sem):
                        def pb(r):
                            return p2[:, r, mine, :].unsqueeze(3).broadcast_to([P, GU, SL, 16])

                        def bb(b):
                            return b[:, mine, :].unsqueeze(2).broadcast_to([P, GU, SL, 16])
                        link(tt(out, pb(0), bb(b1), ALU.mult))
                        link(tt(tmp, pb(1), bb(b2), ALU.mult))
                        tt(out, out, tmp, ALU.add).then_inc(sem, 1)
                    by_power(E[:, :, 0:SL, :], Et[:], prev, B1, B2, q["e_ready"])
                    link(nc.vector.tensor_copy(apt[:], ap[:, :, :, mine]))
                    dve.wait_ge(q["e_ready"], 1)
                    by_power(M2[:], Et[:], pfwd, C1, C2, q["m2_ready"])
                    dve.wait_ge(q["m_turned"], 1)
                    nc.vector.tensor_copy(M1[:].rearrange("p g n -> p (g n)"), bank[2][:]).then_inc(q["m_placed"], 1)
                    dve.wait_ge(q["k_summed"], 1)
                    nc.vector.tensor_copy(TT[:].rearrange("p g n -> p (g n)"), bank[3][:]).then_inc(q["k_placed"], 1)
                    for b in range(2):
                        dve.wait_ge(q["v_summed"], b + 1)
                        nc.vector.tensor_copy(X[:, 2 * b:2 * b + 2, 1:], bank[4 + b][:].rearrange("p (g n) -> p g n", g=2)).then_inc(q["scanned"], 1)
                    for lv in range(LEVELS):
                        if lv >= 2:
                            dve.wait_ge(q["stepped"], 2 * lv - 2)
                        for gi in range(GU):
                            dve.wait_ge(q["rj_ready"], GU * lv + gi + 1)
                            nc.vector.scalar_tensor_tensor(R[:, lv % 2, gi, :], const(g, "ident"), apt[:, 0, lv, gi:gi + 1],
                                                           RJ[:, lv % 2, gi, :], ALU.mult, ALU.add).then_inc(q["r_ready"], 1)
                        by = 1 << lv
                        for b in range(2):
                            dve.wait_ge(q["stepped"], 2 * lv + b + 1)
                            dve.wait_ge(q["scanned"], 2 * lv + b + 1)
                            gs = slice(2 * b, 2 * b + 2)
                            tt(X[:, gs, 1 + by:], X[:, gs, 1 + by:],
                               bank[(lv % 2) * 2 + b][:].rearrange("p (g n) -> p g n", g=2)[:, :, :SC - by], ALU.add).then_inc(q["scanned"], 1)

                @block.scalar
                def _(act):
                    nc.scalar.copy(ucp[:], UY[:, :, mine, :]).then_inc(q["u_copied"], 1)
                    nc.scalar.copy(c1[:], C1[:, mine, :]).then_inc(q["u_copied"], 1)
                    for b in range(2):
                        act.wait_ge(q["u_turned"], b + 1)
                        nc.scalar.copy(U[:, 2 * b:2 * b + 2, :].rearrange("p g n -> p (g n)"), bank[b][:]).then_inc(q["u_placed"], 1)
                    act.wait_ge(q["m2_ready"], 1)
                    for lv in range(LEVELS):
                        for gi in range(GU):
                            if lv >= 2:
                                act.wait_ge(q["r_ready"], GU * (lv - 2) + gi + 1)
                            nc.scalar.activation(RJ[:, lv % 2, gi, :], const(g, "swap"), ACT.Copy,
                                                 scale=apt[:, 1, lv, gi:gi + 1]).then_inc(q["rj_ready"], 1)
                    for f in range(2):
                        act.wait_ge(q["y_summed"], f + 1)
                        nc.scalar.copy(UY[:, f, mine, :], bank[6 + f][:].rearrange("p (g n) -> p g n", g=GU)).then_inc(q["y_placed"], 1)

                @block.tensor
                def _(pe):
                    ident = const(g, "ident")
                    pe.wait_ge(q["u_copied"], 2)
                    for b in range(2):
                        for gi in (2 * b, 2 * b + 1):
                            for f in range(2):
                                at = (gi % 2) * SC + f * P
                                mm = pe.transpose(bank[b][:, at:at + P], ucp[:, f, gi, :], ident)
                        mm.then_inc(q["u_turned"], 1)
                    pe.wait_ge(q["e_ready"], 1)
                    for gi in range(GU):
                        mm = pe.transpose(bank[2][:, gi * P:(gi + 1) * P], E[:, gi, 0:SL, :].rearrange("p s c -> p (s c)"), ident)
                    mm.then_inc(q["m_turned"], 1)
                    for gi in range(GU):
                        for i in range(SL):
                            at = gi * P + i * 16
                            mm = pe.matmul(bank[3][:, at:at + 16], E[:, gi, SL - 1 - i:2 * SL - 1 - i, :].rearrange("p s c -> p (s c)"),
                                           c1[:, gi, :], start=True, stop=True)
                    mm.then_inc(q["k_summed"], 1)
                    pe.wait_ge(q["m_placed"], 1)
                    for b in range(2):
                        pe.wait_ge(q["u_placed"], b + 1)
                        for gi in (2 * b, 2 * b + 1):
                            mm = pe.matmul(bank[4 + b][:, (gi % 2) * SC:(gi % 2 + 1) * SC], M1[:, gi, :], U[:, gi, :], start=True, stop=True)
                        mm.then_inc(q["v_summed"], 1)
                    pe.wait_ge(q["k_placed"], 1)
                    for lv in range(LEVELS):
                        by = 1 << lv
                        for b in range(2):
                            pe.wait_ge(q["scanned"], 2 * lv + b + 1)
                            for gi in (2 * b, 2 * b + 1):
                                pe.wait_ge(q["r_ready"], GU * lv + gi + 1)
                                at = (gi % 2) * SC
                                mm = pe.matmul(bank[(lv % 2) * 2 + b][:, at:at + SC - by], R[:, lv % 2, gi, :],
                                               X[:, gi, 1:1 + SC - by], start=True, stop=True)
                            mm.then_inc(q["stepped"], 1)
                    pe.wait_ge(q["scanned"], 2 * LEVELS + 2)
                    for f in range(2):
                        for gi in range(GU):
                            to = bank[6 + f][:, gi * P:(gi + 1) * P]
                            pe.matmul(to, U[:, gi, f * P:(f + 1) * P], TT[:, gi, :], start=True, stop=False)
                            mm = pe.matmul(to, X[:, gi, f * P:(f + 1) * P], M2[:, gi].rearrange("p i c -> p (i c)"),
                                           start=False, stop=True)
                        mm.then_inc(q["y_summed"], 1)
            s.end()

        ycT = g["ycT"]
        G2 = 2 * math.sqrt(2 / math.pi)
        with nc.Block() as block:
            units = [(hc, f, i0) for hc in range(2) for f in range(2) for i0 in (0, 4)]

            @block.tensor
            def _(pe):
                for n, (hc, f, i0) in enumerate(units):
                    if n >= 4:
                        pe.wait_ge(q["skipped"], n - 3)
                    pe.wait_ge(q["u_copied"], n + 1)
                    for i in range(4):
                        mm = pe.transpose(bank[n % 4][:, i * P:(i + 1) * P], ycp[:, n % 2, i, :], const(g, "ident"))
                    mm.then_inc(q["y_turned"], 1)
                for n in range(8):
                    c, tb = n % 2, n // 2
                    pe.wait_ge(q["gelued"], 4 + tb + 1)
                    if n >= 4:
                        pe.wait_ge(q["glued"], n - 3)
                    for k in range(2):
                        mm = pe.matmul(bank[4 + n % 4][:], glu[:, k, c * P:(c + 1) * P], ycT[:, k, tb * 512:(tb + 1) * 512],
                                       start=k == 0, stop=k == 1)
                    mm.then_inc(q["opened"], 1)

            @block.vector
            def _(dve):
                link = Chain(dve, q["dve_done"])
                for n, (hc, f, i0) in enumerate(units):
                    dve.wait_ge(q["y_turned"], n + 1)

                    def tokens(a):
                        return a[:, hc, f * 1024:(f + 1) * 1024].rearrange("p (n i) -> p i n", i=SL)[:, i0:i0 + 4, :]
                    nc.vector.scalar_tensor_tensor(tokens(ycT), tokens(uc), dcol[:, 0, hc:hc + 1],
                                                   bank[n % 4][:].rearrange("p (i n) -> p i n", i=4), ALU.mult, ALU.add).then_inc(q["skipped"], 1)
                dve.wait_ge(q["skipped"], 8)
                for n in range(8):
                    c, tb = n // 4, n % 4
                    y = ycT[:, c, tb * 512:(tb + 1) * 512]
                    b = uc[:, c, tb * 512:(tb + 1) * 512]
                    link(nc.vector.tensor_tensor(b, y, y, ALU.mult))
                    link(nc.vector.tensor_scalar(b, b, 0.044715, 1.0, ALU.mult, ALU.add))
                    nc.vector.tensor_tensor(b, b, y, ALU.mult).then_inc(q["squared"], 1)
                for n in range(8):
                    c, tb = n // 4, n % 4
                    y = ycT[:, c, tb * 512:(tb + 1) * 512]
                    b = uc[:, c, tb * 512:(tb + 1) * 512]
                    dve.wait_ge(q["gated"], n + 1)
                    nc.vector.tensor_tensor(y, y, b, ALU.mult).then_inc(q["gelued"], 1)
                for n in range(8):
                    c, tb = n % 2, n // 2
                    y = ycT[:, c, tb * 512:(tb + 1) * 512]
                    b = uc[:, c, tb * 512:(tb + 1) * 512]
                    dve.wait_ge(q["opened"], n - n % 2 + 2)
                    dve.wait_ge(q["glued"], n + 1)
                    nc.vector.tensor_tensor(y, y, b, ALU.mult).then_inc(q["ready"], 1)

            @block.scalar
            def _(act):
                for n, (hc, f, i0) in enumerate(units):
                    if n >= 2:
                        act.wait_ge(q["y_turned"], n - 1)
                    for i in range(4):
                        ins = nc.scalar.copy(ycp[:, n % 2, i, :].rearrange("p (g c) -> p g c", c=16),
                                             UY[:, f, hc * 8:(hc + 1) * 8, (i0 + i) * 16:(i0 + i + 1) * 16])
                    ins.then_inc(q["u_copied"], 1)
                for n in range(8):
                    c, tb = n // 4, n % 4
                    b = uc[:, c, tb * 512:(tb + 1) * 512]
                    act.wait_ge(q["squared"], n + 1)
                    nc.scalar.activation(b, b, ACT.Sigmoid, scale=G2).then_inc(q["gated"], 1)
                for n in range(8):
                    c, tb = n % 2, n // 2
                    act.wait_ge(q["opened"], n + 1)
                    act.wait_ge(q["gelued"], 4 * c + tb + 1)
                    nc.scalar.activation(uc[:, c, tb * 512:(tb + 1) * 512], bank[4 + n % 4][:], ACT.Sigmoid,
                                         bias=dcol[:, 1, c:c + 1]).then_inc(q["glued"], 1)
        s.end()


def stage_project(nc, g):
    hT = g["hT"]
    CH = 8
    parts = (("z", g["w_in"][0], V0 // P, IN_W // P - 2 * HEADS, IN_W // P, g["zT"]),
             ("qk", g["w_in"][0], Q0 // P, 2 * HEADS, IN_W // P, g["zT"]),
             ("gate", g["gate_w"][0], 0, 3 * KD, 3 * KD, g["gateT"]))
    with Stage(nc, "project") as s:
        h_lo = s.sb("h_lo", [P, KD, T], F32R)
        cos, sin = s.sb("cos", [P, T]), s.sb("sin", [P, T])
        pos = cos[:].bitcast(I32)
        ang, tmp = s.sb("ang", [P, T]), s.sb("tmp", [P, T])
        half_pi = s.sb("half_pi", [P, 1])
        sq2, rs2, qn2 = (s.sb(n, [P, 2, 512]) for n in ("sq2", "rs2", "qn2"))
        tt = s.sb("tt", [P, 512])
        gcol = s.sb("gcol", [P, 2])
        eps = s.sb("eps", [P, 1])
        h_hi = s.sb("h_hi", [P, KD, T], F32R)
        raw = s.sb("raw", [P, KD, P])
        w_hi = [s.sb(f"w_hi{b}", [P, KD, P], F32R) for b in range(2)]
        w_lo = [s.sb(f"w_lo{b}", [P, KD, P], F32R) for b in range(2)]
        o = s.sb("o", [P, 2, 512])
        gb = s.sb("gb", [P, 3 * KD])
        gbt = s.sb("gbt", [P, CH])
        bank = [s.ps(f"bank{i}", [P, 512]) for i in range(8)]
        raw_ready, small, h_high, h_split, w_high, w_split, biased, summed, evacuated = (
            s.sem(n) for n in "raw_ready small h_high h_split w_high w_split biased summed evacuated".split())
        squared, meaned, rooted, normed, rotated, dve_done = (
            s.sem(n) for n in "squared meaned rooted normed rotated dve_done".split())
        wrapped, sined = s.sem("wrapped"), s.sem("sined")
        stored = [s.sem("stored0"), s.sem("stored1")]
        units = [(u, tb) for u in range(CH) for tb in range(TB)]

        with nc.Block() as block:
            @block.sync
            def _(sp):
                sp.dma_start(gb[:], g["gate_b"].rearrange("a (k p) -> p (a k)", p=P),
                             allow_slow_non_contiguous=True).then_inc(small, 16)
                sp.dma_start(pos, g["positions"].broadcast_to([P, T])).then_inc(small, 16)
                for j, n in enumerate(("q_norm_g", "k_norm_g")):
                    for m in range(2):
                        sp.dma_start(gcol[m * DH:(m + 1) * DH, j:j + 1], g[n].rearrange("a n -> n a"),
                                     allow_slow_non_contiguous=True).then_inc(small, 16)

            @block.scalar
            def _(act):
                for k in range(KD):
                    nc.scalar.copy(h_hi[:, k, :], hT[:, k, :]).then_inc(h_high, 1)

            @block.gpsimd
            def _(pool):
                nc.gpsimd.memset(eps[:], EPS).then_inc(biased, 1)
                pool.wait_ge(small, 16 * 6)
                nc.gpsimd.tensor_scalar(gcol[:, 0:1], gcol[:, 0:1], DH ** -0.5, None, ALU.mult).then_inc(biased, 1)
                nc.gpsimd.memset(half_pi[:], math.pi / 2).then_inc(biased, 1)

            @block.vector
            def _(dve):
                for k in range(KD):
                    dve.wait_ge(h_high, k + 1)
                    nc.vector.tensor_tensor(h_lo[:, k, :], hT[:, k, :], h_hi[:, k, :].bitcast(F32), ALU.subtract).then_inc(h_split, 1)
        s.end()
        for number, (part, w, first, count, chunks, out) in enumerate(parts):
            def column(c):
                return (c % count + first) % chunks * P
            w = w.rearrange("(k p) n -> p k n", p=P)
            only = count == CH

            def load_raw(sp, turn, u):
                if only and u + 2 >= CH:
                    _, w_next, first_next, _, _, _ = parts[number + 1]
                    c = (first_next + u + 2 - CH) * P
                    src = w_next.rearrange("(k p) n -> p k n", p=P)[:, :, c:c + P]
                else:
                    src = w[:, :, bass.ds(column(turn * CH + (u + 2)), P)]
                sp.dma_start(raw[:], src).then_inc(raw_ready, 16)

            def split(act, dve, b, n):
                if act is not None:
                    nc.scalar.copy(w_hi[b][:].rearrange("p k n -> p (k n)"), raw[:].rearrange("p k n -> p (k n)")).then_inc(w_high, 1)
                if dve is not None:
                    dve.wait_ge(w_high, n)
                    nc.vector.tensor_tensor(w_lo[b][:].rearrange("p k n -> p (k n)"), raw[:].rearrange("p k n -> p (k n)"),
                                            w_hi[b][:].rearrange("p k n -> p (k n)").bitcast(F32), ALU.subtract).then_inc(w_split, 1)

            if number == 0:
                with nc.Block() as block:
                    @block.sync
                    def _(sp):
                        sp.dma_start(raw[:], w[:, :, column(0):column(0) + P]).then_inc(raw_ready, 16)
                        sp.wait_ge(w_split, 1)
                        sp.dma_start(raw[:], w[:, :, column(1):column(1) + P]).then_inc(raw_ready, 16)
                        sp.wait_ge(raw_ready, 32)

                    @block.scalar
                    def _(act):
                        act.wait_ge(raw_ready, 16)
                        split(act, None, 0, 1)

                    @block.vector
                    def _(dve):
                        split(None, dve, 0, 1)
                s.end()
            with nc.Fori(0, count // CH) as turn:
                with nc.Block() as block:
                    @block.sync
                    def _(sp):
                        for n, (u, tb) in enumerate(units):
                            if tb == 0:
                                sp.wait_ge(w_split, u + 1)
                                load_raw(sp, turn, u)
                            sp.wait_ge(evacuated, n + 1)
                            sp.dma_start(out[bass.ds((turn * CH + (u + first)) % chunks, 1), :, tb * 512:(tb + 1) * 512].rearrange("a p n -> p (a n)"),
                                         o[:, n % 2, :]).then_inc(stored[n % 2], 16)
                        for b in range(2):
                            sp.wait_ge(stored[b], 16 * len(units) // 2)
                        sp.wait_ge(raw_ready, 16 * CH)

                    @block.tensor
                    def _(pe):
                        banks = 4 if part == "qk" else 8

                        def mean(n):
                            pe.wait_ge(squared, n + 1)
                            if n >= 2:
                                pe.wait_ge(rooted, n - 1)
                            pe.matmul(bank[4 + n % 2][:], const(g, "half"), sq2[:, n % 2, :], start=True, stop=True).then_inc(meaned, 1)

                        def rotate(n):
                            pe.wait_ge(normed, n + 1)
                            if n >= 2:
                                pe.wait_ge(evacuated, n - 1)
                            pe.matmul(bank[6 + n % 2][:], const(g, "rot"), qn2[:, n % 2, :], start=True, stop=True).then_inc(rotated, 1)

                        for n, (u, tb) in enumerate(units):
                            if tb == 0 and u >= 1:
                                pe.wait_ge(w_split, u)
                            if n >= banks:
                                pe.wait_ge(normed if part == "qk" else evacuated, n + 1 - banks)
                            at = slice(tb * 512, (tb + 1) * 512)
                            b = u % 2
                            for k in range(KD):
                                pe.matmul(bank[n % banks][:], w_hi[b][:, k, :], h_hi[:, k, at], start=k == 0, stop=False)
                                pe.matmul(bank[n % banks][:], w_hi[b][:, k, :], h_lo[:, k, at], start=False, stop=False)
                                mm = pe.matmul(bank[n % banks][:], w_lo[b][:, k, :], h_hi[:, k, at], start=False, stop=k == KD - 1)
                            mm.then_inc(summed, 1)
                            if part == "qk" and n >= 1:
                                mean(n - 1)
                            if part == "qk" and n >= 2:
                                rotate(n - 2)
                        if part == "qk":
                            mean(len(units) - 1)
                            rotate(len(units) - 2)
                            rotate(len(units) - 1)

                    @block.scalar
                    def _(act):
                        if part == "gate":
                            act.wait_ge(biased, 1)

                        def root(n):
                            act.wait_ge(meaned, n + 1)
                            if n >= 2:
                                act.wait_ge(normed, n - 1)
                            nc.scalar.activation(rs2[:, n % 2, :], bank[4 + n % 2][:], ACT.Sqrt, bias=eps[:]).then_inc(rooted, 1)
                        for n, (u, tb) in enumerate(units):
                            if part == "z" and n == 4 * TB:
                                act.wait_ge(wrapped, 1)
                                nc.scalar.activation(sin[:], ang[:], ACT.Sin).then_inc(sined, 1)
                                nc.scalar.activation(cos[:], tmp[:], ACT.Sin, scale=-1.0, bias=half_pi[:]).then_inc(sined, 1)
                            if tb == 0:
                                if u >= 1:
                                    act.wait_ge(raw_ready, 16 * u)
                                    act.wait_ge(summed, TB * u)
                                split(act, None, (u + 1) % 2, u + 1)
                            act.wait_ge(summed, n + 1)
                            if part == "qk":
                                if n >= 2:
                                    act.wait_ge(meaned, n - 1)
                                nc.scalar.activation(sq2[:, n % 2, :], bank[n % 4][:], ACT.Square).then_inc(squared, 1)
                                if n >= 1:
                                    root(n - 1)
                                continue
                            if n >= 2:
                                act.wait_ge(stored[n % 2], 16 * (n // 2))
                            if part == "gate":
                                nc.scalar.activation(o[:, n % 2, :], bank[n % 8][:], ACT.Sigmoid, bias=gbt[:, u:u + 1]).then_inc(evacuated, 1)
                            else:
                                nc.scalar.copy(o[:, n % 2, :], bank[n % 8][:]).then_inc(evacuated, 1)
                        if part == "qk":
                            root(len(units) - 1)

                    @block.vector
                    def _(dve):
                        if part == "gate":
                            nc.vector.tensor_copy(gbt[:], gb[:, bass.ds(turn * CH, CH)]).then_inc(biased, 1)
                        link = Chain(dve, dve_done)

                        def norm(n):
                            m = units[n][0] // HEADS
                            dve.wait_ge(rooted, n + 1)
                            link(nc.vector.reciprocal(rs2[:, n % 2, :], rs2[:, n % 2, :]))
                            if n >= 2:
                                dve.wait_ge(rotated, n - 1)
                            nc.vector.scalar_tensor_tensor(qn2[:, n % 2, :], bank[n % 4][:], gcol[:, m:m + 1], rs2[:, n % 2, :],
                                                           ALU.mult, ALU.mult).then_inc(normed, 1)

                        def angles(u):
                            if u == 0:
                                link(nc.vector.tensor_copy(ang[:], pos))
                                link(nc.vector.tensor_scalar(ang[:], ang[:], const(g, "inv"), None, ALU.mult))
                            if u == 1:
                                wrap_angle(nc, link, ang[:], tmp[:])
                            if u == 2:
                                nc.vector.scalar_tensor_tensor(tmp[:], ang[:], -1.0, ang[:], ALU.mult, ALU.max).then_inc(wrapped, 1)
                            if u == 5:
                                dve.wait_ge(sined, 1)
                                link(nc.vector.tensor_scalar(sin[:], sin[:], const(g, "sign"), None, ALU.mult))

                        def rope(n):
                            tb = units[n][1]
                            at = slice(tb * 512, (tb + 1) * 512)
                            dve.wait_ge(normed, n + 1)
                            if n >= 2:
                                dve.wait_ge(stored[n % 2], 16 * (n // 2))
                            link(nc.vector.tensor_tensor(o[:, n % 2, :], qn2[:, n % 2, :], cos[:, at], ALU.mult))
                            dve.wait_ge(rotated, n + 1)
                            link(nc.vector.tensor_tensor(tt[:], bank[6 + n % 2][:], sin[:, at], ALU.mult))
                            nc.vector.tensor_tensor(o[:, n % 2, :], o[:, n % 2, :], tt[:], ALU.add).then_inc(evacuated, 1)

                        for n, (u, tb) in enumerate(units):
                            if tb == 0:
                                split(None, dve, (u + 1) % 2, u + 1)
                                if part == "z":
                                    angles(u)
                            if part == "qk":
                                norm(n)
                                if n >= 1:
                                    rope(n - 1)
                        if part == "qk":
                            rope(len(units) - 1)
                s.end()


def stage_merge(nc, g):
    RING = 4
    CH = 4
    projs = [g[n][0].rearrange("(k p) n -> p k n", p=P) for n in ("proj_a", "proj_b", "proj_c")]
    gateT = g["gateT"].rearrange("(b k) p n -> p k b n", b=3)
    ks = [(0, 2), (2, 4), (6, 2)]
    with Stage(nc, "merge") as s:
        wp = s.sb("wp", [P, 2, KD, P])
        sg = s.sb("sg", [P, RING, 3, 512])
        mx = s.sb("mx", [P, 2, 512])
        bank = [s.ps(f"bank{i}", [P, 512]) for i in range(8)]
        w_ready = [s.sem("w_ready0"), s.sem("w_ready1")]
        g_ready = [s.sem(f"g_ready{i}") for i in range(RING)]
        summed, multiplied, mixed, dve_done = (s.sem(n) for n in "summed multiplied mixed dve_done".split())
        stored = [s.sem("stored0"), s.sem("stored1")]
        units = [(u, tb, br) for u in range(CH) for tb in range(TB) for br in range(3)]

        def load(sp, b, j):
            for br in range(3):
                k0, kn = ks[br]
                sp.dma_start(wp[:, b, k0:k0 + kn], projs[br][:, :, bass.ds(j * P, P)]).then_inc(w_ready[b], 16)

        def load_gates(sp, m, j):
            tb = m % TB
            for br in range(3):
                sp.dma_start(sg[:, m % RING, br], gateT[:, bass.ds(j, 1), br, tb * 512:(tb + 1) * 512].rearrange("p a n -> p (a n)")
                             ).then_inc(g_ready[m % RING], 16)

        with nc.Block() as block:
            @block.sync
            def _(sp):
                load(sp, 0, 0)
                for m in range(RING):
                    load_gates(sp, m, 0)
                sp.wait_ge(w_ready[0], 48)
                for m in range(RING):
                    sp.wait_ge(g_ready[m], 48)
        s.end()
        with nc.Fori(0, KD // CH) as turn:
            with nc.Block() as block:
                @block.sync
                def _(sp):
                    for m in range(CH * TB):
                        u, tb = m // TB, m % TB
                        if tb == 0:
                            if u >= 1:
                                sp.wait_ge(summed, 3 * m)
                            load(sp, (u + 1) % 2, (turn * CH + (u + 1)) % KD)
                        sp.wait_ge(mixed, m + 1)
                        sp.dma_start(g["mixT"][:, bass.ds(turn * CH + u, 1), tb * 512:(tb + 1) * 512].rearrange("p a n -> p (a n)"),
                                     mx[:, m % 2, :]).then_inc(stored[m % 2], 16)
                        load_gates(sp, m + RING, (turn * CH + (u + 1)) % KD)
                    for b in range(2):
                        sp.wait_ge(stored[b], 16 * CH * TB // 2)
                        sp.wait_ge(w_ready[b], 48 * CH // 2)
                    for m in range(RING):
                        sp.wait_ge(g_ready[m], 48 * CH)

                @block.tensor
                def _(pe):
                    for n, (u, tb, br) in enumerate(units):
                        if n % 12 == 0 and u >= 1:
                            pe.wait_ge(w_ready[u % 2], 48 * ((u + 1) // 2))
                        if n >= 8:
                            pe.wait_ge(multiplied, n - 7)
                        k0, kn = ks[br]
                        y = (g["yaT"], g["ybT"], g["ycT"])[br]
                        for k in range(kn):
                            mm = pe.matmul(bank[n % 8][:], wp[:, u % 2, k0 + k, :], y[:, k, tb * 512:(tb + 1) * 512],
                                           start=k == 0, stop=k == kn - 1)
                        mm.then_inc(summed, 1)

                @block.vector
                def _(dve):
                    for n, (u, tb, br) in enumerate(units):
                        m = n // 3
                        if br == 0 and m >= 2:
                            dve.wait_ge(stored[m % 2], 16 * (m // 2))
                        if br == 0 and m >= RING:
                            dve.wait_ge(g_ready[m % RING], 48 * (m // RING))
                        dve.wait_ge(summed, n + 1)
                        gate = sg[:, m % RING, br, :]
                        to = mx[:, m % 2, :] if br == 0 else gate
                        nc.vector.tensor_tensor(to, gate, bank[n % 8][:], ALU.mult).then_inc(multiplied, 1)
                        if br >= 1:
                            dve.wait_ge(multiplied, n + 1)
                            if br == 2:
                                dve.wait_ge(dve_done, m + 1)
                            nc.vector.tensor_tensor(mx[:, m % 2, :], mx[:, m % 2, :], gate, ALU.add).then_inc(mixed if br == 2 else dve_done, 1)
            s.end()


def stage_out(nc, g, lg):
    U = 4
    x_t = g["x"][0].rearrange("(t p) n -> p t n", p=P)
    x1_t = g["x1"].rearrange("(t p) n -> p t n", p=P)
    h2_t = g["h2"].rearrange("(t p) n -> p t n", p=P)
    with Stage(nc, "out") as s:
        w = s.sb("w", [P, KD, D])
        w_hi = s.sb("w_hi", [P, KD, D], F32R)
        w_lo = s.sb("w_lo", [P, KD, D], F32R)
        m_hi = [s.sb(f"m_hi{b}", [P, KD, P], F32R) for b in range(2)]
        m_lo = [s.sb(f"m_lo{b}", [P, KD, P], F32R) for b in range(2)]
        rows = s.sb("rows", [P, 3, D])
        wr = s.sb("wr", [P, KD, 36])
        mT = s.sb("mT", [P, U, KD, P])
        x = s.sb("x", [P, U, D])
        h2 = s.sb("h2", [P, 2, D])
        t = s.sb("t", [P, D])
        h2T = s.sb("h2T", [P, 2, KD, P])
        sq = s.sb("sq", [P, D])
        ss = s.sb("ss", [P, U])
        eps = s.sb("eps", [P, 1])
        bank = [s.ps(f"bank{i}", [P, 512]) for i in range(8)]
        names = ("small dve_done act_done summed added squared rooted scaled shifted turned placed routed logged stored_x w_high w_split m_high m_split w_ready").split()
        q = {n: s.sem(n) for n in names}
        m_ready = [s.sem(f"m_ready{i}") for i in range(U)]
        x_ready = [s.sem(f"x_ready{i}") for i in range(U)]
        stored = [s.sem("stored0"), s.sem("stored1")]

        def load_m(sp, i, turn):
            sp.dma_start(mT[:, i], g["mixT"][:, :, bass.ds(turn * 512 + i * P, P)]).then_inc(m_ready[i], 16)

        with nc.Block() as block:
            @block.sync
            def _(sp):
                sp.dma_start(w[:], g["w_out"][0].rearrange("(k p) n -> p k n", p=P)).then_inc(q["w_ready"], 16)
                for i, r in enumerate((0, 1, 2)):
                    sp.dma_start(rows[:, i, :], g["rows"][r:r + 1, :].broadcast_to([P, D])).then_inc(q["small"], 16)
                sp.dma_start(wr[:, :, 0:4], g["router_g_w"][0].rearrange("(k p) n -> p k n", p=P)).then_inc(q["small"], 16)
                sp.dma_start(wr[:, :, 4:36], g["router_e_w"][0].rearrange("(k p) n -> p k n", p=P)).then_inc(q["small"], 16)
                for i in range(U):
                    load_m(sp, i, 0)
                sp.wait_ge(q["small"], 80)
                for i in range(U):
                    sp.wait_ge(m_ready[i], 16)

            @block.gpsimd
            def _(pool):
                nc.gpsimd.memset(eps[:], EPS).then_inc(q["logged"], 1)

            @block.scalar
            def _(act):
                act.wait_ge(q["w_ready"], 16)
                for k in range(KD):
                    nc.scalar.copy(w_hi[:, k, :], w[:, k, :]).then_inc(q["w_high"], 1)

            @block.vector
            def _(dve):
                for k in range(KD):
                    dve.wait_ge(q["w_high"], k + 1)
                    nc.vector.tensor_tensor(w_lo[:, k, :], w[:, k, :], w_hi[:, k, :].bitcast(F32), ALU.subtract).then_inc(q["w_split"], 1)
        s.end()
        with nc.Fori(0, NT // U) as turn:
            with nc.Block() as block:
                @block.sync
                def _(sp):
                    for i in range(U):
                        sp.dma_start(x[:, i, :], x_t[:, bass.ds(turn * U + i, 1), :].rearrange("p a n -> p (a n)")).then_inc(x_ready[i], 16)
                    nxt = (turn + 1) % (NT // U)
                    for i in range(U + 1):
                        if i < U:
                            sp.wait_ge(q["m_split"], i + 1)
                            load_m(sp, i, nxt)
                        if i >= 1:
                            j = i - 1
                            sp.wait_ge(q["stored_x"], j + 1)
                            sp.dma_start(x1_t[:, bass.ds(turn * U + j, 1), :].rearrange("p a n -> p (a n)"), x[:, j, :]).then_inc(q["small"], 16)
                            sp.wait_ge(q["shifted"], j + 1)
                            sp.dma_start(h2_t[:, bass.ds(turn * U + j, 1), :].rearrange("p a n -> p (a n)"), h2[:, j % 2, :]).then_inc(stored[j % 2], 16)
                    for b in range(2):
                        sp.wait_ge(stored[b], 16 * U // 2)
                    sp.wait_ge(q["small"], 16 * U)
                    for i in range(U):
                        sp.wait_ge(m_ready[i], 16)

                @block.tensor
                def _(pe):
                    def product(i):
                        pe.wait_ge(q["m_split"], i + 1)
                        for nh in range(2):
                            b = (i % 2) * 2 + nh
                            if i >= 2:
                                pe.wait_ge(q["added"], 2 * (i - 2) + nh + 1)
                            at = slice(nh * 512, (nh + 1) * 512)
                            for k in range(KD):
                                pe.matmul(bank[b][:], m_hi[i % 2][:, k, :], w_hi[:, k, at], start=k == 0, stop=False)
                                pe.matmul(bank[b][:], m_hi[i % 2][:, k, :], w_lo[:, k, at], start=False, stop=False)
                                mm = pe.matmul(bank[b][:], m_lo[i % 2][:, k, :], w_hi[:, k, at], start=False, stop=k == KD - 1)
                            mm.then_inc(q["summed"], 1)

                    def route(i):
                        pe.wait_ge(q["shifted"], i + 1)
                        for half in range(2):
                            if i >= 1:
                                pe.wait_ge(q["placed"], 2 * (i - 1) + half + 1)
                            for j in range(4):
                                k = half * 4 + j
                                mm = pe.transpose(bank[4 + half][:, j * P:(j + 1) * P], h2[:, i % 2, k * P:(k + 1) * P], const(g, "ident"))
                            mm.then_inc(q["turned"], 1)
                        pe.wait_ge(q["placed"], 2 * i + 2)
                        if i >= 2:
                            pe.wait_ge(q["logged"], i - 1)
                        for k in range(KD):
                            mm = pe.matmul(bank[6 + i % 2][:, 0:36], h2T[:, i % 2, k, :], wr[:, k, :], start=k == 0, stop=k == KD - 1)
                        mm.then_inc(q["routed"], 1)
                    product(0)
                    for i in range(U):
                        if i + 1 < U:
                            product(i + 1)
                        route(i)

                @block.vector
                def _(dve):
                    link = Chain(dve, q["dve_done"])

                    def rest(i):
                        dve.wait_ge(q["m_high"], i + 1)
                        nc.vector.tensor_tensor(m_lo[i % 2][:].rearrange("p k n -> p (k n)"), mT[:, i].rearrange("p k n -> p (k n)"),
                                                m_hi[i % 2][:].rearrange("p k n -> p (k n)").bitcast(F32), ALU.subtract).then_inc(q["m_split"], 1)
                    rest(0)
                    rest(1)
                    for i in range(U):
                        dve.wait_ge(x_ready[i], 16)
                        for nh in range(2):
                            at = slice(nh * 512, (nh + 1) * 512)
                            dve.wait_ge(q["summed"], 2 * i + nh + 1)
                            if i >= 1:
                                dve.wait_ge(q["stored_x"], i)
                            nc.vector.tensor_tensor(t[:, at], bank[(i % 2) * 2 + nh][:], rows[:, 0, at], ALU.mult).then_inc(q["added"], 1)
                        dve.wait_ge(q["added"], 2 * i + 2)
                        nc.vector.tensor_tensor(x[:, i, :], x[:, i, :], t[:], ALU.add).then_inc(q["stored_x"], 1)
                        if i + 2 < U:
                            rest(i + 2)
                        dve.wait_ge(q["rooted"], i + 1)
                        link(nc.vector.reciprocal(ss[:, i:i + 1], ss[:, i:i + 1]))
                        if i >= 2:
                            dve.wait_ge(q["turned"], 2 * i - 2)
                            dve.wait_ge(stored[i % 2], 16)
                        nc.vector.scalar_tensor_tensor(h2[:, i % 2, :], x[:, i, :], ss[:, i:i + 1], rows[:, 2, :], ALU.mult, ALU.mult).then_inc(q["scaled"], 1)

                @block.gpsimd
                def _(pool):
                    for i in range(U):
                        pool.wait_ge(q["scaled"], i + 1)
                        nc.gpsimd.tensor_tensor(h2[:, i % 2, :], h2[:, i % 2, :], rows[:, 1, :], ALU.add).then_inc(q["shifted"], 1)

                @block.scalar
                def _(act):
                    link = Chain(act, q["act_done"])

                    def high(i):
                        nc.scalar.copy(m_hi[i % 2][:].rearrange("p k n -> p (k n)"), mT[:, i].rearrange("p k n -> p (k n)")).then_inc(q["m_high"], 1)
                    high(0)
                    high(1)
                    for i in range(U + 1):
                        if i < U:
                            if i + 2 < U:
                                act.wait_ge(q["summed"], 2 * i + 2)
                                high(i + 2)
                            act.wait_ge(q["stored_x"], i + 1)
                            if i >= 1:
                                act.wait_ge(q["squared"], i)
                            nc.scalar.activation(sq[:], x[:, i, :], ACT.Square, accum_out=ss[:, i:i + 1]).then_inc(q["squared"], 1)
                            act.wait_ge(q["squared"], i + 1)
                            nc.scalar.activation(ss[:, i:i + 1], ss[:, i:i + 1], ACT.Sqrt, scale=1.0 / D, bias=eps[:]).then_inc(q["rooted"], 1)
                        if i >= 1:
                            j = i - 1
                            for half in range(2):
                                act.wait_ge(q["turned"], 2 * j + half + 1)
                                if j >= 2:
                                    act.wait_ge(q["routed"], j - 1)
                                nc.scalar.copy(h2T[:, j % 2, half * 4:half * 4 + 4, :], bank[4 + half][:].rearrange("p (a n) -> p a n", n=P)).then_inc(q["placed"], 1)
                            act.wait_ge(q["routed"], j + 1)
                            nc.scalar.copy(lg[:, bass.ds(turn * U + j, 1), :].rearrange("p a n -> p (a n)"), bank[6 + j % 2][:, 0:36]).then_inc(q["logged"], 1)
            s.end()


def stage_route(nc, g, r, lg):
    NB = 72
    with Stage(nc, "route") as s:
        rb = s.sb("rb", [P, 36])
        gm, sm = s.sb("gm", [P, NT]), s.sb("sm", [P, NT])
        eg = s.sb("eg", [P, NT, 4])
        cand = s.sb("cand", [P, NT, 4])
        em = s.sb("em", [P, NT, 32])
        top = s.sb("top", [P, NT, 8])
        idx = s.sb("idx", [P, NT, 8], U32)
        ef = s.sb("ef", [P, 2, NT])
        O = s.sb("O", [P, 2, NT, NE])
        M = s.sb("M", [P, NT, NE])
        rank = s.sb("rank", [P, NT, NE])
        pre = s.sb("pre", [P, NT + 1, NE])
        cs = s.sb("cs", [P, NT, NE])
        ti = s.sb("ti", [P, NE], I32)
        nb = s.sb("nb", [P, NE])
        e0, e1 = s.sb("e0", [P, NE]), s.sb("e1", [P, NE])
        dest = s.sb("dest", [P, 2, NT])
        at = s.sb("at", [P, 2, NT], I32)
        hi = s.sb("hi", [P, 2, NT], I32)
        scat = s.sb("scat", [P, 2, NT], U32)
        tok = s.sb("tok", [P, NT], U32)
        zero = s.sb("zero", [P, NB], U32)
        cmp = s.sb("cmp", [1, 96, NE])
        blk = s.sb("blk", [1, 96])
        pa, pb = s.ps("pa", [P, 512]), s.ps("pb", [P, 512])
        names = "small dve_done act_done shifted exped diffed exped2 counted ranked placed ready zeroed".split()
        q = {n: s.sem(n) for n in names}
        q["scattered"] = s.kept_sem("scattered")
        with nc.Block() as block:
            @block.sync
            def _(sp):
                sp.dma_start(rb[:, 0:4], g["router_g_b"].broadcast_to([P, 4])).then_inc(q["small"], 16)
                sp.dma_start(rb[:, 4:36], g["router_e_b"].broadcast_to([P, 32])).then_inc(q["small"], 16)

            @block.scalar
            def _(act):
                act.wait_ge(q["shifted"], 1)
                nc.scalar.activation(eg[:], eg[:], ACT.Exp).then_inc(q["exped"], 1)
                act.wait_ge(q["diffed"], 1)
                nc.scalar.activation(sm[:], sm[:], ACT.Exp).then_inc(q["exped2"], 1)

            @block.tensor
            def _(pe):
                pe.wait_ge(q["counted"], 1)
                m = M[:].rearrange("p t e -> p (t e)")
                pe.matmul(pa[:], const(g, "before"), m, start=True, stop=True).then_inc(q["ranked"], 1)
                pe.matmul(pb[:], const(g, "ones"), m, start=True, stop=True).then_inc(q["ranked"], 1)

            @block.gpsimd
            def _(pool):
                nc.gpsimd.memset(zero[:], 0.0).then_inc(q["zeroed"], 1)
                pool.wait_ge(q["zeroed"], 1)
                pool.dma_start(g["slots"].rearrange("(p b) a -> p (b a)", p=P), zero[:]).then_inc(q["scattered"], 16)
                pool.wait_ge(q["scattered"], 16)
                pool.wait_ge(q["ready"], 1)
                for a in range(2):
                    for t in range(NT):
                        pool.indirect_dma_start(out=g["slots"], out_offset=bass.IndirectOffsetOnAxis(ap=scat[:, a, t:t + 1], axis=0),
                                                in_=tok[:, t:t + 1], in_offset=None).then_inc(q["scattered"], 16)
                pool.wait_ge(q["scattered"], 16 * (1 + 2 * NT))
                pool.dma_start(r["slot_tok"][:], g["slots"].rearrange("(p b) a -> p (b a)", p=P)).then_inc(q["scattered"], 16)
                pool.wait_ge(q["scattered"], 16 * (2 + 2 * NT))

            @block.vector
            def _(dve):
                link = Chain(dve, q["dve_done"])
                tt, ts = nc.vector.tensor_tensor, nc.vector.tensor_scalar

                def over(a, shape):
                    return a.unsqueeze(2).broadcast_to(shape)
                link(nc.vector.tensor_copy(tok[:], const(g, "tok")))
                dve.wait_ge(q["small"], 32)
                link(tt(lg[:], lg[:], rb[:].unsqueeze(1).broadcast_to([P, NT, 36]), ALU.add))
                gl, el = lg[:, :, 0:4], lg[:, :, 4:36]
                link(nc.vector.tensor_reduce(gm[:], gl, AX, ALU.max))
                link(tt(cand[:], gl, over(gm[:], [P, NT, 4]), ALU.is_equal))
                tt(eg[:], gl, over(gm[:], [P, NT, 4]), ALU.subtract).then_inc(q["shifted"], 1)
                link(ts(cand[:], cand[:], -1000.0, None, ALU.mult))
                link(tt(cand[:], cand[:], const(g, "iota")[:, 0:4].unsqueeze(1).broadcast_to([P, NT, 4]), ALU.add))
                link(nc.vector.tensor_reduce(gm[:], cand[:], AX, ALU.min))
                link(tt(cand[:], cand[:], over(gm[:], [P, NT, 4]), ALU.is_equal))
                link(ts(cand[:], cand[:], -NEG, NEG, ALU.mult, ALU.add))
                for k in range(8):
                    link(tt(em[:].rearrange("p t (a b) -> p t a b", b=8)[:, :, :, k],
                            el.rearrange("p t (a b) -> p t a b", b=8)[:, :, :, k], cand[:], ALU.add))
                for t in range(NT):
                    link(nc.vector.max(top[:, t, :], em[:, t, :]))
                    link(nc.vector.max_index(idx[:, t, :], top[:, t, :], em[:, t, :]))
                dve.wait_ge(q["exped"], 1)
                link(nc.vector.tensor_reduce(gm[:], eg[:], AX, ALU.add))
                tt(sm[:], top[:, :, 1], top[:, :, 0], ALU.subtract).then_inc(q["diffed"], 1)
                dve.wait_ge(q["exped2"], 1)
                link(ts(r["wt"][:, 0, :], sm[:], 1.0, None, ALU.add))
                link(tt(r["wt"][:, 0, :], r["wt"][:, 0, :], gm[:], ALU.mult))
                link(nc.vector.reciprocal(r["wt"][:, 0, :], r["wt"][:, 0, :]))
                link(tt(r["wt"][:, 1, :], r["wt"][:, 0, :], sm[:], ALU.mult))
                for a in range(2):
                    link(nc.vector.tensor_copy(ef[:, a, :], idx[:, :, a]))
                    link(tt(O[:, a], const(g, "iota").unsqueeze(1).broadcast_to([P, NT, NE]), over(ef[:, a, :], [P, NT, NE]), ALU.is_equal))
                tt(M[:], O[:, 0], O[:, 1], ALU.add).then_inc(q["counted"], 1)
                link(nc.vector.memset(pre[:, 0, :], 0.0))
                dve.wait_ge(q["ranked"], 2)
                link(nc.vector.tensor_copy(cs[:].rearrange("p t e -> p (t e)"), pb[:]))
                for t in range(NT):
                    link(tt(pre[:, t + 1, :], pre[:, t, :], cs[:, t, :], ALU.add))
                link(ts(ti[:], pre[:, NT, :], 127.0, None, ALU.add))
                link(ts(ti[:], ti[:], 7, None, ALU.arith_shift_right))
                link(nc.vector.tensor_copy(nb[:], ti[:]))
                link(ts(nb[:], nb[:], 1.0, None, ALU.max))
                link(nc.vector.tensor_copy(e0[:], nb[:]))
                frm, to = e0, e1
                for lv in range(5):
                    by = 1 << lv
                    link(nc.vector.tensor_copy(to[:, :by], frm[:, :by]))
                    link(tt(to[:, by:], frm[:, by:], frm[:, :NE - by], ALU.add))
                    frm, to = to, frm
                ends, starts = frm, to
                link(tt(starts[:], ends[:], nb[:], ALU.subtract))
                link(ts(starts[:], starts[:], float(P), None, ALU.mult))
                link(tt(rank[:], pa[:].rearrange("p (t e) -> p t e", e=NE), pre[:, 0:NT, :], ALU.add))
                link(tt(rank[:], rank[:], starts[:].unsqueeze(1).broadcast_to([P, NT, NE]), ALU.add))
                for a in range(2):
                    link(tt(O[:, a], O[:, a], rank[:], ALU.mult))
                    link(nc.vector.tensor_reduce(dest[:, a, :], O[:, a], AX, ALU.add))
                link(nc.vector.tensor_copy(r["dest"][:], dest[:]))
                link(nc.vector.tensor_copy(at[:], dest[:]))
                link(ts(hi[:], at[:], 7, None, ALU.arith_shift_right))
                link(ts(at[:], at[:], 127, None, ALU.bitwise_and))
                link(ts(at[:], at[:], float(NB), None, ALU.mult))
                link(tt(scat[:], at[:], hi[:], ALU.add))
                nc.vector.memset(nb[:], 0.0).then_inc(q["ready"], 1)
                link(tt(cmp[:], ends[0:1, :].unsqueeze(1).broadcast_to([1, 96, NE]),
                        const(g, "blk")[0:1, :].unsqueeze(2).broadcast_to([1, 96, NE]), ALU.is_le))
                link(nc.vector.tensor_reduce(blk[:], cmp[:], AX, ALU.add))
                link(ts(blk[:], blk[:], float(NE - 1), None, ALU.min))
                link(nc.vector.tensor_copy(r["blk"][0:1, 0:96], blk[:]))
                link(nc.vector.tensor_copy(r["blk"][0:1, 96:96 + NE], ends[0:1, :]))
                link(ts(r["blk"][0:1, 128:129], r["blk"][0:1, 96 + NE - 1:96 + NE], 1, None, ALU.arith_shift_right))
        s.end()


def stage_experts(nc, g, r):
    w1, w3 = (g[n][0].rearrange("e (k p) n -> e p k n", p=P) for n in ("moe_w1", "moe_w3"))
    w2 = g["moe_w2"][0].rearrange("e (k p) n -> e p k n", p=P)
    KF = FF // P
    W13, SLOT = KD * FF, 3 * KD * FF
    h2 = g["h2"]
    with Stage(nc, "moe") as s:
        W = s.sb("W", [P, 2 * SLOT])
        x = [s.sb(f"x{i}", [P, D]) for i in range(2)]
        idx = [s.sb(f"idx{i}", [P, 1], U32) for i in range(2)]
        xT = s.sb("xT", [P, 2, KD, P])
        sg, hm = s.sb("sg", [P, FF]), s.sb("hm", [P, FF])
        hT = s.sb("hT", [P, KF, P])
        y = s.sb("y", [P, 2, D])
        xb = [s.ps(f"xb{i}", [P, 512]) for i in range(2)]
        h1b, h3b, htb = s.ps("h1b", [P, 512]), s.ps("h3b", [P, 512]), s.ps("htb", [P, 512])
        yb = [s.ps(f"yb{i}", [P, 512]) for i in range(2)]
        names = ("w13_arrived w2_arrived block_done idx_copied x_turned x_placed h_summed gated silued hidden h_turned h_placed "
                 "y_placed go gathering finished").split()
        q = {n: s.sem(n) for n in names}
        w13_ready = [s.sem("w13_ready0"), s.sem("w13_ready1")]
        w2_ready = [s.sem("w2_ready0"), s.sem("w2_ready1")]
        x_ready = [s.kept_sem("x_ready0"), s.kept_sem("x_ready1")]
        stored = [s.sem("stored0"), s.sem("stored1")]

        def pairs(eng):
            return eng.value_load(r["blk"][0:1, 128:129], min_val=NE // 2, max_val=32)

        with nc.Block() as block:
            @block.sync
            def _(sp):
                def load(e, u, src, c0, k, sem):
                    sp.dma_start(W[:, u * SLOT + c0:u * SLOT + c0 + W13].rearrange("p (k n) -> p k n", k=k),
                                 src[bass.ds(e, 1)].rearrange("a p k n -> p (a k) n")).then_inc(sem[u], 16)

                def load_13(e, u):
                    load(e, u, w1, 0, KD, w13_ready)
                    load(e, u, w3, W13, KD, w13_ready)

                def load_2(e, u):
                    load(e, u, w2, 2 * W13, KF, w2_ready)
                for u in range(2):
                    load_13(u, u)
                    load_2(u, u)
                    sp.wait_ge(w13_ready[u], 32)
                    sp.sem_inc(q["w13_arrived"], 1)
                    sp.wait_ge(w2_ready[u], 16)
                    sp.sem_inc(q["w2_arrived"], 1)
                with sp.Fori(1, NE // 2) as i:
                    for u in range(2):
                        end = sp.value_load(r["blk"][0:1, bass.ds(i * 2 + (96 + u - 2), 1)], min_val=1, max_val=64)
                        sp.wait_ge(q["h_summed"], end * 2)
                        sp.sem_inc(q["go"], 1)
                        load_13(i * 2 + u, u)
                        sp.wait_ge(q["block_done"], end)
                        sp.sem_inc(q["go"], 1)
                        load_2(i * 2 + u, u)
                        sp.wait_ge(w13_ready[u], i * 32 + 32)
                        sp.sem_inc(q["w13_arrived"], 1)
                        sp.wait_ge(w2_ready[u], i * 16 + 16)
                        sp.sem_inc(q["w2_arrived"], 1)

            @block.gpsimd
            def _(pool):
                def gather(b, n, par):
                    pool.wait_ge(q["x_turned"], b + 1)
                    nc.gpsimd.tensor_copy(idx[par][:], r["slot_tok"][:, bass.ds(b, 1)]).then_inc(q["idx_copied"], 1)
                    pool.wait_ge(q["idx_copied"], b + 1)
                    pool.sem_inc(q["gathering"], 1)
                    pool.indirect_dma_start(out=x[par][:], out_offset=None, in_=h2,
                                            in_offset=bass.IndirectOffsetOnAxis(ap=idx[par][:, 0:1], axis=0)).then_inc(x_ready[par], 16)
                count = pairs(pool)
                gather(0, 0, 0)
                gather(1, 0, 1)
                with pool.Fori(0, count) as i:
                    for b, par in ((i * 2 + 2, 0), (i * 2 + 3, 1)):
                        gather(b, i + 1, par)
                pool.wait_ge(x_ready[1], count * 16 + 16)
                pool.sem_inc(q["finished"], 1)

            @block.tensor
            def _(pe):
                ident = const(g, "ident")

                def turn_x(b, n, par):
                    pe.wait_ge(x_ready[par], n * 16 + 16)
                    for half in range(2):
                        for j in range(4):
                            k = half * 4 + j
                            mm = pe.transpose(xb[half][:, j * P:(j + 1) * P], x[par][:, k * P:(k + 1) * P], ident)
                    mm.then_inc(q["x_turned"], 1)

                def products_13(b, par, e):
                    pe.wait_ge(q["x_placed"], b * 2 + 2)
                    pe.wait_ge(q["w13_arrived"], e + 1)
                    base = (e % 2) * SLOT
                    for hb, c0 in ((h1b, 0), (h3b, W13)):
                        for k in range(KD):
                            mm = pe.matmul(hb[:], xT[:, par, k, :], W[:, bass.ds(base + (c0 + k * FF), FF)], start=k == 0, stop=k == KD - 1)
                        mm.then_inc(q["h_summed"], 1)

                def turn_h(b):
                    pe.wait_ge(q["hidden"], b + 1)
                    for k in range(KF):
                        mm = pe.transpose(htb[:, k * P:(k + 1) * P], hm[:, k * P:(k + 1) * P], ident)
                    mm.then_inc(q["h_turned"], 1)

                def product_2(b, e):
                    pe.wait_ge(q["h_placed"], b + 1)
                    pe.wait_ge(q["y_placed"], b * 2 + 2)
                    pe.wait_ge(q["w2_arrived"], e + 1)
                    base = (e % 2) * SLOT + 2 * W13
                    for nh in range(2):
                        for k in range(KF):
                            mm = pe.matmul(yb[nh][:], hT[:, k, :], W[:, bass.ds(base + (k * D + nh * 512), 512)], start=k == 0, stop=k == KF - 1)
                    mm.then_inc(q["block_done"], 1)

                def expert(b):
                    return pe.value_load(r["blk"][0:1, bass.ds(b, 1)], min_val=0, max_val=NE - 1)
                count = pairs(pe)
                pe.sem_inc(q["x_turned"], 2)
                turn_x(0, 0, 0)
                products_13(0, 0, expert(0))
                turn_x(1, 0, 1)
                turn_h(0)
                with pe.Fori(0, count) as i:
                    for b, par in ((i * 2 + 1, 1), (i * 2 + 2, 0)):
                        products_13(b, par, expert(b))
                        turn_x(b + 1, i + 1, 1 - par)
                        product_2(b - 1, expert(b - 1))
                        turn_h(b)
                product_2(count * 2, expert(count * 2))

            @block.scalar
            def _(act):
                def place_x(b, par):
                    act.wait_ge(q["x_turned"], b + 3)
                    for half in range(2):
                        nc.scalar.copy(xT[:, par, half * 4:half * 4 + 4, :], xb[half][:].rearrange("p (a n) -> p a n", n=P)).then_inc(q["x_placed"], 1)

                def place_y(b, n, par):
                    act.wait_ge(q["block_done"], b + 1)
                    act.wait_ge(stored[par], n * 16 + 16)
                    for nh in range(2):
                        nc.scalar.copy(y[:, par, nh * 512:(nh + 1) * 512], yb[nh][:]).then_inc(q["y_placed"], 1)
                    act.wait_ge(q["y_placed"], b * 2 + 4)
                    act.dma_start(g["ybuf"][bass.ds(b * P, P), :], y[:, par, :]).then_inc(stored[par], 16)
                count = pairs(act)
                act.sem_inc(q["y_placed"], 2)
                for par in range(2):
                    act.sem_inc(stored[par], 16)
                place_x(0, 0)
                act.wait_ge(q["h_summed"], 1)
                nc.scalar.activation(sg[:], h1b[:], ACT.Sigmoid).then_inc(q["gated"], 1)
                place_x(1, 1)
                with act.Fori(0, count) as i:
                    for b, par in ((i * 2 + 1, 1), (i * 2 + 2, 0)):
                        act.wait_ge(q["h_summed"], b * 2 + 1)
                        act.wait_ge(q["hidden"], b)
                        nc.scalar.activation(sg[:], h1b[:], ACT.Sigmoid).then_inc(q["gated"], 1)
                        place_x(b + 1, 1 - par)
                        place_y(b - 1, i, 1 - par)
                place_y(count * 2, count, 0)
                act.wait_ge(stored[0], count * 16 + 32)
                act.wait_ge(stored[1], count * 16 + 16)
                act.sem_inc(q["finished"], 1)

            @block.vector
            def _(dve):
                def hidden(b, first=False):
                    dve.wait_ge(q["gated"], b + 1)
                    if not first:
                        dve.wait_ge(q["h_turned"], b)
                    nc.vector.tensor_tensor(hm[:], sg[:], h1b[:], ALU.mult).then_inc(q["silued"], 1)
                    dve.wait_ge(q["silued"], b + 1)
                    dve.wait_ge(q["h_summed"], b * 2 + 2)
                    nc.vector.tensor_tensor(hm[:], hm[:], h3b[:], ALU.mult).then_inc(q["hidden"], 1)

                def place_h(b):
                    dve.wait_ge(q["h_turned"], b + 1)
                    nc.vector.tensor_copy(hT[:].rearrange("p k n -> p (k n)"), htb[:]).then_inc(q["h_placed"], 1)
                count = pairs(dve)
                hidden(0, True)
                place_h(0)
                with dve.Fori(0, count) as i:
                    for b in (i * 2 + 1, i * 2 + 2):
                        hidden(b)
                        place_h(b)
        s.end()


def stage_combine(nc, g, r):
    U = 8
    x1_t = g["x1"].rearrange("(t p) n -> p t n", p=P)
    o_t = g["out"][0].rearrange("(t p) n -> p t n", p=P)
    with Stage(nc, "comb") as s:
        row = s.sb("row", [P, D])
        x = s.sb("x", [P, U, D])
        ya = [[s.sb(f"y{a}{i}", [P, D]) for i in range(U)] for a in range(2)]
        idx = s.sb("idx", [P, 2, U], U32)
        wt = s.sb("wt", [P, 2, U])
        small, copied, weighted, summed, scaled, done, stored = (s.sem(n) for n in "small copied weighted summed scaled done stored".split())
        x_ready = [s.sem(f"x_ready{i}") for i in range(U)]
        y_ready = [s.kept_sem(f"y_ready{i}") for i in range(U)]
        with nc.Block() as block:
            @block.sync
            def _(sp):
                sp.dma_start(row[:], g["rows"][3:4, :].broadcast_to([P, D])).then_inc(small, 16)
                sp.wait_ge(small, 16)
        s.end()
        with nc.Fori(0, NT // U) as turn:
            with nc.Block() as block:
                @block.sync
                def _(sp):
                    for i in range(U):
                        sp.dma_start(x[:, i, :], x1_t[:, bass.ds(turn * U + i, 1), :].rearrange("p a n -> p (a n)")).then_inc(x_ready[i], 16)
                    for i in range(U):
                        sp.wait_ge(done, i + 1)
                        sp.dma_start(o_t[:, bass.ds(turn * U + i, 1), :].rearrange("p a n -> p (a n)"), x[:, i, :]).then_inc(stored, 16)
                    sp.wait_ge(stored, 16 * U)

                @block.gpsimd
                def _(pool):
                    nc.gpsimd.tensor_copy(idx[:], r["dest"][:, :, bass.ds(turn * U, U)]).then_inc(copied, 1)
                    pool.wait_ge(copied, 1)
                    for i in range(U):
                        for a in range(2):
                            pool.indirect_dma_start(out=ya[a][i][:], out_offset=None, in_=g["ybuf"],
                                                    in_offset=bass.IndirectOffsetOnAxis(ap=idx[:, a, i:i + 1], axis=0)).then_inc(y_ready[i], 16)

                @block.scalar
                def _(act):
                    nc.scalar.copy(wt[:], r["wt"][:, :, bass.ds(turn * U, U)]).then_inc(weighted, 1)
                    act.wait_ge(weighted, 1)
                    for i in range(U):
                        act.wait_ge(y_ready[i], turn * 32 + 32)
                        nc.scalar.activation(ya[0][i][:], ya[0][i][:], ACT.Copy, scale=wt[:, 0, i:i + 1]).then_inc(scaled, 1)

                @block.vector
                def _(dve):
                    for i in range(U):
                        dve.wait_ge(scaled, i + 1)
                        dve.wait_ge(x_ready[i], 16)
                        a, b = ya[0][i][:], ya[1][i][:]
                        nc.vector.scalar_tensor_tensor(a, b, wt[:, 1, i:i + 1], a, ALU.mult, ALU.add).then_inc(summed, 1)
                        dve.wait_ge(summed, 3 * i + 1)
                        nc.vector.tensor_tensor(a, a, row[:], ALU.mult).then_inc(summed, 1)
                        dve.wait_ge(summed, 3 * i + 2)
                        nc.vector.tensor_tensor(x[:, i, :], x[:, i, :], a, ALU.add).then_inc(summed, 1)
                        dve.wait_ge(summed, 3 * i + 3)
                        dve.sem_inc(done, 1)
            s.end()


INPUTS = ("x c positions ada_w ada_b norm1_g w_in pool_w pool_scale q_norm_g k_norm_g lambda_q1 lambda_k1 lambda_q2 lambda_k2 "
          "subln_g lam_re lam_im log_dt b_re b_im c_re c_im d_skip glu_w glu_b proj_a proj_b proj_c gate_w gate_b w_out norm2_g "
          "router_g_w router_g_b router_e_w router_e_b moe_w1 moe_w3 moe_w2").split()


def program(nc, g):
    g["rows"] = nc.dram_tensor("rows", (4, D), F32, kind="Internal").ap()
    g["mixT"] = nc.dram_tensor("mixT", (P, KD, T), F32, kind="Internal").ap()
    g["zT"] = nc.dram_tensor("zT", (IN_W // P, P, T), F32, kind="Internal").ap()
    g["gateT"] = nc.dram_tensor("gateT", (3 * KD, P, T), F32, kind="Internal").ap()
    for n in ("x1", "h2"):
        g[n] = nc.dram_tensor(n, (T, D), F32, kind="Internal").ap()
    g["slots"] = nc.dram_tensor("slots", (P * 72, 1), U32, kind="Internal").ap()
    g["ybuf"] = nc.dram_tensor("ybuf", (NB_OUT * P, D), F32, kind="Internal").ap()
    with ExitStack() as keep:
        def sb(name, shape, dt=F32, ctx=keep):
            return ctx.enter_context(nc.sbuf_tensor(name, shape, dt))
        g["consts"] = sb("consts", [P, CONST_W])
        g["col1"] = sb("col1", [P, 2, KD])
        stage_mod(nc, g)
        with ExitStack() as normed:
            g["hT"] = sb("hT", [P, KD, T], ctx=normed)
            stage_norm1(nc, g)
        stage_project(nc, g)
        with ExitStack() as mixers:
            g["ybT"] = sb("ybT", [P, HEADS, T], ctx=mixers)
            stage_attention(nc, g)
            g["yaT"] = sb("yaT", [P, 2, T], ctx=mixers)
            g["ycT"] = sb("ycT", [P, 2, T], ctx=mixers)
            with nc.sbuf_tensor("uc", [P, 2, T], F32) as uc:
                stage_pool(nc, g, uc)
                stage_ssm(nc, g, uc)
            stage_merge(nc, g)
        moe_part(nc, g, sb)


def moe_part(nc, g, sb):
    lg = sb("lg", [P, NT, 36])
    r = {"wt": sb("wt", [P, 2, NT]), "dest": sb("dest", [P, 2, NT], U32),
         "slot_tok": sb("slot_tok", [P, 72], U32), "blk": sb("blk", [1, 136], I32)}
    stage_out(nc, g, lg)
    stage_route(nc, g, r, lg)
    stage_experts(nc, g, r)
    stage_combine(nc, g, r)


def kernel(**inputs):
    import numpy as _np
    import concourse.bacc as _bacc
    from concourse.bass_utils import run_bass_kernel_spmd as _run

    nc = _bacc.Bacc("TRN2", target_bir_lowering=False, num_devices=1)
    arrays, g = {}, {}
    for name in INPUTS:
        a = _np.ascontiguousarray(inputs[name])
        arrays[f"in_{name}"] = a
        g[name] = nc.dram_tensor(f"in_{name}", a.shape, mybir.dt.from_np(a.dtype), kind="ExternalInput").ap()
    pack = constant_pack()
    arrays["const_pack"] = pack
    g["const_pack"] = nc.dram_tensor("const_pack", pack.shape, F32, kind="ExternalInput").ap()
    g["out"] = nc.dram_tensor("out", (1, T, D), F32, kind="ExternalOutput").ap()
    program(nc, g)
    r = _run(nc, [arrays], core_ids=[0])
    return r.results[0]["out"]
```
